# Optimizing a Trainium2 kernel written in Bass

```python
import math
import jax
import jax.numpy as jnp
from jax import lax
import numpy as np

D_MODEL = 1024
BATCH = 1
SEQ = 128
DEPTH = 2
DEC_BATCH = 1
DEC_SEQ = 256
PAST_LEN = 128

GRID_W = 64
EPS = 1e-6
ATTN_BLOCK = 128
ROPE_BASE = 10000.0

A_HEADS = 16
A_NOPE = 64
A_ROPE = 32
A_QK = A_NOPE + A_ROPE
A_V = 64
A_QLORA = 512
A_KVLORA = 256

B_HEADS = 4
B_DK = 128
B_DV = 256
B_GATE_RANK = 16
B_GATE_NORM = 16.0
B_CHUNK = 16

C_HEADS = 16
C_HEADDIM = 64
C_INNER = C_HEADS * C_HEADDIM
C_GROUPS = 2
C_STATE = 128
C_XBC = C_INNER + 2 * C_GROUPS * C_STATE
C_CONV = 5
C_CHUNK = 64

N_EXPERTS = 16
N_EXPERT_GROUPS = 4
TOP_K = 2
D_EXPERT = 512

IN_SPLITS = (
    ('a_cq', A_QLORA), ('a_ckv', A_KVLORA), ('a_krope', A_ROPE),
    ('b_q', B_HEADS * B_DK), ('b_k', B_HEADS * B_DK), ('b_v', B_HEADS * B_DV),
    ('b_og', B_HEADS * B_DV), ('b_gf', B_GATE_RANK), ('b_gb', B_GATE_RANK),
    ('c_z', C_INNER), ('c_xbc', C_XBC), ('c_dtf', C_HEADS), ('c_dtb', C_HEADS),
    ('gates', 3 * D_MODEL),
)
D_IN = (A_QLORA + A_KVLORA + A_ROPE + 2 * B_HEADS * B_DK + 2 * B_HEADS * B_DV
        + 2 * B_GATE_RANK + C_INNER + C_XBC + 2 * C_HEADS + 3 * D_MODEL)

kernel_name = 'mla_gla_ssd_moe_prefix_diffusion'

def rmsnorm(x, w):
    xf = x.astype(jnp.float32)
    y = xf * lax.rsqrt(jnp.mean(xf * xf, axis=-1, keepdims=True) + EPS)
    return (y * w.astype(jnp.float32)).astype(x.dtype)

def ada_rmsnorm(x, w, shift, scale):
    return rmsnorm(x, w) * (1.0 + scale) + shift

def modulation(cvec, w, b):
    m = jax.nn.silu(cvec) @ w + b
    return m.reshape(m.shape[:-1] + (6, D_MODEL))

def split_proj(h, w):
    u = h @ w
    parts = {}
    start = 0
    for name, size in IN_SPLITS:
        parts[name] = u[..., start:start + size]
        start += size
    return parts

def flip(t):
    return jnp.flip(t, axis=1)

def axial_rope_angles(rows):
    t = jnp.arange(rows * GRID_W)
    row = (t // GRID_W).astype(jnp.float32)
    col = (t % GRID_W).astype(jnp.float32)
    n_freq = A_ROPE // 4
    inv_freq = 1.0 / (ROPE_BASE ** (jnp.arange(n_freq, dtype=jnp.float32) / n_freq))
    ang = jnp.concatenate([row[:, None] * inv_freq, col[:, None] * inv_freq], axis=-1)
    return jnp.cos(ang), jnp.sin(ang)

def rope_tail(t, cos, sin):
    head, tail = t[..., :A_NOPE], t[..., A_NOPE:]
    pairs = tail.astype(jnp.float32).reshape(tail.shape[:-1] + (A_ROPE // 2, 2))
    x1, x2 = pairs[..., 0], pairs[..., 1]
    cs, sn = cos[None, :, None, :], sin[None, :, None, :]
    rot = jnp.stack([x1 * cs - x2 * sn, x1 * sn + x2 * cs], axis=-1).reshape(tail.shape)
    return jnp.concatenate([head, rot.astype(t.dtype)], axis=-1)

def mla_queries(cq, P, l):
    q = rmsnorm(cq, P['a_q_norm'][l]) @ P['a_wq'][l]
    q = q.reshape(q.shape[:2] + (A_HEADS, A_QK))
    return rmsnorm(q, P['a_qk_qnorm'][l])

def mla_keys_values(ckv, krope, P, l):
    kv = (ckv @ P['a_wkv'][l]).reshape(ckv.shape[:2] + (A_HEADS, A_NOPE + A_V))
    k_nope, v = kv[..., :A_NOPE], kv[..., A_NOPE:]
    k_rope = jnp.broadcast_to(krope[:, :, None, :], k_nope.shape[:3] + (A_ROPE,))
    k = rmsnorm(jnp.concatenate([k_nope, k_rope], axis=-1), P['a_qk_knorm'][l])
    return k, v

def attend(q, k, v):
    Bsz, Lq, H, dk = q.shape
    nb = Lq // ATTN_BLOCK
    scale = dk ** -0.5
    qb = jnp.moveaxis(q.reshape(Bsz, nb, ATTN_BLOCK, H, dk), 1, 0)

    def one_block(qblk):
        s = jnp.einsum('bqhd,bkhd->bhqk', qblk, k).astype(jnp.float32) * scale
        p = jax.nn.softmax(s, axis=-1).astype(v.dtype)
        return jnp.einsum('bhqk,bkhd->bqhd', p, v)

    o = lax.map(one_block, qb)
    return jnp.moveaxis(o, 0, 1).reshape(Bsz, Lq, H, v.shape[-1])

def gla_log_decay(low, w, b):
    return jax.nn.log_sigmoid((low @ w + b).astype(jnp.float32)) / B_GATE_NORM

def gla_chunked(q, k, v, logg, s0):
    Bsz, L, H, DK = q.shape
    DV = v.shape[-1]
    n, C = L // B_CHUNK, B_CHUNK
    qc = q.astype(jnp.float32).reshape(Bsz, n, C, H, DK) * (DK ** -0.5)
    kc = k.astype(jnp.float32).reshape(Bsz, n, C, H, DK)
    vc = v.astype(jnp.float32).reshape(Bsz, n, C, H, DV)
    bcum = jnp.cumsum(logg.reshape(Bsz, n, C, H, DK), axis=2)
    causal = jnp.tril(jnp.ones((C, C), dtype=bool))[:, :, None, None]
    rel = jnp.exp(jnp.where(causal, bcum[:, :, :, None] - bcum[:, :, None, :], -jnp.inf))
    attn = jnp.einsum('bnihd,bnjhd,bnijhd->bnhij', qc, kc, rel)
    o_intra = jnp.einsum('bnhij,bnjhv->bnihv', attn, vc)
    btot = bcum[:, :, -1]
    ds = jnp.einsum('bnjhd,bnjhv->bnhdv', kc * jnp.exp(btot[:, :, None] - bcum), vc)

    def step(s, inp):
        dec, d = inp
        return dec[..., None] * s + d, s

    s_fin, s_prev = lax.scan(step, s0.astype(jnp.float32),
                             (jnp.moveaxis(jnp.exp(btot), 1, 0), jnp.moveaxis(ds, 1, 0)))
    o_inter = jnp.einsum('bnihd,bnhdv->bnihv', qc * jnp.exp(bcum), jnp.moveaxis(s_prev, 0, 1))
    o = (o_intra + o_inter).reshape(Bsz, L, H, DV)
    return o.astype(v.dtype), s_fin

def ssd_chunked(x, dt, A, Bm, Cm, s0):
    Bsz, L, H, P = x.shape
    G, N = Bm.shape[2], Bm.shape[3]
    R = H // G
    n, C = L // C_CHUNK, C_CHUNK
    xc = x.astype(jnp.float32).reshape(Bsz, n, C, G, R, P)
    dtc = dt.reshape(Bsz, n, C, G, R)
    Bc = Bm.astype(jnp.float32).reshape(Bsz, n, C, G, N)
    Cc = Cm.astype(jnp.float32).reshape(Bsz, n, C, G, N)
    acum = jnp.cumsum(dtc * A.reshape(G, R), axis=2)
    causal = jnp.tril(jnp.ones((C, C), dtype=bool))[:, :, None, None]
    Lm = jnp.exp(jnp.where(causal, acum[:, :, :, None] - acum[:, :, None, :], -jnp.inf))
    CB = jnp.einsum('bnigs,bnjgs->bnijg', Cc, Bc)
    y_diag = jnp.einsum('bnijg,bnijgr,bnjgr,bnjgrp->bnigrp', CB, Lm, dtc, xc)
    atot = acum[:, :, -1]
    wj = jnp.exp(atot[:, :, None] - acum) * dtc
    ds = jnp.einsum('bnjgr,bnjgrp,bnjgs->bngrps', wj, xc, Bc)

    def step(s, inp):
        dec, d = inp
        return dec[..., None, None] * s + d, s

    s0g = s0.astype(jnp.float32).reshape(Bsz, G, R, P, N)
    s_fin, s_prev = lax.scan(step, s0g, (jnp.moveaxis(jnp.exp(atot), 1, 0), jnp.moveaxis(ds, 1, 0)))
    y_off = jnp.einsum('bnigs,bngrps,bnigr->bnigrp', Cc, jnp.moveaxis(s_prev, 0, 1), jnp.exp(acum))
    y = (y_diag + y_off).reshape(Bsz, L, H, P)
    return y.astype(x.dtype), s_fin.reshape(Bsz, H, P, N)

def dwconv_centred(x, w, b):
    K, Ch = w.shape
    y = lax.conv_general_dilated(x, w[:, None, :], window_strides=(1,),
                                 padding=[((K - 1) // 2, (K - 1) // 2)],
                                 dimension_numbers=('NWC', 'WIO', 'NWC'),
                                 feature_group_count=Ch)
    return y + b

def gla_branch(u, P, l, s0_fwd, s0_bwd):
    Bsz, L = u['b_q'].shape[:2]
    hk = (Bsz, L, B_HEADS, B_DK)
    hv = (Bsz, L, B_HEADS, B_DV)
    q = u['b_q'].reshape(hk)
    k = u['b_k'].reshape(hk)
    v = u['b_v'].reshape(hv)
    g_f = gla_log_decay(u['b_gf'], P['b_wg'][l, 0], P['b_bg'][l, 0]).reshape(hk)
    g_b = gla_log_decay(u['b_gb'], P['b_wg'][l, 1], P['b_bg'][l, 1]).reshape(hk)
    o_f, s_f = gla_chunked(q, k, v, g_f, s0_fwd)
    o_b, s_b = gla_chunked(flip(q), flip(k), flip(v), flip(g_b), s0_bwd)
    o = rmsnorm(o_f + flip(o_b), P['b_onorm'][l]) * jax.nn.silu(u['b_og']).reshape(hv)
    return o.reshape(Bsz, L, B_HEADS * B_DV) @ P['b_wo'][l], s_f, s_b

def ssd_branch(u, P, l, s0_fwd, s0_bwd):
    Bsz, L = u['c_z'].shape[:2]
    xbc = jax.nn.silu(dwconv_centred(u['c_xbc'], P['c_conv_w'][l], P['c_conv_b'][l]))
    xs = xbc[..., :C_INNER].reshape(Bsz, L, C_HEADS, C_HEADDIM)
    Bm = xbc[..., C_INNER:C_INNER + C_GROUPS * C_STATE].reshape(Bsz, L, C_GROUPS, C_STATE)
    Cm = xbc[..., C_INNER + C_GROUPS * C_STATE:].reshape(Bsz, L, C_GROUPS, C_STATE)
    dt_f = jax.nn.softplus(u['c_dtf'].astype(jnp.float32) + P['c_dt_bias'][l, 0].astype(jnp.float32))
    dt_b = jax.nn.softplus(u['c_dtb'].astype(jnp.float32) + P['c_dt_bias'][l, 1].astype(jnp.float32))
    A_f = -jnp.exp(P['c_A_log'][l, 0].astype(jnp.float32))
    A_b = -jnp.exp(P['c_A_log'][l, 1].astype(jnp.float32))
    y_f, s_f = ssd_chunked(xs, dt_f, A_f, Bm, Cm, s0_fwd)
    y_b, s_b = ssd_chunked(flip(xs), flip(dt_b), A_b, flip(Bm), flip(Cm), s0_bwd)
    y = y_f + flip(y_b) + P['c_D'][l][:, None] * xs
    y = rmsnorm(y.reshape(Bsz, L, C_INNER) * jax.nn.silu(u['c_z']), P['c_norm'][l])
    return y @ P['c_wo'][l], s_f, s_b

def mixer_sublayer(h, P, l, ctx_kv, gla0, ssd0, rope):
    u = split_proj(h, P['w_in'][l])
    ckv = rmsnorm(u['a_ckv'], P['a_kv_norm'][l])
    krope = u['a_krope']
    q = mla_queries(u['a_cq'], P, l)
    k, v = mla_keys_values(ckv, krope, P, l)
    if rope is not None:
        q = rope_tail(q, rope[0], rope[1])
        k = rope_tail(k, rope[0], rope[1])
    if ctx_kv is not None:
        k = jnp.concatenate([k, ctx_kv[0]], axis=1)
        v = jnp.concatenate([v, ctx_kv[1]], axis=1)
    Bsz, L = h.shape[:2]
    o_a = attend(q, k, v).reshape(Bsz, L, A_HEADS * A_V) @ P['a_wo'][l]
    o_b, sg_f, sg_b = gla_branch(u, P, l, gla0[0], gla0[1])
    o_c, ss_f, ss_b = ssd_branch(u, P, l, ssd0[0], ssd0[1])
    g = jax.nn.sigmoid(u['gates'].astype(jnp.float32)).astype(h.dtype)
    g = g.reshape(Bsz, L, 3, D_MODEL)
    merged = g[:, :, 0] * o_a + g[:, :, 1] * o_b + g[:, :, 2] * o_c
    out = merged @ P['w_out'][l]
    return out, ckv, krope, jnp.stack([sg_f, sg_b], axis=1), jnp.stack([ss_f, ss_b], axis=1)

def moe(h, P, l):
    Bsz, L, D = h.shape
    t = h.reshape(Bsz * L, D)
    scores = jax.nn.sigmoid((t @ P['router_w']).astype(jnp.float32))
    sel = scores + P['router_bias'].astype(jnp.float32)
    per_group = N_EXPERTS // N_EXPERT_GROUPS
    group_score = jnp.sum(lax.top_k(sel.reshape(-1, N_EXPERT_GROUPS, per_group), TOP_K)[0], axis=-1)
    best = jnp.argmax(group_score, axis=-1)
    in_group = jnp.arange(N_EXPERTS)[None, :] // per_group == best[:, None]
    _, idx = lax.top_k(jnp.where(in_group, sel, -jnp.inf), TOP_K)
    w = jnp.take_along_axis(scores, idx, axis=-1)
    w = w / jnp.sum(w, axis=-1, keepdims=True)
    gate = jnp.einsum('tk,tke->te', w, jax.nn.one_hot(idx, N_EXPERTS, dtype=jnp.float32)).astype(h.dtype)
    hid = jax.nn.silu(jnp.einsum('td,edf->tef', t, P['e_w1'][l])) * jnp.einsum('td,edf->tef', t, P['e_w3'][l])
    out = jnp.einsum('tef,efd->td', hid * gate[:, :, None], P['e_w2'][l])
    return out.reshape(Bsz, L, D)

def trunk_layer(x, cvec, P, l, ctx_kv, gla0, ssd0, rope):
    m = modulation(cvec, P['w_ada'][l], P['b_ada'][l])
    h = ada_rmsnorm(x, P['norm1'][l], m[:, None, 0], m[:, None, 1])
    mix, ckv, krope, s_gla, s_ssd = mixer_sublayer(h, P, l, ctx_kv, gla0, ssd0, rope)
    x = x + m[:, None, 2] * mix
    h = ada_rmsnorm(x, P['norm2'][l], m[:, None, 3], m[:, None, 4])
    x = x + m[:, None, 5] * moe(h, P, l)
    return x, ckv, krope, s_gla, s_ssd

def setup_inputs(seed: int = 0) -> dict:
    key = jax.random.key(seed)
    keys = iter(jax.random.split(key, 40))

    def nrm(shape, scale):
        return scale * jax.random.normal(next(keys), shape, dtype=jnp.float32)

    def gain(shape):
        return 1.0 + 0.05 * jax.random.normal(next(keys), shape, dtype=jnp.float32)

    dt = jnp.exp(jax.random.uniform(next(keys), (DEPTH, 2, C_HEADS), dtype=jnp.float32,
                                    minval=math.log(1e-3), maxval=math.log(1e-1)))
    c_dt_bias = dt + jnp.log(-jnp.expm1(-dt))
    c_A_log = jnp.log(jax.random.uniform(next(keys), (DEPTH, 2, C_HEADS), dtype=jnp.float32,
                                         minval=1.0, maxval=16.0))
    hbk = B_HEADS * B_DK
    hbv = B_HEADS * B_DV
    return {
        'x_prompt': nrm((BATCH, SEQ, D_MODEL), 1.0),
        'x_sample': nrm((DEC_BATCH, DEC_SEQ, D_MODEL), 1.0),
        'cache_ckv': nrm((DEC_BATCH, DEPTH, PAST_LEN, A_KVLORA), 1.0),
        'cache_krope': nrm((DEC_BATCH, DEPTH, PAST_LEN, A_ROPE), 1.0),
        'state_gla': nrm((DEC_BATCH, DEPTH, 2, B_HEADS, B_DK, B_DV), 1.0),
        'state_ssd': nrm((DEC_BATCH, DEPTH, 2, C_HEADS, C_HEADDIM, C_STATE), 0.1),
        'c': nrm((DEC_BATCH, D_MODEL), 1.0),
        'c_ctx': nrm((D_MODEL,), 1.0),
        'w_ada': nrm((DEPTH, D_MODEL, 6 * D_MODEL), 0.5 * D_MODEL ** -0.5),
        'b_ada': nrm((DEPTH, 6 * D_MODEL), 0.02),
        'norm1': gain((DEPTH, D_MODEL)),
        'norm2': gain((DEPTH, D_MODEL)),
        'w_in': nrm((DEPTH, D_MODEL, D_IN), D_MODEL ** -0.5),
        'a_q_norm': gain((DEPTH, A_QLORA)),
        'a_wq': nrm((DEPTH, A_QLORA, A_HEADS * A_QK), A_QLORA ** -0.5),
        'a_kv_norm': gain((DEPTH, A_KVLORA)),
        'a_wkv': nrm((DEPTH, A_KVLORA, A_HEADS * (A_NOPE + A_V)), A_KVLORA ** -0.5),
        'a_qk_qnorm': gain((DEPTH, A_QK)),
        'a_qk_knorm': gain((DEPTH, A_QK)),
        'a_wo': nrm((DEPTH, A_HEADS * A_V, D_MODEL), (A_HEADS * A_V) ** -0.5),
        'b_wg': nrm((DEPTH, 2, B_GATE_RANK, hbk), B_GATE_RANK ** -0.5),
        'b_bg': nrm((DEPTH, 2, hbk), 0.1),
        'b_onorm': gain((DEPTH, B_DV)),
        'b_wo': nrm((DEPTH, hbv, D_MODEL), hbv ** -0.5),
        'c_conv_w': nrm((DEPTH, C_CONV, C_XBC), C_CONV ** -0.5),
        'c_conv_b': nrm((DEPTH, C_XBC), 0.02),
        'c_dt_bias': c_dt_bias,
        'c_A_log': c_A_log,
        'c_D': gain((DEPTH, C_HEADS)),
        'c_norm': gain((DEPTH, C_INNER)),
        'c_wo': nrm((DEPTH, C_INNER, D_MODEL), C_INNER ** -0.5),
        'w_out': nrm((DEPTH, D_MODEL, D_MODEL), D_MODEL ** -0.5),
        'router_w': nrm((D_MODEL, N_EXPERTS), D_MODEL ** -0.5),
        'router_bias': nrm((N_EXPERTS,), 0.01),
        'e_w1': nrm((DEPTH, N_EXPERTS, D_MODEL, D_EXPERT), D_MODEL ** -0.5),
        'e_w3': nrm((DEPTH, N_EXPERTS, D_MODEL, D_EXPERT), D_MODEL ** -0.5),
        'e_w2': nrm((DEPTH, N_EXPERTS, D_EXPERT, D_MODEL), D_EXPERT ** -0.5),
    }

def reference(x_prompt, x_sample, cache_ckv, cache_krope, state_gla, state_ssd, c, c_ctx,
              w_ada, b_ada, norm1, norm2, w_in, a_q_norm, a_wq, a_kv_norm, a_wkv,
              a_qk_qnorm, a_qk_knorm, a_wo, b_wg, b_bg, b_onorm, b_wo, c_conv_w, c_conv_b,
              c_dt_bias, c_A_log, c_D, c_norm, c_wo, w_out, router_w, router_bias,
              e_w1, e_w3, e_w2):
    P = dict(w_ada=w_ada, b_ada=b_ada, norm1=norm1, norm2=norm2, w_in=w_in,
             a_q_norm=a_q_norm, a_wq=a_wq, a_kv_norm=a_kv_norm, a_wkv=a_wkv,
             a_qk_qnorm=a_qk_qnorm, a_qk_knorm=a_qk_knorm, a_wo=a_wo,
             b_wg=b_wg, b_bg=b_bg, b_onorm=b_onorm, b_wo=b_wo,
             c_conv_w=c_conv_w, c_conv_b=c_conv_b, c_dt_bias=c_dt_bias, c_A_log=c_A_log,
             c_D=c_D, c_norm=c_norm, c_wo=c_wo, w_out=w_out,
             router_w=router_w, router_bias=router_bias, e_w1=e_w1, e_w3=e_w3, e_w2=e_w2)

    bp = x_prompt.shape[0]
    z_gla = jnp.zeros((bp, B_HEADS, B_DK, B_DV), jnp.float32)
    z_ssd = jnp.zeros((bp, C_HEADS, C_HEADDIM, C_STATE), jnp.float32)
    xp = x_prompt
    ckvs, kropes, glas, ssds = [], [], [], []
    for l in range(DEPTH):
        xp, ckv, krope, s_gla, s_ssd = trunk_layer(xp, c_ctx[None], P, l, None,
                                                   (z_gla, z_gla), (z_ssd, z_ssd), None)
        ckvs.append(ckv)
        kropes.append(krope)
        glas.append(s_gla)
        ssds.append(s_ssd)
    y_prompt = xp
    new_ckv = jnp.stack(ckvs, axis=1)
    new_krope = jnp.stack(kropes, axis=1)
    new_state_gla = jnp.stack(glas, axis=1).astype(x_prompt.dtype)
    new_state_ssd = jnp.stack(ssds, axis=1).astype(x_prompt.dtype)

    rows = x_sample.shape[1] // GRID_W
    rope = axial_rope_angles(rows)
    xs = x_sample
    for l in range(DEPTH):
        k_ctx, v_ctx = mla_keys_values(cache_ckv[:, l], cache_krope[:, l], P, l)
        xs = trunk_layer(xs, c, P, l, (k_ctx, v_ctx),
                         (state_gla[:, l, 0], state_gla[:, l, 1]),
                         (state_ssd[:, l, 0], state_ssd[:, l, 1]), rope)[0]
    y_sample = xs
    return (y_prompt, y_sample, new_ckv, new_krope, new_state_gla, new_state_ssd)


_drawn_inputs = setup_inputs


def setup_inputs(seed=0):
    import zlib

    import numpy as np

    out = dict(_drawn_inputs(seed))
    spreads = {}
    factors = {'cache_ckv': 2.781,
     'cache_krope': 2.978,
     'state_gla': 3.83,
     'a_q_norm': 2.992,
     'a_qk_knorm': 4.683,
     'c_D': 3.313}
    for name, (base, spread) in spreads.items():
        noise = np.random.default_rng([zlib.crc32(name.encode()), seed]).standard_normal(out[name].shape)
        drawn = base * np.exp(spread * noise) if base else spread * noise
        out[name] = jnp.asarray(drawn.astype(out[name].dtype))
    for name, factor in factors.items():
        out[name] = (out[name] * factor).astype(out[name].dtype)
    return out
```

```python
from contextlib import ExitStack

import concourse.bass as bass
from concourse import mybir

F32 = mybir.dt.float32
ALU = mybir.AluOpType
ACT = mybir.ActivationFunctionType
AX_X = mybir.AxisListType.X

P = 128
D = 1024
DEPTH = 2
NT = 3
T = NT * P
KD = D // P
EPS = 1e-6
H_A, NOPE, ROPE, V_A = 16, 64, 32, 64
QK = NOPE + ROPE
QL, KVL = 512, 256
NKT = NT + 1
H_B, DK, DV = 4, 128, 256
RANK = 16
GATE_NORM = 16.0
H_C, HP, N_ST, G_C = 16, 64, 128, 2
XBC = H_C * HP + 2 * G_C * N_ST
NX = XBC // P
TAPS = 5
PAD = TAPS // 2
X_P, X_S = PAD, 3 * PAD + P
XW = X_S + 2 * P + PAD
YW = XW - 2 * PAD
NE, NG = 16, 4
EG = NE // NG
DE = 512
BIG = 1e30
CLAMP = 80.0

CQ, CKV, KROPE, BQ, BK, BV, OG, GLOW, Z, CX, DTC, GATES = (
    0, 512, 768, 800, 1312, 1824, 2848, 3872, 3904, 4928, 6464, 6496)

C_ID, C_REL, C_CUM, C_AFT, C_ONE, C_SEL, C_COS, C_SIN, C_RANK = 0, 128, 384, 640, 896, 1024, 1026, 1058, 1090
N_CONST = 1106
V_N1, V_N2, V_BADA, V_QN, V_KVN, V_CN, V_BON, V_CW, V_CB = 0, 8, 16, 64, 68, 70, 78, 86, 146
N_VEC = 158
R_QW, R_KW, R_DTB, R_ALOG, R_D, R_RB = 0, 96, 192, 224, 256, 272
N_ROW = 288

N_ADA = 12
W_CQ, W_CKV, W_WQ, W_WKV, W_GA, W_AO = 12, 13, 14, 16, 17, 19
W_BQ, W_BK, W_BV, W_OG, W_GB, W_BO = 21, 22, 23, 25, 27, 29
W_Z, W_CX, W_GC, W_CO, W_OUT, W_MOE = 31, 33, 36, 38, 40, 42
RING = 3


def trunk_kernel(nc, x, cond, consts, vecs, rows, w_small, w_gate_low, router_w, cache_ckv, cache_krope,
                 state_gla, state_ssd, w_ada, w_in, a_wq, a_wkv, a_wo, b_wo, c_wo, w_out, e_w1, e_w3, e_w2,
                 y, new_ckv, new_krope, new_gla, new_ssd):
    with ExitStack() as ctx:
        def sb(name, shape):
            return ctx.enter_context(nc.sbuf_tensor(name, shape, F32))

        ring = sb("ring", [P, RING, 4096])
        xT = sb("xT", [P, KD, T])
        hT = sb("hT", [P, KD, T])
        mT = sb("mT", [P, KD, T])
        cst = sb("cst", [P, N_CONST])
        vec = sb("vec", [P, N_VEC])
        row = sb("row", [P, N_ROW])
        wsm = sb("wsm", [P, KD, 96])
        wgl = sb("wgl", [2 * RANK + 1, 2, 512])
        rw = sb("rw", [P, KD, NE])
        condT = sb("condT", [P, KD, 2])
        scond = sb("scond", [P, KD, 2])
        mod = sb("mod", [P, 6, KD, 2])
        amp = sb("amp", [P, 2, KD, 2])
        dtraw = sb("dtraw", [P, NT, 32])
        lowT = sb("lowT", [2 * RANK + 1, T])
        rstd = sb("rstd", [P, T])
        arena = sb("arena", [P, 26500])
        ps = ctx.enter_context(nc.psum_tensor("ps", [P, 8, 512], F32))

        names = (
            "xin", "cond_ready", "params_in", "cache_in", "squares_ready", "root_ready", "weighted",
            "h_ready", "cqn_ready", "ckvn_ready", "sq_ready", "stat_ready", "head_root", "rotary_in",
            "nmax_ready", "abs_ready", "soft_ready", "logdecay_ready", "clamped_ready", "decay_ready",
            "qk_ready", "gla_state_in", "scaled_state", "state_ready", "o_ready", "conv_ready",
            "xbc_ready", "ssd_state_in", "diff_ready", "decayed_ready", "mask_ready", "xw_ready",
            "yoff_ready", "y_ready", "merged_ready", "zeroed", "hidden_ready", "moe_ready", "stored",
            "act_step", "dve_step", "pool_step")
        sem = {n: ctx.enter_context(nc.semaphore(n)) for n in names}
        w_loaded = [ctx.enter_context(nc.semaphore(f"w_loaded{i}")) for i in range(RING)]
        psum_full = [ctx.enter_context(nc.semaphore(f"psum_full{i}")) for i in range(8)]
        psum_free = [ctx.enter_context(nc.semaphore(f"psum_free{i}")) for i in range(8)]

        count, waited = {}, {}
        job = {}
        uses = [0] * 8
        turn = [0]
        last_use = {}

        def counts(name):
            count[name] = count.get(name, 0) + 1
            return sem[name], 1

        def counted(name):
            return sem[name], count[name]

        def following(eng, name, by=1):
            key = (str(eng.engine), name)
            waited[key] = waited.get(key, 0) + by
            return sem[name], waited[key]

        def claim(pe, key, bank=None):
            if bank is None:
                bank = turn[0] % 8
                turn[0] += 1
            job[key] = (bank, uses[bank])
            if uses[bank]:
                pe.wait_ge(psum_free[bank], uses[bank])
            uses[bank] += 1
            return ps[:, bank, :]

        def bank(key):
            return ps[:, job[key][0], :]

        def makes(key):
            return psum_full[job[key][0]], 1

        def made(key):
            return psum_full[job[key][0]], job[key][1] + 1

        def reads(key):
            return psum_free[job[key][0]], 1

        def read(key):
            return psum_free[job[key][0]], job[key][1] + 1

        def carve(off, *shape):
            n = 1
            for s in shape:
                n *= s
            v = arena[:, off:off + n]
            if len(shape) == 2:
                return v.rearrange("p (a b) -> p a b", b=shape[1])
            if len(shape) == 3:
                return v.rearrange("p (a b c) -> p a b c", b=shape[1], c=shape[2])
            if len(shape) == 4:
                return v.rearrange("p (a b c d) -> p a b c d", b=shape[1], c=shape[2], d=shape[3])
            return v

        ident = cst[:, C_ID:C_ID + P]
        ones = cst[:, C_ONE:C_ONE + P]

        def rel(d):
            return cst[:, C_REL + P * d:C_REL + P * d + P]

        def cum(d):
            return cst[:, C_CUM + P * d:C_CUM + P * d + P]

        def aft(d):
            return cst[:, C_AFT + P * d:C_AFT + P * d + P]

        COND = ((slice(0, P), 0), (slice(P, T), 1))

        def tok(t):
            return slice(t * P, t * P + P)

        def quad(ap):
            return ap.rearrange("p (a b) -> p a b", b=P)

        def over(ap, n):
            return ap.unsqueeze(2).broadcast_to([ap.shape[0], ap.shape[1], n])

        def each(ap, n):
            return ap.unsqueeze(1).broadcast_to([ap.shape[0], n, ap.shape[1]])

        def chunk(n, k, w):
            return ring[:, n % RING, 0:k * w].rearrange("p (k w) -> p k w", k=k)

        def kpn(ap, i):
            return ap[bass.ds(i, 1)].rearrange("a (k p) n -> p (a k) n", p=P)

        def weight_source(n, l):
            cols = {W_CQ: (CQ, 512), W_CKV: (CKV, KVL), W_BQ: (BQ, 512), W_BK: (BK, 512)}
            for base, col, m in ((W_GA, GATES, 2), (W_GB, GATES + D, 2), (W_GC, GATES + 2 * D, 2), (W_BV, BV, 2),
                                 (W_OG, OG, 2), (W_Z, Z, 2), (W_CX, CX, 3)):
                for i in range(m):
                    cols[base + i] = (col + 512 * i, 512)
            if n < N_ADA:
                return kpn(w_ada, l)[:, :, 512 * n:512 * n + 512], KD, 512
            if n in cols:
                c, w = cols[n]
                return kpn(w_in, l)[:, :, c:c + w], KD, w
            if n in (W_WQ, W_WQ + 1):
                i = n - W_WQ
                return kpn(a_wq, l)[:, :, 768 * i:768 * i + 768], QL // P, 768
            if n == W_WKV:
                return kpn(a_wkv, l), KVL // P, 2048
            for base, ap in ((W_AO, a_wo), (W_BO, b_wo), (W_CO, c_wo), (W_OUT, w_out)):
                if n in (base, base + 1):
                    return kpn(ap, l)[:, :, 512 * (n - base):512 * (n - base) + 512], KD, 512
            raise AssertionError(n)

        def expert_source(i, l, e):
            k = (KD, KD, DE // P)[i]
            return kpn((e_w1, e_w3, e_w2)[i], l * NE + e), k, 4096 // k

        def load_weights(sp, l, n0, n1):
            for n in range(n0, n1):
                if n >= RING:
                    sp.wait_ge(*made(last_use[n - RING]))
                src, k, w = weight_source(n, l) if n < W_MOE else expert_source(n - W_MOE, l, 0)
                sp.dma_start(chunk(n, k, w), src).then_inc(w_loaded[n % RING], 16)

        def weights(pe, n, k, w):
            pe.wait_ge(w_loaded[n % RING], 16 * (n // RING + 1))
            return chunk(n, k, w)

        def matmuls(pe, out, pairs):
            for i, (a, b) in enumerate(pairs):
                ins = pe.matmul(out, a, b, start=(i == 0), stop=(i == len(pairs) - 1))
            return ins

        def feature_major(pe, n, key, src, m=4):
            w = weights(pe, n, KD, P * m)
            for j in range(m):
                matmuls(pe, claim(pe, (key, j))[:, 0:T],
                        [(w[:, k, P * j:P * j + P], src[:, k, :]) for k in range(KD)]).then_inc(*makes((key, j)))
            last_use[n] = (key, m - 1)

        def token_major(pe, n, key):
            w = weights(pe, n, KD, 512)
            for t in range(NT):
                matmuls(pe, claim(pe, (key, t)), [(hT[:, k, tok(t)], w[:, k, :]) for k in range(KD)]).then_inc(*makes((key, t)))
            last_use[n] = (key, NT - 1)

        def square_sum(pe, key, sq, kd, made_from=()):
            out = claim(pe, key)
            if not made_from:
                pe.wait_ge(*following(pe, "squares_ready"))
            for k in made_from:
                pe.wait_ge(*read(k))
            matmuls(pe, out[:, 0:T], [(ones, sq[:, k, :]) for k in range(kd)]).then_inc(*makes(key))

        def transposed(pe, key, srcs, bank=None):
            out = claim(pe, key, bank)
            for i, s in enumerate(srcs):
                ins = pe.transpose(out[0:s.shape[1], i * P:i * P + P], s, ident)
            ins.then_inc(*makes(key))

        def root_mean(dve, key, n):
            dve.wait_ge(*made(key))
            s = bank(key)
            dve.tensor_scalar(rstd[:, :], s[:, 0:T], 1.0 / n, EPS, ALU.mult, ALU.add).then_inc(*reads(key))
            dve.wait_ge(*read(key))
            dve.wait_ge(*following(dve, "root_ready"))
            dve.reciprocal(rstd[:, :], rstd[:, :]).then_inc(*counts("dve_step"))
            dve.wait_ge(*counted("dve_step"))

        def root(act, key):
            act.wait_ge(*read(key))
            act.activation(rstd[:, :], rstd[:, :], ACT.Sqrt).then_inc(*counts("root_ready"))

        def norm_dve(dve, key):
            root_mean(dve, key, D)
            dve.tensor_tensor(hT[:, :, :], xT[:, :, :], each(rstd[:, :], KD), ALU.mult).then_inc(*counts("weighted"))

        def norm_act(act, i, key, sq):
            act.activation(sq, xT[:, :, :], ACT.Square).then_inc(*counts("squares_ready"))
            root(act, key)
            act.wait_ge(*following(act, "weighted"))
            for k in range(KD):
                for ts, c in COND:
                    ins = act.activation(hT[:, k, ts], hT[:, k, ts], ACT.Identity,
                                         bias=mod[:, 3 * i, k, c:c + 1], scale=amp[:, i, k, c:c + 1])
            ins.then_inc(*counts("h_ready"))

        def gate_act(act, key, gT):
            for i in range(2):
                for j in range(4):
                    act.wait_ge(*made(((key, i), j)))
                    s = bank(((key, i), j))
                    act.activation(gT[:, 4 * i + j, :], s[:, 0:T], ACT.Sigmoid).then_inc(*reads(((key, i), j)))
                    act.wait_ge(*read(((key, i), j)))

        def gated_sum(dve, key, gkey, gT, first):
            for i in range(2):
                for j in range(4):
                    d = 4 * i + j
                    dve.wait_ge(*made(((key, i), j)))
                    s = bank(((key, i), j))
                    dve.wait_ge(*read(((gkey, i), j)))
                    if first:
                        dve.tensor_tensor(mT[:, d, :], s[:, 0:T], gT[:, d, :], ALU.mult).then_inc(*reads(((key, i), j)))
                        dve.wait_ge(*read(((key, i), j)))
                    else:
                        dve.tensor_tensor(gT[:, d, :], s[:, 0:T], gT[:, d, :], ALU.mult).then_inc(*reads(((key, i), j)))
                        dve.wait_ge(*read(((key, i), j)))
                        ins = dve.tensor_tensor(mT[:, d, :], mT[:, d, :], gT[:, d, :], ALU.add)
                        ins.then_inc(*counts("dve_step"))
                        dve.wait_ge(*counted("dve_step"))

        def to_features(pe, key, src):
            for t in range(NT):
                for q in range(2):
                    transposed(pe, (key, t, q), [src[:, t, 512 * q + P * i:512 * q + P * i + P] for i in range(4)])

        def features_dve(dve, key, dst, w=None):
            for t in range(NT):
                for q in range(2):
                    dve.wait_ge(*made((key, t, q)))
                    s = quad(bank((key, t, q)))
                    out = dst[:, 4 * q:4 * q + 4, tok(t)]
                    if w is None:
                        ins = dve.tensor_copy(out, s)
                    else:
                        ins = dve.tensor_tensor(out, s, over(vec[:, w + 4 * q:w + 4 * q + 4], P), ALU.mult)
                    ins.then_inc(*reads((key, t, q)))
                    dve.wait_ge(*read((key, t, q)))

        def project_pe(pe, n, key, src, tkey):
            for t in range(NT):
                for q in range(2):
                    pe.wait_ge(*read((tkey, t, q)))
            for i in range(2):
                feature_major(pe, n + i, (key, i), src)

        x_in = carve(0, NT, D)
        with nc.Block() as block:
            @block.tensor
            def _(pe):
                pe.wait_ge(sem["xin"], 64)
                to_features(pe, "x", x_in)

            @block.sync
            def _(sp):
                sp.dma_start(x_in, x.rearrange("(t p) d -> p t d", p=P)).then_inc(sem["xin"], 16)
                sp.dma_start(cst[:, :], consts).then_inc(sem["xin"], 16)
                sp.dma_start(condT[:, :, :], cond).then_inc(sem["xin"], 16)
                sp.dma_start(rw[:, :, :], router_w.rearrange("(k p) e -> p k e", p=P)).then_inc(sem["xin"], 16)
                sp.wait_ge(sem["xin"], 64)

            @block.vector
            def _(dve):
                dve.memset(lowT[2 * RANK:2 * RANK + 1, :], 1.0).then_inc(*counts("dve_step"))
                dve.wait_ge(*counted("dve_step"))
                features_dve(dve, "x", xT)

            @block.scalar
            def _(act):
                act.wait_ge(sem["xin"], 64)
                act.activation(scond[:, :, :], condT[:, :, :], ACT.Silu).then_inc(*counts("cond_ready"))
                act.wait_ge(*counted("cond_ready"))

        def clear_counts():
            for s in list(sem.values()) + w_loaded + psum_full + psum_free:
                nc.sync.sem_clear(s)
            nc.all_engine_barrier()
            for d in (count, waited, job, last_use):
                d.clear()
            for b in range(8):
                uses[b] = 0

        clear_counts()

        q_tok = carve(0, NT, H_A, QK)
        k_tok = carve(4608, NKT, H_A, QK)
        v_a = carve(10752, NKT, H_A, V_A)
        cqT = carve(14848, QL // P, T)
        sq4 = carve(16384, QL // P, T)
        ckvT = carve(17920, KVL // P, T + P)
        kr = carve(18944, NKT, ROPE)
        cache_tok = carve(19072, KVL)
        o_tok = carve(19328, NT, D)
        head_qT = carve(22400, 2, T)
        head_kT = carve(23168, 2, T + P)
        probs = carve(24192, 2, T)
        probsT = carve(24960, 2, T)
        sq2 = carve(22400, KVL // P, T)
        stat = carve(25728, 2, NKT * H_A)
        nmax = carve(25856, 2)
        rsum = carve(25872, NT, H_A)
        ckv_out = carve(25920, KVL)
        rope_tmp = carve(14848, 4, H_A, ROPE // 2)
        sq_heads = carve(19328, NKT * H_A, QK)
        sq_x = carve(19328, KD, T)
        gT = carve(0, KD, T)
        oT = carve(4608, KD, T)

        with nc.Fori(0, DEPTH) as l:
            with nc.Block() as block:
                @block.tensor
                def _(pe):
                    for n in range(N_ADA):
                        w = weights(pe, n, KD, 512)
                        m = claim(pe, ("mod", n))
                        for j in range(4):
                            ins = matmuls(pe, m[:, 2 * j:2 * j + 2],
                                          [(w[:, k, P * j:P * j + P], scond[:, k, :]) for k in range(KD)])
                        ins.then_inc(*makes(("mod", n)))
                        last_use[n] = ("mod", n)
                    square_sum(pe, "n1", sq_x, KD)
                    pe.wait_ge(*following(pe, "h_ready"))
                    feature_major(pe, W_CQ, "cq", hT)
                    feature_major(pe, W_CKV, "ckv", hT, 2)
                    pe.wait_ge(*following(pe, "params_in", 64))
                    out = claim(pe, "krdt")
                    for t in range(NT):
                        ins = matmuls(pe, out[:, 64 * t:64 * t + 64],
                                      [(hT[:, k, tok(t)], wsm[:, k, 0:64]) for k in range(KD)])
                    ins.then_inc(*makes("krdt"))
                    out = claim(pe, "low")
                    matmuls(pe, out[0:2 * RANK, 0:T], [(wsm[:, k, 64:96], hT[:, k, :]) for k in range(KD)]).then_inc(*makes("low"))
                    pe.wait_ge(*following(pe, "cache_in", 32))
                    transposed(pe, "cache", [cache_tok[:, 0:P], cache_tok[:, P:2 * P]])
                    square_sum(pe, "ncq", sq4, QL // P, [("cq", j) for j in range(QL // P)])
                    square_sum(pe, "nckv", sq2, KVL // P, [("ckv", j) for j in range(KVL // P)])
                    pe.wait_ge(*following(pe, "cqn_ready"))
                    for c in range(2):
                        w = weights(pe, W_WQ + c, QL // P, 768)
                        for t in range(NT):
                            for h in range(2):
                                matmuls(pe, claim(pe, ("q", c, t, h))[:, 0:384],
                                        [(cqT[:, k, tok(t)], w[:, k, 384 * h:384 * h + 384])
                                         for k in range(QL // P)]).then_inc(*makes(("q", c, t, h)))
                        last_use[W_WQ + c] = ("q", c, NT - 1, 1)
                    pe.wait_ge(*following(pe, "ckvn_ready"))
                    pe.wait_ge(*read("cache"))
                    transposed(pe, "ckv_out", [ckvT[:, 0, 0:P], ckvT[:, 1, 0:P]])
                    w = weights(pe, W_WKV, KVL // P, 2048)
                    for t in range(NKT):
                        for h in range(4):
                            matmuls(pe, claim(pe, ("kv", t, h)),
                                    [(ckvT[:, k, tok(t)], w[:, k, 512 * h:512 * h + 512])
                                     for k in range(KVL // P)]).then_inc(*makes(("kv", t, h)))
                    last_use[W_WKV] = ("kv", NKT - 1, 3)

                @block.sync
                def _(sp):
                    for dst, src in ((vec[:, :], vecs), (row[:, :], rows)):
                        sp.dma_start(dst, src[bass.ds(l, 1)].rearrange("a p n -> p (a n)")).then_inc(sem["params_in"], 16)
                    sp.dma_start(wsm[:, :, :], kpn(w_small, l)).then_inc(sem["params_in"], 16)
                    sp.dma_start(wgl[:, :, :], w_gate_low[bass.ds(l, 1)].rearrange("a r d n -> r (a d) n")
                                 ).then_inc(sem["params_in"], 16)
                    sp.dma_start(cache_tok, cache_ckv[bass.ds(l, 1)].rearrange("a p n -> p (a n)")
                                 ).then_inc(sem["cache_in"], 16)
                    sp.dma_start(kr[:, NT, :], cache_krope[bass.ds(l, 1)].rearrange("a p n -> p (a n)")
                                 ).then_inc(sem["cache_in"], 16)
                    load_weights(sp, l, 0, W_GA + RING)
                    sp.wait_ge(*read("krdt"))
                    sp.dma_start(new_krope[bass.ds(l, 1)].rearrange("a p n -> p (a n)"), kr[:, 0, :]
                                 ).then_inc(sem["stored"], 16)
                    sp.wait_ge(*read("ckv_out"))
                    sp.dma_start(new_ckv[bass.ds(l, 1)].rearrange("a p n -> p (a n)"), ckv_out
                                 ).then_inc(sem["stored"], 16)
                    sp.wait_ge(*following(sp, "stored", 32))

                @block.scalar
                def _(act):
                    norm_act(act, 0, "n1", sq_x)
                    for j in range(QL // P):
                        act.wait_ge(*made(("cq", j)))
                        s = bank(("cq", j))
                        act.activation(cqT[:, j, :], s[:, 0:T], ACT.Copy).then_inc(*counts("act_step"))
                        act.wait_ge(*counted("act_step"))
                        act.activation(sq4[:, j, :], s[:, 0:T], ACT.Square).then_inc(*reads(("cq", j)))
                        act.wait_ge(*read(("cq", j)))
                    for j in range(KVL // P):
                        act.wait_ge(*made(("ckv", j)))
                        s = bank(("ckv", j))
                        act.activation(ckvT[:, j, 0:T], s[:, 0:T], ACT.Copy).then_inc(*counts("act_step"))
                        act.wait_ge(*counted("act_step"))
                        act.activation(sq2[:, j, :], s[:, 0:T], ACT.Square).then_inc(*reads(("ckv", j)))
                        act.wait_ge(*read(("ckv", j)))
                    root(act, "ncq")
                    root(act, "nckv")
                    for c in range(2):
                        for t in range(NT):
                            for h in range(2):
                                act.wait_ge(*read(("q", c, t, h)))
                    act.activation(sq_heads[:, 0:NT * H_A, :], q_tok.rearrange("p t h d -> p (t h) d"), ACT.Square).then_inc(*counts("sq_ready"))
                    for t in range(NKT):
                        for h in range(4):
                            act.wait_ge(*made(("kv", t, h)))
                            s = bank(("kv", t, h)).rearrange("p (h d) -> p h d", h=4)
                            act.activation(v_a[:, t, 4 * h:4 * h + 4, :], s[:, :, NOPE:], ACT.Copy).then_inc(*counts("act_step"))
                            act.wait_ge(*counted("act_step"))
                            act.activation(k_tok[:, t, 4 * h:4 * h + 4, 0:NOPE], s[:, :, 0:NOPE], ACT.Copy).then_inc(*reads(("kv", t, h)))
                            act.wait_ge(*read(("kv", t, h)))
                    act.wait_ge(*following(act, "stat_ready"))
                    act.activation(stat[:, 0, 0:NT * H_A], stat[:, 0, 0:NT * H_A], ACT.Sqrt).then_inc(*counts("head_root"))
                    act.wait_ge(*following(act, "rotary_in"))
                    act.activation(sq_heads, k_tok.rearrange("p t h d -> p (t h) d"), ACT.Square).then_inc(*counts("sq_ready"))
                    act.wait_ge(*following(act, "stat_ready"))
                    act.activation(stat[:, 1, :], stat[:, 1, :], ACT.Sqrt).then_inc(*counts("head_root"))

                @block.gpsimd
                def _(pool):
                    pool.wait_ge(*following(pool, "cache_in", 32))
                    pool.wait_ge(*read("krdt"))
                    for t in range(NKT):
                        ins = pool.tensor_copy(k_tok[:, t, :, NOPE:], each(kr[:, t, :], H_A))
                    ins.then_inc(*counts("rotary_in"))

                @block.vector
                def _(dve):
                    dve.wait_ge(*following(dve, "params_in", 64))
                    modc = mod.rearrange("p s k c -> p (s k) c")
                    for n in range(N_ADA):
                        dve.wait_ge(*made(("mod", n)))
                        s = bank(("mod", n))
                        dve.tensor_tensor(modc[:, 4 * n:4 * n + 4, :],
                                          s[:, 0:8].rearrange("p (a b) -> p a b", b=2),
                                          over(vec[:, V_BADA + 4 * n:V_BADA + 4 * n + 4], 2), ALU.add).then_inc(*reads(("mod", n)))
                        dve.wait_ge(*read(("mod", n)))
                    for i, w in ((0, V_N1), (1, V_N2)):
                        dve.scalar_tensor_tensor(out=amp[:, i, :, :], in0=mod[:, 3 * i + 1, :, :], scalar=1.0,
                                                 in1=over(vec[:, w:w + KD], 2), op0=ALU.add, op1=ALU.mult).then_inc(*counts("dve_step"))
                        dve.wait_ge(*counted("dve_step"))
                    norm_dve(dve, "n1")
                    dve.wait_ge(*made("krdt"))
                    s = bank("krdt")[:, 0:NT * 64].rearrange("p (t c) -> p t c", c=64)
                    dve.tensor_copy(dtraw[:, :, :], s[:, :, 32:64]).then_inc(*counts("dve_step"))
                    dve.wait_ge(*counted("dve_step"))
                    dve.tensor_copy(kr[:, 0:NT, :], s[:, :, 0:32]).then_inc(*reads("krdt"))
                    dve.wait_ge(*read("krdt"))
                    dve.wait_ge(*made("low"))
                    dve.tensor_copy(lowT[0:2 * RANK, :], bank("low")[0:2 * RANK, 0:T]).then_inc(*reads("low"))
                    dve.wait_ge(*read("low"))
                    dve.wait_ge(*made("cache"))
                    dve.tensor_copy(ckvT[:, :, T:], quad(bank("cache")[:, 0:2 * P])).then_inc(*reads("cache"))
                    dve.wait_ge(*read("cache"))
                    root_mean(dve, "ncq", QL)
                    for j in range(QL // P):
                        ins = dve.scalar_tensor_tensor(out=cqT[:, j, :], in0=cqT[:, j, :], scalar=vec[:, V_QN + j:V_QN + j + 1],
                                                       in1=rstd[:, :], op0=ALU.mult, op1=ALU.mult)
                    ins.then_inc(*counts("cqn_ready"))
                    dve.wait_ge(*counted("cqn_ready"))
                    root_mean(dve, "nckv", KVL)
                    for j in range(KVL // P):
                        ins = dve.scalar_tensor_tensor(out=ckvT[:, j, 0:T], in0=ckvT[:, j, 0:T],
                                                       scalar=vec[:, V_KVN + j:V_KVN + j + 1],
                                                       in1=rstd[:, :], op0=ALU.mult, op1=ALU.mult)
                    ins.then_inc(*counts("ckvn_ready"))
                    dve.wait_ge(*counted("ckvn_ready"))
                    for c in range(2):
                        for t in range(NT):
                            for h in range(2):
                                dve.wait_ge(*made(("q", c, t, h)))
                                s = bank(("q", c, t, h))
                                h0 = 8 * c + 4 * h
                                dve.tensor_copy(q_tok[:, t, h0:h0 + 4, :],
                                                s[:, 0:384].rearrange("p (h d) -> p h d", d=QK)).then_inc(*reads(("q", c, t, h)))
                                dve.wait_ge(*read(("q", c, t, h)))
                    dve.wait_ge(*made("ckv_out"))
                    dve.tensor_copy(ckv_out, bank("ckv_out")[:, 0:KVL]).then_inc(*reads("ckv_out"))
                    dve.wait_ge(*read("ckv_out"))

                    def head_norm(x, n, i, scale, w):
                        heads = x.rearrange("p t h d -> p (t h) d")
                        st = stat[:, i, 0:n]
                        dve.wait_ge(*following(dve, "sq_ready"))
                        dve.tensor_reduce(st, sq_heads[:, 0:n, :], AX_X, ALU.add).then_inc(*counts("dve_step"))
                        dve.wait_ge(*counted("dve_step"))
                        dve.tensor_scalar(st, st, 1.0 / QK, EPS, ALU.mult, ALU.add).then_inc(*counts("stat_ready"))
                        dve.wait_ge(*counted("stat_ready"))
                        dve.wait_ge(*following(dve, "head_root"))
                        dve.reciprocal(st, st).then_inc(*counts("dve_step"))
                        dve.wait_ge(*counted("dve_step"))
                        dve.tensor_tensor(heads, heads, over(st, QK), ALU.mult).then_inc(*counts("dve_step"))
                        dve.wait_ge(*counted("dve_step"))
                        dve.scalar_tensor_tensor(out=heads, in0=heads, scalar=scale, in1=each(row[:, w:w + QK], n),
                                                 op0=ALU.mult, op1=ALU.mult).then_inc(*counts("dve_step"))
                        dve.wait_ge(*counted("dve_step"))

                    def rotate(x):
                        for t in (1, 2):
                            pairs = x[:, t, :, NOPE:].rearrange("p h (m two) -> p h two m", two=2)
                            x1, x2 = pairs[:, :, 0, :], pairs[:, :, 1, :]
                            cos = each(cst[:, C_COS + 16 * (t - 1):C_COS + 16 * t], H_A)
                            sin = each(cst[:, C_SIN + 16 * (t - 1):C_SIN + 16 * t], H_A)
                            for i, (a, b) in enumerate(((x1, cos), (x2, sin), (x1, sin), (x2, cos))):
                                ins = dve.tensor_tensor(rope_tmp[:, i, :, :], a, b, ALU.mult)
                                ins.then_inc(*counts("dve_step"))
                                dve.wait_ge(*counted("dve_step"))
                            dve.tensor_tensor(x1, rope_tmp[:, 0], rope_tmp[:, 1], ALU.subtract).then_inc(*counts("dve_step"))
                            dve.wait_ge(*counted("dve_step"))
                            dve.tensor_tensor(x2, rope_tmp[:, 2], rope_tmp[:, 3], ALU.add).then_inc(*counts("dve_step"))
                            dve.wait_ge(*counted("dve_step"))

                    head_norm(q_tok, NT * H_A, 0, float(QK) ** -0.5, R_QW)
                    rotate(q_tok)
                    head_norm(k_tok, NKT * H_A, 1, 1.0, R_KW)
                    rotate(k_tok)

            STEPS = [(h, t) for h in range(H_A) for t in range(NT)]
            KEYS = ((0, 1), (1, NKT), (1, NKT))
            B_S, B_PT, B_TR, B_PV = 0, 2, 4, 5
            with nc.Block() as block:
                @block.tensor
                def _(pe):
                    def head(h):
                        transposed(pe, ("qT", h), [q_tok[:, t, h, :] for t in range(NT)], B_TR)
                        transposed(pe, ("kT", h), [k_tok[:, t, h, :] for t in range(NKT)], B_TR)

                    def scores(i):
                        h, t = STEPS[i]
                        k0, k1 = KEYS[t]
                        if t == 0:
                            pe.wait_ge(*read(("qT", h)))
                            pe.wait_ge(*read(("kT", h)))
                        out = claim(pe, ("s", i), B_S + i % 2)
                        pe.matmul(out[:, 0:P * (k1 - k0)], head_qT[0:QK, h % 2, tok(t)],
                                  head_kT[0:QK, h % 2, P * k0:P * k1], start=True, stop=True).then_inc(*makes(("s", i)))

                    def turn_probs(i):
                        h, t = STEPS[i]
                        k0, k1 = KEYS[t]
                        pe.wait_ge(*read(("s", i)))
                        transposed(pe, ("pt", i), [probs[:, i % 2, P * k:P * k + P] for k in range(k1 - k0)], B_PT + i % 2)

                    def weigh_values(i):
                        h, t = STEPS[i]
                        k0, k1 = KEYS[t]
                        if h % 8 == 0:
                            claim(pe, ("pv", t, h // 8), B_PV + t)
                        pe.wait_ge(*read(("pt", i)))
                        c = V_A * (h % 8)
                        ins = matmuls(pe, ps[:, B_PV + t, c:c + V_A],
                                      [(probsT[:, i % 2, P * k:P * k + P], v_a[:, k0 + k, h, :]) for k in range(k1 - k0)])
                        if h % 8 == 7:
                            ins.then_inc(*makes(("pv", t, h // 8)))

                    head(0)
                    for i in range(len(STEPS) + 2):
                        if i < len(STEPS):
                            scores(i)
                            if i % NT == 1 and i // NT + 1 < H_A:
                                head(i // NT + 1)
                        if 1 <= i <= len(STEPS):
                            turn_probs(i - 1)
                        if i >= 2:
                            weigh_values(i - 2)

                @block.scalar
                def _(act):
                    def queries(h):
                        act.wait_ge(*made(("qT", h)))
                        act.activation(head_qT[0:QK, h % 2, :], bank(("qT", h))[0:QK, 0:T], ACT.Copy).then_inc(*reads(("qT", h)))
                        act.wait_ge(*read(("qT", h)))

                    queries(0)
                    for i, (h, t) in enumerate(STEPS):
                        n = P * (KEYS[t][1] - KEYS[t][0])
                        if i >= 2:
                            act.wait_ge(*made(("pt", i - 2)))
                        act.wait_ge(*following(act, "nmax_ready"))
                        act.wait_ge(*made(("s", i)))
                        s = bank(("s", i))
                        act.activation(probs[:, i % 2, 0:n], s[:, 0:n], ACT.Exp, bias=nmax[:, i % 2:i % 2 + 1],
                                       accum_out=rsum[:, t, h:h + 1]).then_inc(*reads(("s", i)))
                        act.wait_ge(*read(("s", i)))
                        if i % NT == 1 and i // NT + 1 < H_A:
                            queries(i // NT + 1)

                @block.vector
                def _(dve):
                    def keys(h):
                        dve.wait_ge(*made(("kT", h)))
                        dve.tensor_copy(head_kT[0:QK, h % 2, :], bank(("kT", h))[0:QK, :]).then_inc(*reads(("kT", h)))
                        dve.wait_ge(*read(("kT", h)))

                    def turned(i):
                        h, t = STEPS[i]
                        n = P * (KEYS[t][1] - KEYS[t][0])
                        dve.wait_ge(*made(("pt", i)))
                        dve.tensor_copy(probsT[:, i % 2, 0:n], bank(("pt", i))[:, 0:n]).then_inc(*reads(("pt", i)))
                        dve.wait_ge(*read(("pt", i)))

                    def heads_out(t, g):
                        dve.wait_ge(*made(("pv", t, g)))
                        s = bank(("pv", t, g)).rearrange("p (h d) -> p h d", d=V_A)
                        r = rsum[:, t, 8 * g:8 * g + 8]
                        dve.reciprocal(r, r).then_inc(*counts("dve_step"))
                        dve.wait_ge(*counted("dve_step"))
                        dve.tensor_tensor(o_tok[:, t, 512 * g:512 * g + 512].rearrange("p (h d) -> p h d", d=V_A),
                                          s, over(r, V_A), ALU.mult).then_inc(*reads(("pv", t, g)))
                        dve.wait_ge(*read(("pv", t, g)))

                    keys(0)
                    for i in range(len(STEPS) + 3):
                        if i < len(STEPS):
                            h, t = STEPS[i]
                            n = P * (KEYS[t][1] - KEYS[t][0])
                            dve.wait_ge(*made(("s", i)))
                            s = bank(("s", i))
                            dve.tensor_reduce(nmax[:, i % 2:i % 2 + 1], s[:, 0:n], AX_X, ALU.max, negate=True).then_inc(*counts("nmax_ready"))
                            if i % NT == 1 and i // NT + 1 < H_A:
                                keys(i // NT + 1)
                        if 1 <= i <= len(STEPS):
                            turned(i - 1)
                        if i >= 3:
                            h, t = STEPS[i - 3]
                            if h % 8 == 7:
                                heads_out(t, h // 8)

                @block.sync
                def _(sp):
                    load_weights(sp, l, W_GA + RING, W_GA + RING)

            with nc.Block() as block:
                @block.tensor
                def _(pe):
                    for i in range(2):
                        feature_major(pe, W_GA + i, ("ga", i), hT)
                    to_features(pe, "oa", o_tok)
                    project_pe(pe, W_AO, "ao", oT, "oa")

                @block.scalar
                def _(act):
                    gate_act(act, "ga", gT)

                @block.vector
                def _(dve):
                    features_dve(dve, "oa", oT)
                    gated_sum(dve, "ao", "ga", gT, True)

                @block.sync
                def _(sp):
                    load_weights(sp, l, W_GA + RING, W_BQ + RING)

            q_b = carve(0, NT, H_B, DK)
            k_b = carve(1536, NT, H_B, DK)
            v_b = carve(3072, NT, H_B, DV)
            og = carve(6144, NT, D)
            logdec = carve(9216, 2, NT, H_B * DK)
            o_b = carve(12288, NT, D)
            soft = carve(12288, 2, NT, H_B * DK)
            sq_b = carve(9216, NT * H_B, DV)
            gla_s = carve(15360, 2, H_B, DV)
            gla_p = carve(17408, 2, H_B, DV)
            clamped = carve(19456, 512)
            up = carve(19968, H_B * DK)
            down = carve(20480, H_B * DK)
            qt = carve(20992, H_B, DK)
            kt = carve(21504, H_B, DK)
            qtT = carve(22016, H_B, P)
            ktT = carve(22528, H_B, P)
            att = carve(23040, H_B, P)
            ecol = carve(23552, 2, H_B, 2)
            stat_b = carve(23568, NT * H_B)
            SCAN = ((0, 0), (1, 0), (0, 1), (1, 2), (0, 2), (1, 1))
            FIRST = (0, 2, 3)
            LAST = (4, 5)
            with nc.Block() as block:
                @block.tensor
                def _(pe):
                    token_major(pe, W_BQ, "bq")
                    token_major(pe, W_BK, "bk")
                    for t in range(NT):
                        for d in range(2):
                            pe.matmul(claim(pe, ("lg", t, d)), lowT[:, tok(t)], wgl[:, d, :], start=True, stop=True).then_inc(*makes(("lg", t, d)))
                    for i in range(2):
                        token_major(pe, W_BV + i, ("bv", i))
                    for i in range(2):
                        token_major(pe, W_OG + i, ("og", i))
                    pe.wait_ge(*following(pe, "logdecay_ready"))
                    for s, (d, t) in enumerate(SCAN):
                        pe.matmul(claim(pe, ("b", s)), rel(d), logdec[:, d, t, :], start=True, stop=True).then_inc(*makes(("b", s)))
                        out = claim(pe, ("ec", s))
                        for h in range(H_B):
                            ins = pe.matmul(out[:, 2 * h:2 * h + 2], logdec[:, d, t, DK * h:DK * h + DK],
                                            cst[:, C_SEL:C_SEL + 2], start=True, stop=True)
                        ins.then_inc(*makes(("ec", s)))
                        pe.wait_ge(*following(pe, "qk_ready"))
                        transposed(pe, ("qtT", s), [qt[:, h, :] for h in range(H_B)])
                        transposed(pe, ("ktT", s), [kt[:, h, :] for h in range(H_B)])
                        pe.wait_ge(*read(("qtT", s)))
                        pe.wait_ge(*read(("ktT", s)))
                        out = claim(pe, ("att", s))
                        for h in range(H_B):
                            ins = pe.matmul(out[:, P * h:P * h + P], ktT[:, h, :], qtT[:, h, :], start=True, stop=True)
                        ins.then_inc(*makes(("att", s)))
                        if s == 0:
                            for i in range(2):
                                for u in range(NT):
                                    pe.wait_ge(*read((("bv", i), u)))
                        if s not in LAST:
                            for g in range(2):
                                out = claim(pe, ("ds", s, g))
                                for h in (2 * g, 2 * g + 1):
                                    c = DV * (h % 2)
                                    ins = pe.matmul(out[:, c:c + DV], kt[:, h, :], v_b[:, t, h, :], start=True, stop=True)
                                ins.then_inc(*makes(("ds", s, g)))
                        pe.wait_ge(*read(("att", s)))
                        if t:
                            pe.wait_ge(*following(pe, "scaled_state"))
                        for g in range(2):
                            out = claim(pe, ("o", s, g))
                            for h in (2 * g, 2 * g + 1):
                                c = DV * (h % 2)
                                pairs = [(att[:, h, :], v_b[:, t, h, :])]
                                if t:
                                    pairs.append((qtT[:, h, :], gla_s[:, d, h, :]))
                                ins = matmuls(pe, out[:, c:c + DV], pairs)
                            ins.then_inc(*makes(("o", s, g)))

                @block.scalar
                def _(act):
                    for t in range(NT):
                        act.wait_ge(*made(("bq", t)))
                        s = bank(("bq", t)).rearrange("p (h d) -> p h d", d=DK)
                        act.activation(q_b[:, t, :, :], s, ACT.Copy, scale=float(DK) ** -0.5).then_inc(*reads(("bq", t)))
                        act.wait_ge(*read(("bq", t)))
                    for i in range(2):
                        for t in range(NT):
                            act.wait_ge(*made((("og", i), t)))
                            s = bank((("og", i), t))
                            act.activation(og[:, t, 512 * i:512 * i + 512], s, ACT.Silu).then_inc(*reads((("og", i), t)))
                            act.wait_ge(*read((("og", i), t)))
                    act.wait_ge(*following(act, "abs_ready"))
                    act.activation(soft, soft, ACT.Exp, scale=-1.0).then_inc(*counts("act_step"))
                    act.wait_ge(*counted("act_step"))
                    act.activation(soft, soft, ACT.Ln, bias=1.0).then_inc(*counts("soft_ready"))
                    for s in range(len(SCAN)):
                        act.wait_ge(*following(act, "clamped_ready"))
                        act.activation(up, clamped, ACT.Exp).then_inc(*counts("act_step"))
                        act.wait_ge(*counted("act_step"))
                        act.activation(down, clamped, ACT.Exp, scale=-1.0).then_inc(*counts("decay_ready"))
                        act.wait_ge(*made(("ec", s)))
                        act.activation(ecol[:, s % 2, :, :],
                                       bank(("ec", s))[:, 0:2 * H_B].rearrange("p (h e) -> p h e", e=2),
                                       ACT.Exp).then_inc(*reads(("ec", s)))
                        act.wait_ge(*read(("ec", s)))
                        act.wait_ge(*made(("qtT", s)))
                        act.activation(qtT, quad(bank(("qtT", s))), ACT.Copy).then_inc(*reads(("qtT", s)))
                        act.wait_ge(*read(("qtT", s)))
                    act.wait_ge(*following(act, "o_ready"))
                    act.activation(sq_b, o_b.rearrange("p t (h d) -> p (t h) d", d=DV), ACT.Square).then_inc(*counts("sq_ready"))
                    act.wait_ge(*following(act, "stat_ready"))
                    act.activation(stat_b, stat_b, ACT.Sqrt).then_inc(*counts("head_root"))

                @block.gpsimd
                def _(pool):
                    pool.wait_ge(*following(pool, "gla_state_in", 32))
                    for s, (d, t) in enumerate(SCAN):
                        if t:
                            pool.wait_ge(*read(("ec", s)))
                            if s in LAST:
                                pool.wait_ge(*following(pool, "state_ready", 1))
                            ins = pool.tensor_tensor(gla_s[:, d, :, :], gla_s[:, d, :, :],
                                                     over(ecol[:, s % 2, :, d], DV), ALU.mult)
                            ins.then_inc(*counts("scaled_state"))

                @block.vector
                def _(dve):
                    for t in range(NT):
                        dve.wait_ge(*made(("bk", t)))
                        s = bank(("bk", t)).rearrange("p (h d) -> p h d", d=DK)
                        dve.tensor_copy(k_b[:, t, :, :], s).then_inc(*reads(("bk", t)))
                        dve.wait_ge(*read(("bk", t)))
                    for t in range(NT):
                        for d in range(2):
                            dve.wait_ge(*made(("lg", t, d)))
                            s = bank(("lg", t, d))
                            dve.tensor_copy(logdec[:, d, t, :], s).then_inc(*reads(("lg", t, d)))
                            dve.wait_ge(*read(("lg", t, d)))
                    dve.scalar_tensor_tensor(out=soft, in0=logdec, scalar=-1.0, in1=logdec,
                                             op0=ALU.mult, op1=ALU.max).then_inc(*counts("abs_ready"))
                    dve.wait_ge(*counted("abs_ready"))
                    dve.tensor_scalar(logdec, logdec, 0.0, 1.0 / GATE_NORM, ALU.min, ALU.mult).then_inc(*counts("dve_step"))
                    dve.wait_ge(*counted("dve_step"))
                    for i in range(2):
                        for t in range(NT):
                            dve.wait_ge(*made((("bv", i), t)))
                            s = bank((("bv", i), t)).rearrange("p (h d) -> p h d", d=DV)
                            dve.tensor_copy(v_b[:, t, 2 * i:2 * i + 2, :], s).then_inc(*reads((("bv", i), t)))
                            dve.wait_ge(*read((("bv", i), t)))
                    dve.wait_ge(*following(dve, "soft_ready"))
                    dve.scalar_tensor_tensor(out=logdec, in0=soft, scalar=-1.0 / GATE_NORM, in1=logdec,
                                             op0=ALU.mult, op1=ALU.add).then_inc(*counts("logdecay_ready"))
                    dve.wait_ge(*counted("logdecay_ready"))
                    for t in range(NT):
                        dve.wait_ge(*read(("bq", t)))
                    for s, (d, t) in enumerate(SCAN):
                        dve.wait_ge(*made(("b", s)))
                        dve.tensor_scalar(clamped, bank(("b", s)), CLAMP, -CLAMP, ALU.min, ALU.max).then_inc(*reads(("b", s)))
                        dve.wait_ge(*read(("b", s)))
                        dve.tensor_copy(stat_b[:, 0:1], cst[:, 0:1]).then_inc(*counts("clamped_ready"))
                        dve.wait_ge(*following(dve, "decay_ready"))
                        dve.tensor_tensor(qt, q_b[:, t, :, :], up.rearrange("p (h d) -> p h d", d=DK), ALU.mult).then_inc(*counts("dve_step"))
                        dve.wait_ge(*counted("dve_step"))
                        dve.tensor_tensor(kt, k_b[:, t, :, :], down.rearrange("p (h d) -> p h d", d=DK), ALU.mult).then_inc(*counts("qk_ready"))
                        dve.wait_ge(*counted("qk_ready"))
                        dve.wait_ge(*made(("ktT", s)))
                        dve.tensor_copy(ktT, quad(bank(("ktT", s)))).then_inc(*reads(("ktT", s)))
                        dve.wait_ge(*read(("ktT", s)))
                        dve.wait_ge(*made(("att", s)))
                        dve.tensor_tensor(att, quad(bank(("att", s))), each(cum(d), H_B), ALU.mult).then_inc(*reads(("att", s)))
                        dve.wait_ge(*read(("att", s)))
                        for g in range(2):
                            out = o_b[:, t, 512 * g:512 * g + 512]
                            dve.wait_ge(*made(("o", s, g)))
                            p = bank(("o", s, g))
                            if s in FIRST:
                                dve.tensor_copy(out, p).then_inc(*reads(("o", s, g)))
                                dve.wait_ge(*read(("o", s, g)))
                            else:
                                dve.tensor_tensor(out, p, out, ALU.add).then_inc(*reads(("o", s, g)))
                                dve.wait_ge(*read(("o", s, g)))
                        if s not in LAST:
                            dve.wait_ge(*read(("ec", s)))
                            for g in range(2):
                                dve.wait_ge(*made(("ds", s, g)))
                                p = bank(("ds", s, g)).rearrange("p (h d) -> p h d", d=DV)
                                e = over(ecol[:, s % 2, 2 * g:2 * g + 2, 1 - d], DV)
                                if t == 0:
                                    dve.tensor_tensor(gla_p[:, d, 2 * g:2 * g + 2, :], p, e, ALU.mult).then_inc(*reads(("ds", s, g)))
                                    dve.wait_ge(*read(("ds", s, g)))
                                else:
                                    st = gla_s[:, d, 2 * g:2 * g + 2, :]
                                    dve.tensor_tensor(st, p, st, ALU.add).then_inc(*reads(("ds", s, g)))
                                    dve.wait_ge(*read(("ds", s, g)))
                                    ins = dve.tensor_tensor(st, st, e, ALU.mult)
                                    if g:
                                        ins.then_inc(*counts("state_ready"))
                                        dve.wait_ge(*counted("state_ready"))
                                    else:
                                        ins.then_inc(*counts("dve_step"))
                                        dve.wait_ge(*counted("dve_step"))
                    dve.tensor_copy(stat_b[:, 0:1], cst[:, 0:1]).then_inc(*counts("o_ready"))
                    dve.wait_ge(*counted("o_ready"))
                    dve.wait_ge(*following(dve, "sq_ready"))
                    dve.tensor_reduce(stat_b, sq_b, AX_X, ALU.add).then_inc(*counts("dve_step"))
                    dve.wait_ge(*counted("dve_step"))
                    dve.tensor_scalar(stat_b, stat_b, 1.0 / DV, EPS, ALU.mult, ALU.add).then_inc(*counts("stat_ready"))
                    dve.wait_ge(*counted("stat_ready"))
                    dve.wait_ge(*following(dve, "head_root"))
                    dve.reciprocal(stat_b, stat_b).then_inc(*counts("dve_step"))
                    dve.wait_ge(*counted("dve_step"))
                    heads = o_b.rearrange("p t (h d) -> p (t h) d", d=DV)
                    dve.tensor_tensor(heads, heads, over(stat_b, DV), ALU.mult).then_inc(*counts("dve_step"))
                    dve.wait_ge(*counted("dve_step"))
                    for i in range(2):
                        for t in range(NT):
                            dve.wait_ge(*read((("og", i), t)))
                    dve.tensor_tensor(o_b, o_b, og, ALU.mult).then_inc(*counts("dve_step"))
                    dve.wait_ge(*counted("dve_step"))

                @block.sync
                def _(sp):
                    for d in range(2):
                        sp.dma_start(gla_s[:, d, :, :], state_gla[bass.ds(l, 1), d].rearrange("a h k v -> k (a h) v")
                                     ).then_inc(sem["gla_state_in"], 16)
                    load_weights(sp, l, W_BQ + RING, W_GB + RING)
                    for d in range(2):
                        for g in range(2):
                            sp.wait_ge(*read(("ds", d, g)))
                        sp.dma_start(new_gla[bass.ds(l, 1), d].rearrange("a h k v -> k (a h) v"), gla_p[:, d, :, :]
                                     ).then_inc(sem["stored"], 16)
                    sp.wait_ge(*following(sp, "stored", 32))

            gT_b = carve(0, KD, T)
            oT_b = carve(3072, KD, T)
            with nc.Block() as block:
                @block.tensor
                def _(pe):
                    for i in range(2):
                        feature_major(pe, W_GB + i, ("gb", i), hT)
                    to_features(pe, "ob", o_b)
                    project_pe(pe, W_BO, "bo", oT_b, "ob")

                @block.scalar
                def _(act):
                    gate_act(act, "gb", gT_b)

                @block.vector
                def _(dve):
                    features_dve(dve, "ob", oT_b, V_BON)
                    gated_sum(dve, "bo", "gb", gT_b, False)

                @block.sync
                def _(sp):
                    load_weights(sp, l, W_GB + RING, W_Z + RING)

            z_c = carve(0, NT, D)
            xpad = carve(3072, NX, XW)
            xbc = carve(7776, NX, YW)
            xs = carve(12432, NT, D)
            b_tok = carve(15504, NT, G_C, N_ST)
            y_c = carve(16272, NT, D)
            xdt = carve(19344, H_C, HP)
            xw = carve(20368, H_C, HP)
            diff = carve(21392, 2, 512)
            decayed = carve(22416, H_C, P)
            cbm = carve(24464, G_C, P)
            dt = carve(24720, NT, 32)
            dta = carve(24816, NT, 32)
            dtt = carve(24912, NT, 32)
            aexp = carve(25008, 32)
            ex2 = carve(25040, 2, 4, H_C)
            stat_c = carve(25170, NT)
            ssd_in = carve(3072, 2, KD, P)
            ssd_s = carve(5120, 2, H_C * HP)
            ssd_p = carve(7168, H_C * HP)
            ssd_out = (carve(8192, KD, P), carve(25200, KD, P))
            ssd_tmp = carve(9216, 512)
            OUT_COL = (0, X_S - X_P, X_S - X_P + P)
            with nc.Block() as block:
                @block.tensor
                def _(pe):
                    for i in range(2):
                        token_major(pe, W_Z + i, ("z", i))
                    for i in range(3):
                        feature_major(pe, W_CX + i, ("cx", i), hT)
                    for q in range(2):
                        for j in range(4 * q, 4 * q + 4):
                            pe.wait_ge(*following(pe, "xbc_ready"))
                        for t in range(NT):
                            transposed(pe, ("xs", t, q), [xbc[:, j, OUT_COL[t]:OUT_COL[t] + P] for j in range(4 * q, 4 * q + 4)])
                    for j in range(8, NX):
                        pe.wait_ge(*following(pe, "xbc_ready"))
                    for t in range(NT):
                        transposed(pe, ("bt", t), [xbc[:, 8 + g, OUT_COL[t]:OUT_COL[t] + P] for g in range(G_C)])

                @block.scalar
                def _(act):
                    for i in range(2):
                        for t in range(NT):
                            act.wait_ge(*made((("z", i), t)))
                            s = bank((("z", i), t))
                            act.activation(z_c[:, t, 512 * i:512 * i + 512], s, ACT.Silu).then_inc(*reads((("z", i), t)))
                            act.wait_ge(*read((("z", i), t)))
                    for i in range(3):
                        for j in range(4):
                            act.wait_ge(*made((("cx", i), j)))
                            s = bank((("cx", i), j))
                            act.activation(xpad[:, 4 * i + j, X_P:X_P + P], s[:, 0:P], ACT.Copy).then_inc(*counts("act_step"))
                            act.wait_ge(*counted("act_step"))
                            act.activation(xpad[:, 4 * i + j, X_S:X_S + 2 * P], s[:, P:T], ACT.Copy).then_inc(*reads((("cx", i), j)))
                            act.wait_ge(*read((("cx", i), j)))
                    for j in range(NX):
                        act.wait_ge(*following(act, "conv_ready"))
                        act.activation(xbc[:, j, :], xbc[:, j, :], ACT.Silu, bias=vec[:, V_CB + j:V_CB + j + 1]).then_inc(*counts("xbc_ready"))
                    act.wait_ge(*following(act, "abs_ready"))
                    act.activation(dtt, dtt, ACT.Exp, scale=-1.0).then_inc(*counts("act_step"))
                    act.wait_ge(*counted("act_step"))
                    act.activation(dtt, dtt, ACT.Ln, bias=1.0).then_inc(*counts("act_step"))
                    act.wait_ge(*counted("act_step"))
                    act.activation(aexp, row[:, R_ALOG:R_ALOG + 32], ACT.Exp).then_inc(*counts("soft_ready"))

                @block.vector
                def _(dve):
                    for a, b in ((0, X_P), (X_P + P, X_S), (XW - PAD, XW)):
                        dve.memset(xpad[:, :, a:b], 0.0).then_inc(*counts("dve_step"))
                        dve.wait_ge(*counted("dve_step"))
                    dve.tensor_tensor(dt, dtraw[:, :, :], each(row[:, R_DTB:R_DTB + 32], NT), ALU.add).then_inc(*counts("dve_step"))
                    dve.wait_ge(*counted("dve_step"))
                    dve.scalar_tensor_tensor(out=dtt, in0=dt, scalar=-1.0, in1=dt, op0=ALU.mult, op1=ALU.max).then_inc(*counts("abs_ready"))
                    dve.wait_ge(*counted("abs_ready"))
                    dve.tensor_scalar(dt, dt, 0.0, None, ALU.max).then_inc(*counts("dve_step"))
                    dve.wait_ge(*counted("dve_step"))
                    for j in range(NX):
                        dve.wait_ge(*read((("cx", j // 4), j % 4)))
                        for k in range(TAPS):
                            w = vec[:, V_CW + NX * k + j:V_CW + NX * k + j + 1]
                            src = xpad[:, j, k:k + YW]
                            if k == 0:
                                ins = dve.tensor_scalar(xbc[:, j, :], src, w, None, ALU.mult)
                            else:
                                ins = dve.scalar_tensor_tensor(out=xbc[:, j, :], in0=src, scalar=w, in1=xbc[:, j, :],
                                                               op0=ALU.mult, op1=ALU.add)
                            ins.then_inc(*counts("conv_ready" if k == TAPS - 1 else "dve_step"))
                            dve.wait_ge(*counted("conv_ready" if k == TAPS - 1 else "dve_step"))
                    for q in range(2):
                        for t in range(NT):
                            dve.wait_ge(*made(("xs", t, q)))
                            dve.tensor_copy(xs[:, t, 512 * q:512 * q + 512], bank(("xs", t, q))).then_inc(*reads(("xs", t, q)))
                            dve.wait_ge(*read(("xs", t, q)))
                    for t in range(NT):
                        dve.wait_ge(*made(("bt", t)))
                        dve.tensor_copy(b_tok[:, t, :, :], quad(bank(("bt", t))[:, 0:G_C * P])).then_inc(*reads(("bt", t)))
                        dve.wait_ge(*read(("bt", t)))
                    dve.wait_ge(*following(dve, "soft_ready"))
                    dve.tensor_tensor(dt, dt, dtt, ALU.add).then_inc(*counts("dve_step"))
                    dve.wait_ge(*counted("dve_step"))
                    dve.scalar_tensor_tensor(out=dta, in0=dt, scalar=-1.0, in1=each(aexp, NT),
                                             op0=ALU.mult, op1=ALU.mult).then_inc(*counts("dve_step"))
                    dve.wait_ge(*counted("dve_step"))

                @block.sync
                def _(sp):
                    load_weights(sp, l, W_Z + RING, W_GC + RING)

            with nc.Block() as block:
                @block.tensor
                def _(pe):
                    pe.wait_ge(*following(pe, "ssd_state_in", 32))
                    for d in range(2):
                        for q in range(2):
                            transposed(pe, ("si", d, q), [ssd_in[:, d, 4 * q + i, :] for i in range(4)])
                    for s, (d, t) in enumerate(SCAN):
                        col = slice(OUT_COL[t], OUT_COL[t] + P)
                        a = dta[:, t, H_C * d:H_C * d + H_C]
                        out = claim(pe, ("sc", s))
                        for i, m in enumerate((rel(d), cum(d), aft(d), ones)):
                            ins = pe.matmul(out[:, H_C * i:H_C * i + H_C], m, a, start=True, stop=True)
                        ins.then_inc(*makes(("sc", s)))
                        out = claim(pe, ("cb", s))
                        for g in range(G_C):
                            ins = pe.matmul(out[:, P * g:P * g + P], xbc[:, 8 + g, col], xbc[:, 10 + g, col],
                                            start=True, stop=True)
                        ins.then_inc(*makes(("cb", s)))
                        for q in range(4):
                            out = claim(pe, ("ai", s, q))
                            for i in range(4):
                                h = H_C * d + 4 * q + i
                                ins = pe.matmul(out[:, P * i:P * i + P], dta[:, t, h:h + 1].broadcast_to([P, P]), rel(d),
                                                start=True, stop=True)
                            ins.then_inc(*makes(("ai", s, q)))
                        if t:
                            for g in range(G_C):
                                if s in FIRST:
                                    pe.wait_ge(*read(("si", d, g)))
                                else:
                                    pe.wait_ge(*read(("ds", s - 2, g)))
                                if s not in FIRST and g == 0:
                                    pe.wait_ge(*following(pe, "state_ready"))
                                pe.matmul(claim(pe, ("yo", s, g)), xbc[:, 10 + g, col],
                                          ssd_s[:, d, 512 * g:512 * g + 512], start=True, stop=True).then_inc(*makes(("yo", s, g)))
                        pe.wait_ge(*following(pe, "xw_ready"))
                        if s not in LAST:
                            for g in range(G_C):
                                pe.matmul(claim(pe, ("ds", s, g)), b_tok[:, t, g, :],
                                          xw.rearrange("p h d -> p (h d)")[:, 512 * g:512 * g + 512],
                                          start=True, stop=True).then_inc(*makes(("ds", s, g)))
                        for g in range(G_C):
                            pe.wait_ge(*following(pe, "mask_ready", 2))
                            out = claim(pe, ("yd", s, g))
                            for i in range(8):
                                h = 8 * g + i
                                ins = pe.matmul(out[:, HP * i:HP * i + HP], decayed[:, h, :], xdt[:, h, :],
                                                start=True, stop=True)
                            ins.then_inc(*makes(("yd", s, g)))
                        if t == 0:
                            for g in range(G_C):
                                pe.wait_ge(*read(("ds", s, g)))
                            for q in range(2):
                                transposed(pe, ("so", d, q), [ssd_p[:, 512 * q + P * i:512 * q + P * i + P] for i in range(4)])

                @block.scalar
                def _(act):
                    for s, (d, t) in enumerate(SCAN):
                        act.wait_ge(*made(("sc", s)))
                        p = bank(("sc", s)).rearrange("p (a h) -> p a h", h=H_C)
                        act.activation(ex2[:, s % 2, 0, :], p[:, 0, :], ACT.Copy).then_inc(*counts("act_step"))
                        act.wait_ge(*counted("act_step"))
                        act.activation(ex2[:, s % 2, 1:4, :], p[:, 1:4, :], ACT.Exp).then_inc(*reads(("sc", s)))
                        act.wait_ge(*read(("sc", s)))
                        for q in range(4):
                            act.wait_ge(*following(act, "diff_ready"))
                            act.activation(diff[:, q % 2, :], diff[:, q % 2, :], ACT.Exp).then_inc(*counts("decayed_ready"))
                    for t in range(NT):
                        act.wait_ge(*following(act, "y_ready"))
                        act.activation(xs[:, t, :], y_c[:, t, :], ACT.Square, accum_out=stat_c[:, t:t + 1]).then_inc(*counts("sq_ready"))
                    act.wait_ge(*following(act, "stat_ready"))
                    act.activation(stat_c, stat_c, ACT.Sqrt).then_inc(*counts("head_root"))

                @block.gpsimd
                def _(pool):
                    for t in range(NT):
                        ins = pool.tensor_tensor(y_c[:, t, :].rearrange("p (h d) -> p h d", d=HP),
                                                 xs[:, t, :].rearrange("p (h d) -> p h d", d=HP),
                                                 over(row[:, R_D:R_D + H_C], HP), ALU.mult)
                    ins.then_inc(*counts("yoff_ready"))
                    for s, (d, t) in enumerate(SCAN):
                        pool.wait_ge(*read(("sc", s)))
                        if s:
                            pool.wait_ge(*made(("yd", s - 1, 1)))
                        pool.tensor_tensor(xdt, xs[:, t, :].rearrange("p (h d) -> p h d", d=HP),
                                            over(dt[:, t, H_C * d:H_C * d + H_C], HP), ALU.mult).then_inc(*counts("pool_step"))
                        pool.wait_ge(*counted("pool_step"))
                        pool.tensor_tensor(xw, xdt, over(ex2[:, s % 2, 2, :], HP), ALU.mult).then_inc(*counts("xw_ready"))

                @block.vector
                def _(dve):
                    dve.wait_ge(*following(dve, "yoff_ready"))
                    for d in range(2):
                        for q in range(2):
                            dve.wait_ge(*made(("si", d, q)))
                            dve.tensor_copy(ssd_s[:, d, 512 * q:512 * q + 512], bank(("si", d, q))).then_inc(*reads(("si", d, q)))
                            dve.wait_ge(*read(("si", d, q)))
                    for s, (d, t) in enumerate(SCAN):
                        dve.wait_ge(*made(("cb", s)))
                        dve.tensor_tensor(cbm, quad(bank(("cb", s))[:, 0:G_C * P]), each(cum(d), G_C), ALU.mult).then_inc(*reads(("cb", s)))
                        dve.wait_ge(*read(("cb", s)))
                        dve.wait_ge(*read(("sc", s)))
                        for q in range(5):
                            if q < 4:
                                dve.wait_ge(*made(("ai", s, q)))
                                dve.tensor_tensor(quad(diff[:, q % 2, :]), quad(bank(("ai", s, q))),
                                                  over(ex2[:, s % 2, 0, 4 * q:4 * q + 4], P), ALU.subtract).then_inc(*reads(("ai", s, q)))
                                dve.wait_ge(*read(("ai", s, q)))
                                dve.tensor_scalar(diff[:, q % 2, :], diff[:, q % 2, :], 0.0, None, ALU.min).then_inc(*counts("diff_ready"))
                            if q:
                                r = q - 1
                                dve.wait_ge(*following(dve, "decayed_ready"))
                                dve.tensor_tensor(decayed[:, 4 * r:4 * r + 4, :], quad(diff[:, r % 2, :]),
                                                  each(cbm[:, r // 2, :], 4), ALU.mult).then_inc(*counts("mask_ready"))
                                dve.wait_ge(*counted("mask_ready"))
                        for g in range(G_C):
                            out = y_c[:, t, 512 * g:512 * g + 512]
                            if t:
                                dve.wait_ge(*made(("yo", s, g)))
                                dve.tensor_tensor(ssd_tmp.rearrange("p (h d) -> p h d", d=HP),
                                                  bank(("yo", s, g)).rearrange("p (h d) -> p h d", d=HP),
                                                  over(ex2[:, s % 2, 1, 8 * g:8 * g + 8], HP), ALU.mult).then_inc(*counts("dve_step"))
                                dve.wait_ge(*counted("dve_step"))
                                dve.tensor_tensor(out, ssd_tmp, out, ALU.add).then_inc(*reads(("yo", s, g)))
                                dve.wait_ge(*read(("yo", s, g)))
                            dve.wait_ge(*made(("yd", s, g)))
                            dve.tensor_tensor(out, bank(("yd", s, g)), out, ALU.add).then_inc(*reads(("yd", s, g)))
                            dve.wait_ge(*read(("yd", s, g)))
                        if s not in LAST:
                            for g in range(G_C):
                                dve.wait_ge(*made(("ds", s, g)))
                                p = bank(("ds", s, g))
                                if t == 0:
                                    dve.tensor_copy(ssd_p[:, 512 * g:512 * g + 512], p).then_inc(*reads(("ds", s, g)))
                                    dve.wait_ge(*read(("ds", s, g)))
                                else:
                                    st = ssd_s[:, d, 512 * g:512 * g + 512]
                                    sv = st.rearrange("p (h d) -> p h d", d=HP)
                                    dve.tensor_tensor(sv, sv, over(ex2[:, s % 2, 3, 8 * g:8 * g + 8], HP), ALU.mult).then_inc(*counts("dve_step"))
                                    dve.wait_ge(*counted("dve_step"))
                                    dve.tensor_tensor(st, p, st, ALU.add).then_inc(*reads(("ds", s, g)))
                                    dve.wait_ge(*read(("ds", s, g)))
                            if t:
                                dve.tensor_copy(stat_c[:, 0:1], cst[:, 0:1]).then_inc(*counts("state_ready"))
                                dve.wait_ge(*counted("state_ready"))
                        if t == 0:
                            for q in range(2):
                                dve.wait_ge(*made(("so", d, q)))
                                dve.tensor_copy(ssd_out[d][:, 4 * q:4 * q + 4, :], quad(bank(("so", d, q)))).then_inc(*reads(("so", d, q)))
                                dve.wait_ge(*read(("so", d, q)))
                    for t in range(NT):
                        dve.tensor_tensor(y_c[:, t, :], y_c[:, t, :], z_c[:, t, :], ALU.mult).then_inc(*counts("y_ready"))
                        dve.wait_ge(*counted("y_ready"))
                    for t in range(NT):
                        dve.wait_ge(*following(dve, "sq_ready"))
                    dve.tensor_scalar(stat_c, stat_c, 1.0 / D, EPS, ALU.mult, ALU.add).then_inc(*counts("stat_ready"))
                    dve.wait_ge(*counted("stat_ready"))
                    dve.wait_ge(*following(dve, "head_root"))
                    dve.reciprocal(stat_c, stat_c).then_inc(*counts("dve_step"))
                    dve.wait_ge(*counted("dve_step"))
                    for t in range(NT):
                        dve.tensor_scalar(y_c[:, t, :], y_c[:, t, :], stat_c[:, t:t + 1], None, ALU.mult).then_inc(*counts("dve_step"))
                        dve.wait_ge(*counted("dve_step"))

                @block.sync
                def _(sp):
                    for d in range(2):
                        sp.dma_start(ssd_in[:, d, :, :], state_ssd[bass.ds(l, 1), d].rearrange("a (j q) n -> q (a j) n", q=P)
                                     ).then_inc(sem["ssd_state_in"], 16)
                    for d in range(2):
                        for q in range(2):
                            sp.wait_ge(*read(("so", d, q)))
                        sp.dma_start(new_ssd[bass.ds(l, 1), d].rearrange("a (j q) n -> q (a j) n", q=P), ssd_out[d]
                                     ).then_inc(sem["stored"], 16)
                    sp.wait_ge(*following(sp, "stored", 32))

            gT_c = carve(0, KD, T)
            oT_c = carve(3072, KD, T)
            with nc.Block() as block:
                @block.tensor
                def _(pe):
                    for i in range(2):
                        feature_major(pe, W_GC + i, ("gc", i), hT)
                    to_features(pe, "oc", y_c)
                    project_pe(pe, W_CO, "co", oT_c, "oc")
                    pe.wait_ge(*following(pe, "merged_ready"))
                    for i in range(2):
                        feature_major(pe, W_OUT + i, ("out", i), mT)

                @block.scalar
                def _(act):
                    gate_act(act, "gc", gT_c)

                @block.vector
                def _(dve):
                    features_dve(dve, "oc", oT_c, V_CN)
                    gated_sum(dve, "co", "gc", gT_c, False)
                    dve.tensor_copy(stat_c[:, 0:1], cst[:, 0:1]).then_inc(*counts("merged_ready"))
                    dve.wait_ge(*counted("merged_ready"))
                    for i in range(2):
                        for j in range(4):
                            dve.wait_ge(*made((("out", i), j)))
                            s = bank((("out", i), j))
                            k = 4 * i + j
                            for ts, c in COND:
                                ins = dve.scalar_tensor_tensor(out=xT[:, k, ts], in0=s[:, ts], scalar=mod[:, 2, k, c:c + 1],
                                                               in1=xT[:, k, ts], op0=ALU.mult, op1=ALU.add)
                                if c == 0:
                                    ins.then_inc(*counts("dve_step"))
                                    dve.wait_ge(*counted("dve_step"))
                            ins.then_inc(*reads((("out", i), j)))
                            dve.wait_ge(*read((("out", i), j)))

                @block.sync
                def _(sp):
                    load_weights(sp, l, W_GC + RING, W_MOE + RING)

            acc = carve(0, NT, D)
            hid = carve(3072, DE // P, T)
            sil = carve(4608, DE // P, T)
            score = carve(6144, NT, NE)
            sel = carve(6192, NT, NE)
            pairs6 = carve(6240, NT * NG, 6)
            gsum = carve(6320, NT, NG)
            gmax = carve(6332, NT)
            genc = carve(6336, NT, NG)
            gone = carve(6348, NT, NG)
            enc = carve(6400, NT, NE)
            one = carve(6448, NT, NE)
            chosen = carve(6496, NT, NE)
            gate = carve(6544, NT, NE)
            moved = carve(6600, 512)
            B_HID, B_OUT, N_OUT = 0, 4, 3
            with nc.Block() as block:
                base = {}

                @block.tensor
                def _(pe):
                    square_sum(pe, "n2", sq_x, KD)
                    pe.wait_ge(*following(pe, "h_ready"))
                    out = claim(pe, "route")
                    for t in range(NT):
                        ins = matmuls(pe, out[:, NE * t:NE * t + NE], [(hT[:, k, tok(t)], rw[:, k, :]) for k in range(KD)])
                    ins.then_inc(*makes("route"))
                    base.update({b: uses[b] for b in range(8)})
                    pe.wait_ge(*following(pe, "zeroed"))
                    with pe.Fori(0, NE) as e:
                        def slot(i):
                            pe.wait_ge(w_loaded[i], e * 16 + 16 * (W_MOE // RING + 1))
                            k = (KD, KD, DE // P)[i]
                            return chunk(i, k, 4096 // k)

                        w1 = slot(0)
                        w3 = slot(1)
                        for f in range(DE // P):
                            for i, w in ((0, w1), (1, w3)):
                                b = B_HID + 2 * (f % 2) + i
                                pe.wait_ge(psum_free[b], e * 2 + (base[b] + f // 2))
                                matmuls(pe, ps[:, b, 0:T], [(w[:, k, P * f:P * f + P], hT[:, k, :]) for k in range(KD)]
                                        ).then_inc(psum_full[b], 1)
                        w2 = slot(2)
                        pe.wait_ge(sem["hidden_ready"], e * 4 + 4)
                        for n in range(2 * NT):
                            b = B_OUT + n % N_OUT
                            pe.wait_ge(psum_free[b], e * 2 + (base[b] + n // N_OUT))
                            matmuls(pe, ps[:, b, :], [(hid[:, k, tok(n // 2)], w2[:, k, 512 * (n % 2):512 * (n % 2) + 512])
                                                      for k in range(DE // P)]).then_inc(psum_full[b], 1)
                    for b in range(B_HID, B_OUT + N_OUT):
                        uses[b] += 2 * NE
                    pe.wait_ge(*following(pe, "moe_ready"))
                    to_features(pe, "mo", acc)

                @block.sync
                def _(sp):
                    with sp.Fori(1, NE) as e:
                        last = ((B_HID + 2, 2), (B_HID + 3, 2), (B_OUT + N_OUT - 1, 2))
                        for i, (b, n) in enumerate(last):
                            sp.wait_ge(psum_full[b], e * 2 + base[b])
                            src, k, w = expert_source(i, l, e)
                            sp.dma_start(chunk(i, k, w), src).then_inc(w_loaded[i], 16)

                @block.scalar
                def _(act):
                    norm_act(act, 1, "n2", sq_x)
                    act.wait_ge(*made("route"))
                    act.activation(score, bank("route")[:, 0:NT * NE].rearrange("p (t e) -> p t e", e=NE),
                                   ACT.Sigmoid).then_inc(*reads("route"))
                    act.wait_ge(*read("route"))
                    with act.Fori(0, NE) as e:
                        for f in range(DE // P):
                            b = B_HID + 2 * (f % 2)
                            act.wait_ge(psum_full[b], e * 2 + (base[b] + f // 2 + 1))
                            act.activation(sil[:, f, :], ps[:, b, 0:T], ACT.Silu).then_inc(psum_free[b], 1)

                @block.vector
                def _(dve):
                    norm_dve(dve, "n2")
                    dve.memset(acc, 0.0).then_inc(*counts("zeroed"))
                    dve.wait_ge(*read("route"))

                    def step(ins):
                        ins.then_inc(*counts("dve_step"))
                        dve.wait_ge(*counted("dve_step"))

                    flat = sel.rearrange("p t (g e) -> p (t g) e", e=EG)
                    step(dve.tensor_tensor(sel, score, each(row[:, R_RB:R_RB + NE], NT), ALU.add))
                    for c, a, b, w in ((0, 0, 2, 2), (2, 0, 3, 1), (3, 1, 2, 1), (4, 0, 1, 1), (5, 2, 3, 1)):
                        step(dve.tensor_tensor(pairs6[:, :, c:c + w], flat[:, :, a:a + w], flat[:, :, b:b + w], ALU.add))
                    step(dve.tensor_reduce(gsum.rearrange("p t g -> p (t g)"), pairs6, AX_X, ALU.max))

                    def first_max(x, n, e, o):
                        rank = each(cst[:, C_RANK:C_RANK + n], NT)
                        step(dve.tensor_reduce(gmax, x, AX_X, ALU.max))
                        step(dve.tensor_tensor(e, x, over(gmax, n), ALU.is_ge))
                        step(dve.tensor_tensor(e, e, rank, ALU.mult))
                        step(dve.tensor_reduce(gmax, e, AX_X, ALU.max))
                        step(dve.tensor_tensor(o, e, over(gmax, n), ALU.is_equal))

                    first_max(gsum, NG, genc, gone)
                    inside = gone.rearrange("p t g -> p (t g)")
                    step(dve.tensor_tensor(flat, flat, over(inside, EG), ALU.mult))
                    step(dve.tensor_scalar(genc, gone, -1.0, BIG, ALU.add, ALU.mult))
                    step(dve.tensor_tensor(flat, flat, over(genc.rearrange("p t g -> p (t g)"), EG), ALU.add))
                    first_max(sel, NE, enc, chosen)
                    step(dve.scalar_tensor_tensor(out=sel, in0=chosen, scalar=-2.0 * BIG, in1=sel, op0=ALU.mult, op1=ALU.add))
                    first_max(sel, NE, enc, one)
                    step(dve.tensor_tensor(chosen, chosen, one, ALU.add))
                    step(dve.tensor_tensor(gate, score, chosen, ALU.mult))
                    step(dve.tensor_reduce(gmax, gate, AX_X, ALU.add))
                    step(dve.reciprocal(gmax, gmax))
                    step(dve.tensor_tensor(gate, gate, over(gmax, NE), ALU.mult))

                    with dve.Fori(0, NE) as e:
                        for f in range(DE // P):
                            a = B_HID + 2 * (f % 2)
                            dve.wait_ge(psum_full[a + 1], e * 2 + (base[a + 1] + f // 2 + 1))
                            dve.wait_ge(psum_free[a], e * 2 + (base[a] + f // 2 + 1))
                            dve.tensor_tensor(hid[:, f, :], ps[:, a + 1, 0:T], sil[:, f, :], ALU.mult
                                              ).then_inc(sem["hidden_ready"], 1)
                            dve.wait_ge(sem["hidden_ready"], e * 4 + (f + 1))
                            dve.tensor_copy(moved[:, 0:1], cst[:, 0:1]).then_inc(psum_free[a + 1], 1)
                        for n in range(2 * NT):
                            b = B_OUT + n % N_OUT
                            t = n // 2
                            out = acc[:, t, 512 * (n % 2):512 * (n % 2) + 512]
                            dve.wait_ge(psum_full[b], e * 2 + (base[b] + n // N_OUT + 1))
                            dve.scalar_tensor_tensor(out=out, in0=ps[:, b, :], scalar=gate[:, t, bass.ds(e, 1)], in1=out,
                                                     op0=ALU.mult, op1=ALU.add).then_inc(psum_free[b], 1)
                            dve.wait_ge(psum_free[b], e * 2 + (base[b] + n // N_OUT + 1))
                    dve.tensor_copy(moved[:, 0:1], cst[:, 0:1]).then_inc(*counts("moe_ready"))
                    for t in range(NT):
                        c = 0 if t == 0 else 1
                        for q in range(2):
                            dve.wait_ge(*made(("mo", t, q)))
                            s = quad(bank(("mo", t, q)))
                            dve.tensor_tensor(quad(moved), s, over(mod[:, 5, 4 * q:4 * q + 4, c], P), ALU.mult).then_inc(*reads(("mo", t, q)))
                            dve.wait_ge(*read(("mo", t, q)))
                            out = xT[:, 4 * q:4 * q + 4, tok(t)]
                            dve.tensor_tensor(out, out, quad(moved), ALU.add).then_inc(*counts("dve_step"))
                            dve.wait_ge(*counted("dve_step"))

            clear_counts()

        y_out = carve(0, NT, D)
        with nc.Block() as block:
            @block.tensor
            def _(pe):
                for t in range(NT):
                    for q in range(2):
                        transposed(pe, ("y", t, q), [xT[:, 4 * q + i, tok(t)] for i in range(4)])

            @block.vector
            def _(dve):
                for t in range(NT):
                    for q in range(2):
                        dve.wait_ge(*made(("y", t, q)))
                        dve.tensor_copy(y_out[:, t, 512 * q:512 * q + 512], bank(("y", t, q))).then_inc(*reads(("y", t, q)))
                        dve.wait_ge(*read(("y", t, q)))

            @block.sync
            def _(sp):
                for t in range(NT):
                    for q in range(2):
                        sp.wait_ge(*read(("y", t, q)))
                sp.dma_start(y.rearrange("(t p) d -> p t d", p=P), y_out).then_inc(sem["stored"], 16)
                sp.wait_ge(sem["stored"], 16)


_OUTS = [(NT * P, D), (DEPTH, P, KVL), (DEPTH, P, ROPE), (DEPTH, 2, H_B, DK, DV), (DEPTH, 2, H_C * HP, N_ST)]


def _constants():
    import numpy as np
    s, i = np.arange(P)[:, None], np.arange(P)[None, :]
    half = P // 2
    f = np.float32
    c = np.zeros((P, N_CONST), f)
    c[:, C_ID:C_ID + P] = s == i
    c[:, C_REL:C_REL + P] = (s <= i).astype(f) - (s < half).astype(f)
    c[:, C_REL + P:C_REL + 2 * P] = (s >= i).astype(f) - (s >= half).astype(f)
    c[:, C_CUM:C_CUM + P] = s <= i
    c[:, C_CUM + P:C_CUM + 2 * P] = s >= i
    c[:, C_AFT:C_AFT + P] = s > i
    c[:, C_AFT + P:C_AFT + 2 * P] = s < i
    c[:, C_ONE:C_ONE + P] = 1
    c[:, C_SEL] = (s < half)[:, 0]
    c[:, C_SEL + 1] = (s >= half)[:, 0]
    grid_w, n_freq = 64, ROPE // 4
    tok = np.arange(2 * P)
    inv = (1.0 / (np.float32(10000.0) ** (np.arange(n_freq, dtype=f) / f(n_freq)))).astype(f)
    ang = np.concatenate([(tok // grid_w).astype(f)[:, None] * inv, (tok % grid_w).astype(f)[:, None] * inv], 1)
    for t in range(2):
        c[:, C_COS + 16 * t:C_COS + 16 * t + 16] = np.cos(ang[P * t:P * t + P])
        c[:, C_SIN + 16 * t:C_SIN + 16 * t + 16] = np.sin(ang[P * t:P * t + P])
    c[:, C_RANK:C_RANK + 16] = 16 - np.arange(16)
    return c


def kernel(**inputs):
    import numpy as np
    import concourse.bacc as _bacc
    from concourse import mybir as _mybir
    from concourse.bass_utils import run_bass_kernel_spmd as _run

    a = {k: np.asarray(v) for k, v in inputs.items()}
    f = np.float32

    def features(v):
        return v.reshape(DEPTH, -1, P).transpose(0, 2, 1)

    def rows_of(v):
        return np.broadcast_to(v.reshape(DEPTH, 1, -1), (DEPTH, P, v[0].size))

    w_in = a['w_in']
    gates = np.zeros((DEPTH, 2 * RANK + 1, 2, H_B * DK), f)
    for d in range(2):
        gates[:, RANK * d:RANK * d + RANK, d] = a['b_wg'][:, d]
        gates[:, 2 * RANK, d] = a['b_bg'][:, d]
    vecs = np.concatenate(
        [features(a[n]) for n in ('norm1', 'norm2', 'b_ada', 'a_q_norm', 'a_kv_norm', 'c_norm')]
        + [features(np.tile(a['b_onorm'], (1, H_B))),
           a['c_conv_w'].reshape(DEPTH, TAPS * NX, P).transpose(0, 2, 1), features(a['c_conv_b'])], axis=2)
    rows = np.concatenate(
        [rows_of(a[n]) for n in ('a_qk_qnorm', 'a_qk_knorm', 'c_dt_bias', 'c_A_log', 'c_D')]
        + [np.broadcast_to(a['router_bias'], (DEPTH, P, NE))], axis=2)
    named = [
        ('x', np.concatenate([a['x_prompt'][0], a['x_sample'][0]], 0)),
        ('cond', np.stack([a['c_ctx'], a['c'][0]], 0).reshape(2, KD, P).transpose(2, 1, 0)),
        ('consts', _constants()), ('vecs', vecs), ('rows', rows),
        ('w_small', np.concatenate([w_in[:, :, KROPE:KROPE + ROPE], w_in[:, :, DTC:DTC + 32],
                                    w_in[:, :, GLOW:GLOW + 32]], 2)),
        ('w_gate_low', gates), ('router_w', a['router_w']), ('cache_ckv', a['cache_ckv'][0]),
        ('cache_krope', a['cache_krope'][0]), ('state_gla', a['state_gla'][0]),
        ('state_ssd', a['state_ssd'][0].reshape(DEPTH, 2, H_C * HP, N_ST)),
        ('w_ada', a['w_ada']), ('w_in', w_in), ('a_wq', a['a_wq']), ('a_wkv', a['a_wkv']), ('a_wo', a['a_wo']),
        ('b_wo', a['b_wo']), ('c_wo', a['c_wo']), ('w_out', a['w_out']),
        ('e_w1', a['e_w1'].reshape(DEPTH * NE, D, DE)), ('e_w3', a['e_w3'].reshape(DEPTH * NE, D, DE)),
        ('e_w2', a['e_w2'].reshape(DEPTH * NE, DE, D))]
    nc = _bacc.Bacc("TRN2", target_bir_lowering=False, num_devices=1)
    arrays, args = {}, []
    for name, v in named:
        v = np.ascontiguousarray(v)
        arrays[f"in_{name}"] = v
        args.append(nc.dram_tensor(f"in_{name}", v.shape, _mybir.dt.from_np(v.dtype), kind="ExternalInput").ap())
    for i, shape in enumerate(_OUTS):
        args.append(nc.dram_tensor(f"out_{i}", shape, _mybir.dt.from_np(np.dtype(f)), kind="ExternalOutput").ap())
    trunk_kernel(nc, *args)
    r = _run(nc, [arrays], core_ids=[0]).results[0]
    o = [r[f"out_{i}"] for i in range(len(_OUTS))]
    return (o[0][0:P][None], o[0][P:][None], o[1][None], o[2][None], o[3][None],
            o[4].reshape(1, DEPTH, 2, H_C, HP, N_ST))
```

```python
from contextlib import ExitStack

import concourse.bass as bass
from concourse import mybir

F32 = mybir.dt.float32
ALU = mybir.AluOpType
ACT = mybir.ActivationFunctionType
AX_X = mybir.AxisListType.X

P = 128
D = 1024
DEPTH = 2
NT = 3
T = NT * P
KD = D // P
EPS = 1e-6
H_A, NOPE, ROPE, V_A = 16, 64, 32, 64
QK = NOPE + ROPE
QL, KVL = 512, 256
NKT = NT + 1
H_B, DK, DV = 4, 128, 256
RANK = 16
GATE_NORM = 16.0
H_C, HP, N_ST, G_C = 16, 64, 128, 2
XBC = H_C * HP + 2 * G_C * N_ST
NX = XBC // P
TAPS = 5
PAD = TAPS // 2
X_P, X_S = PAD, 3 * PAD + P
XW = X_S + 2 * P + PAD
YW = XW - 2 * PAD
NE, NG = 16, 4
EG = NE // NG
DE = 512
BIG = 1e30
SLOTS = 96
CLAMP = 80.0

CQ, CKV, KROPE, BQ, BK, BV, OG, GLOW, Z, CX, DTC, GATES = (
    0, 512, 768, 800, 1312, 1824, 2848, 3872, 3904, 4928, 6464, 6496)

C_ID, C_REL, C_CUM, C_AFT, C_ONE, C_SEL, C_COS, C_SIN, C_RANK, C_IOTA = (
    0, 128, 384, 640, 896, 1024, 1026, 1058, 1090, 1106)
N_CONST = 1202
V_N1, V_N2, V_BADA, V_QN, V_KVN, V_CN, V_BON, V_CW, V_CB = 0, 8, 16, 64, 68, 70, 78, 86, 146
N_VEC = 158
R_QW, R_KW, R_DTB, R_ALOG, R_D, R_RB = 0, 96, 192, 224, 256, 272
N_ROW = 288

N_ADA = 12
ADA_FIRST = 4
W_CQ, W_CKV, W_BQ, W_WQ, W_BK, W_WKV, W_BV, W_ADA = 4, 5, 6, 7, 9, 10, 11, 13
W_GA, W_AO, W_OG, W_GB, W_BO = 21, 23, 25, 27, 29
W_Z, W_CX, W_GC, W_CO, W_OUT, W_MOE = 31, 33, 36, 38, 40, 42
RING = 3


def trunk_kernel(nc, x, cond, consts, vecs, rows, w_small, w_gate_low, router_w, cache_ckv, cache_krope,
                 state_gla, state_ssd, w_ada, w_in, a_wq, a_wkv, a_wo, b_wo, c_wo, w_out, e_w1, e_w3, e_w2,
                 y, new_ckv, new_krope, new_gla, new_ssd):
    with ExitStack() as ctx:
        def sb(name, shape):
            return ctx.enter_context(nc.sbuf_tensor(name, shape, F32))

        ring = sb("ring", [P, RING, 4096])
        xT = sb("xT", [P, KD, T])
        hT = sb("hT", [P, KD, T])
        mT = sb("mT", [P, KD, T])
        cst = sb("cst", [P, N_CONST])
        vec = sb("vec", [P, N_VEC])
        row = sb("row", [P, N_ROW])
        wsm = sb("wsm", [P, KD, 96])
        wgl = sb("wgl", [2 * RANK + 1, 2, 512])
        rw = sb("rw", [P, KD, NE])
        condT = sb("condT", [P, KD, 2])
        scond = sb("scond", [P, KD, 2])
        mod = sb("mod", [P, 6, KD, 2])
        amp = sb("amp", [P, 2, KD, 2])
        dtraw = sb("dtraw", [P, NT, 32])
        lowT = sb("lowT", [2 * RANK + 1, T])
        rstd = sb("rstd", [P, T])
        arena = sb("arena", [P, 26500])
        overflow = ctx.enter_context(nc.sbuf_tensor("overflow", [1, 1], mybir.dt.int32))
        ps = ctx.enter_context(nc.psum_tensor("ps", [P, 8, 512], F32))

        names = (
            "xin", "cond_ready", "params_in", "cache_in", "squares_ready", "root_ready", "weighted",
            "h_ready", "cqn_ready", "ckvn_ready", "sq_ready", "summed", "stat_ready", "head_root", "rotary_in",
            "nmax_ready", "abs_ready", "soft_ready", "logdecay_ready", "clamped_ready", "decay_ready",
            "qk_ready", "gla_state_in", "scaled_state", "state_ready", "o_ready", "conv_ready",
            "xbc_ready", "ssd_state_in", "diff_ready", "decayed_ready", "mask_ready", "xw_ready",
            "yoff_ready", "y_ready", "merged_ready", "chosen_ready", "picked", "hidden_ready", "moe_ready", "stored",
            "act_step", "dve_step", "pool_step")
        sem = {n: ctx.enter_context(nc.semaphore(n)) for n in names}
        w_loaded = [ctx.enter_context(nc.semaphore(f"w_loaded{i}")) for i in range(RING)]
        psum_full = [ctx.enter_context(nc.semaphore(f"psum_full{i}")) for i in range(8)]
        psum_free = [ctx.enter_context(nc.semaphore(f"psum_free{i}")) for i in range(8)]

        count, waited = {}, {}
        job = {}
        uses = [0] * 8
        turn = [0]
        last_use = {}

        def counts(name):
            count[name] = count.get(name, 0) + 1
            return sem[name], 1

        def counted(name):
            return sem[name], count[name]

        def following(eng, name, by=1):
            key = (str(eng.engine), name)
            waited[key] = waited.get(key, 0) + by
            return sem[name], waited[key]

        def claim(pe, key, bank=None):
            if bank is None:
                bank = turn[0] % 8
                turn[0] += 1
            job[key] = (bank, uses[bank])
            if uses[bank]:
                pe.wait_ge(psum_free[bank], uses[bank])
            uses[bank] += 1
            return ps[:, bank, :]

        def bank(key):
            return ps[:, job[key][0], :]

        def makes(key):
            return psum_full[job[key][0]], 1

        def made(key):
            return psum_full[job[key][0]], job[key][1] + 1

        def reads(key):
            return psum_free[job[key][0]], 1

        def read(key):
            return psum_free[job[key][0]], job[key][1] + 1

        def carve(off, *shape):
            n = 1
            for s in shape:
                n *= s
            v = arena[:, off:off + n]
            if len(shape) == 2:
                return v.rearrange("p (a b) -> p a b", b=shape[1])
            if len(shape) == 3:
                return v.rearrange("p (a b c) -> p a b c", b=shape[1], c=shape[2])
            if len(shape) == 4:
                return v.rearrange("p (a b c d) -> p a b c d", b=shape[1], c=shape[2], d=shape[3])
            return v

        ident = cst[:, C_ID:C_ID + P]
        ones = cst[:, C_ONE:C_ONE + P]

        def rel(d):
            return cst[:, C_REL + P * d:C_REL + P * d + P]

        def cum(d):
            return cst[:, C_CUM + P * d:C_CUM + P * d + P]

        def aft(d):
            return cst[:, C_AFT + P * d:C_AFT + P * d + P]

        COND = ((slice(0, P), 0), (slice(P, T), 1))

        def tok(t):
            return slice(t * P, t * P + P)

        def quad(ap):
            return ap.rearrange("p (a b) -> p a b", b=P)

        def over(ap, n):
            return ap.unsqueeze(2).broadcast_to([ap.shape[0], ap.shape[1], n])

        def each(ap, n):
            return ap.unsqueeze(1).broadcast_to([ap.shape[0], n, ap.shape[1]])

        def chunk(n, k, w):
            return ring[:, n % RING, 0:k * w].rearrange("p (k w) -> p k w", k=k)

        def kpn(ap, i):
            return ap[bass.ds(i, 1)].rearrange("a (k p) n -> p (a k) n", p=P)

        def weight_source(n, l):
            cols = {W_CQ: (CQ, 512), W_CKV: (CKV, KVL), W_BQ: (BQ, 512), W_BK: (BK, 512)}
            for base, col, m in ((W_GA, GATES, 2), (W_GB, GATES + D, 2), (W_GC, GATES + 2 * D, 2), (W_BV, BV, 2),
                                 (W_OG, OG, 2), (W_Z, Z, 2), (W_CX, CX, 3)):
                for i in range(m):
                    cols[base + i] = (col + 512 * i, 512)
            if n < ADA_FIRST or W_ADA <= n < W_ADA + N_ADA - ADA_FIRST:
                c = 512 * (n if n < ADA_FIRST else n - W_ADA + ADA_FIRST)
                return kpn(w_ada, l)[:, :, c:c + 512], KD, 512
            if n in cols:
                c, w = cols[n]
                return kpn(w_in, l)[:, :, c:c + w], KD, w
            if n in (W_WQ, W_WQ + 1):
                i = n - W_WQ
                return kpn(a_wq, l)[:, :, 768 * i:768 * i + 768], QL // P, 768
            if n == W_WKV:
                return kpn(a_wkv, l), KVL // P, 2048
            for base, ap in ((W_AO, a_wo), (W_BO, b_wo), (W_CO, c_wo), (W_OUT, w_out)):
                if n in (base, base + 1):
                    return kpn(ap, l)[:, :, 512 * (n - base):512 * (n - base) + 512], KD, 512
            raise AssertionError(n)

        def expert_source(i, l, e):
            k = (KD, KD, DE // P)[i]
            return kpn((e_w1, e_w3, e_w2)[i], l * NE + e), k, 4096 // k

        def load_weights(sp, l, n0, n1):
            for n in range(n0, n1):
                if n >= RING:
                    sp.wait_ge(*made(last_use[n - RING]))
                src, k, w = weight_source(n, l) if n < W_MOE else expert_source(n - W_MOE, l, 0)
                sp.dma_start(chunk(n, k, w), src).then_inc(w_loaded[n % RING], 16)

        def weights(pe, n, k, w):
            pe.wait_ge(w_loaded[n % RING], 16 * (n // RING + 1))
            return chunk(n, k, w)

        def matmuls(pe, out, pairs):
            for i, (a, b) in enumerate(pairs):
                ins = pe.matmul(out, a, b, start=(i == 0), stop=(i == len(pairs) - 1))
            return ins

        def feature_major(pe, n, key, src, m=4):
            w = weights(pe, n, KD, P * m)
            for j in range(m):
                matmuls(pe, claim(pe, (key, j))[:, 0:T],
                        [(w[:, k, P * j:P * j + P], src[:, k, :]) for k in range(KD)]).then_inc(*makes((key, j)))
            last_use[n] = (key, m - 1)

        def token_major(pe, n, key):
            w = weights(pe, n, KD, 512)
            for t in range(NT):
                matmuls(pe, claim(pe, (key, t)), [(hT[:, k, tok(t)], w[:, k, :]) for k in range(KD)]).then_inc(*makes((key, t)))
            last_use[n] = (key, NT - 1)

        def square_sum(pe, key, sq, kd, made_from=()):
            out = claim(pe, key)
            if not made_from:
                pe.wait_ge(*following(pe, "squares_ready"))
            for k in made_from:
                pe.wait_ge(*read(k))
            matmuls(pe, out[:, 0:T], [(ones, sq[:, k, :]) for k in range(kd)]).then_inc(*makes(key))

        def transposed(pe, key, srcs, bank=None):
            out = claim(pe, key, bank)
            for i, s in enumerate(srcs):
                ins = pe.transpose(out[0:s.shape[1], i * P:i * P + P], s, ident)
            ins.then_inc(*makes(key))

        def root_mean(dve, key, n):
            dve.wait_ge(*made(key))
            s = bank(key)
            dve.tensor_scalar(rstd[:, :], s[:, 0:T], 1.0 / n, EPS, ALU.mult, ALU.add).then_inc(*reads(key))
            dve.wait_ge(*read(key))
            dve.wait_ge(*following(dve, "root_ready"))
            dve.reciprocal(rstd[:, :], rstd[:, :]).then_inc(*counts("dve_step"))
            dve.wait_ge(*counted("dve_step"))

        def root(act, key):
            act.wait_ge(*read(key))
            act.activation(rstd[:, :], rstd[:, :], ACT.Sqrt).then_inc(*counts("root_ready"))

        def norm_dve(dve, key):
            root_mean(dve, key, D)
            dve.tensor_tensor(hT[:, :, :], xT[:, :, :], each(rstd[:, :], KD), ALU.mult).then_inc(*counts("weighted"))

        def modulation_pe(pe, n):
            c = n if n < ADA_FIRST else n - ADA_FIRST + W_ADA
            w = weights(pe, c, KD, 512)
            m = claim(pe, ("mod", n))
            for j in range(4):
                ins = matmuls(pe, m[:, 2 * j:2 * j + 2], [(w[:, k, P * j:P * j + P], scond[:, k, :]) for k in range(KD)])
            ins.then_inc(*makes(("mod", n)))
            last_use[c] = ("mod", n)

        def modulation_dve(dve, n):
            dve.wait_ge(*made(("mod", n)))
            s = bank(("mod", n))
            modc = mod.rearrange("p s k c -> p (s k) c")
            dve.tensor_tensor(modc[:, 4 * n:4 * n + 4, :], s[:, 0:8].rearrange("p (a b) -> p a b", b=2),
                              over(vec[:, V_BADA + 4 * n:V_BADA + 4 * n + 4], 2), ALU.add).then_inc(*reads(("mod", n)))
            dve.wait_ge(*read(("mod", n)))

        def amplitude(dve, i, w):
            dve.scalar_tensor_tensor(out=amp[:, i, :, :], in0=mod[:, 3 * i + 1, :, :], scalar=1.0,
                                     in1=over(vec[:, w:w + KD], 2), op0=ALU.add, op1=ALU.mult
                                     ).then_inc(*counts("dve_step"))
            dve.wait_ge(*counted("dve_step"))

        def norm_act(act, i, key, sq):
            act.activation(sq, xT[:, :, :], ACT.Square).then_inc(*counts("squares_ready"))
            root(act, key)
            act.wait_ge(*following(act, "weighted"))
            for k in range(KD):
                for ts, c in COND:
                    ins = act.activation(hT[:, k, ts], hT[:, k, ts], ACT.Identity,
                                         bias=mod[:, 3 * i, k, c:c + 1], scale=amp[:, i, k, c:c + 1])
            ins.then_inc(*counts("h_ready"))

        def gate_act(act, key, gT):
            for i in range(2):
                for j in range(4):
                    act.wait_ge(*made(((key, i), j)))
                    s = bank(((key, i), j))
                    act.activation(gT[:, 4 * i + j, :], s[:, 0:T], ACT.Sigmoid).then_inc(*reads(((key, i), j)))
                    act.wait_ge(*read(((key, i), j)))

        def gated_sum(dve, key, gkey, gT, first):
            for i in range(2):
                for j in range(4):
                    d = 4 * i + j
                    dve.wait_ge(*made(((key, i), j)))
                    s = bank(((key, i), j))
                    dve.wait_ge(*read(((gkey, i), j)))
                    if first:
                        dve.tensor_tensor(mT[:, d, :], s[:, 0:T], gT[:, d, :], ALU.mult).then_inc(*reads(((key, i), j)))
                        dve.wait_ge(*read(((key, i), j)))
                    else:
                        dve.tensor_tensor(gT[:, d, :], s[:, 0:T], gT[:, d, :], ALU.mult).then_inc(*reads(((key, i), j)))
                        dve.wait_ge(*read(((key, i), j)))
                        ins = dve.tensor_tensor(mT[:, d, :], mT[:, d, :], gT[:, d, :], ALU.add)
                        ins.then_inc(*counts("dve_step"))
                        dve.wait_ge(*counted("dve_step"))

        def to_features(pe, key, src):
            for t in range(NT):
                for q in range(2):
                    transposed(pe, (key, t, q), [src[:, t, 512 * q + P * i:512 * q + P * i + P] for i in range(4)])

        def features_dve(dve, key, dst, w=None):
            for t in range(NT):
                for q in range(2):
                    dve.wait_ge(*made((key, t, q)))
                    s = quad(bank((key, t, q)))
                    out = dst[:, 4 * q:4 * q + 4, tok(t)]
                    if w is None:
                        ins = dve.tensor_copy(out, s)
                    else:
                        ins = dve.tensor_tensor(out, s, over(vec[:, w + 4 * q:w + 4 * q + 4], P), ALU.mult)
                    ins.then_inc(*reads((key, t, q)))
                    dve.wait_ge(*read((key, t, q)))

        def project_pe(pe, n, key, src, tkey):
            for t in range(NT):
                for q in range(2):
                    pe.wait_ge(*read((tkey, t, q)))
            for i in range(2):
                feature_major(pe, n + i, (key, i), src)

        x_in = carve(0, NT, D)
        with nc.Block() as block:
            @block.tensor
            def _(pe):
                pe.wait_ge(sem["xin"], 64)
                to_features(pe, "x", x_in)

            @block.sync
            def _(sp):
                sp.dma_start(x_in, x.rearrange("(t p) d -> p t d", p=P)).then_inc(sem["xin"], 16)
                sp.dma_start(cst[:, :], consts).then_inc(sem["xin"], 16)
                sp.dma_start(condT[:, :, :], cond).then_inc(sem["xin"], 16)
                sp.dma_start(rw[:, :, :], router_w.rearrange("(k p) e -> p k e", p=P)).then_inc(sem["xin"], 16)
                sp.wait_ge(sem["xin"], 64)

            @block.vector
            def _(dve):
                dve.memset(lowT[2 * RANK:2 * RANK + 1, :], 1.0).then_inc(*counts("dve_step"))
                dve.wait_ge(*counted("dve_step"))
                features_dve(dve, "x", xT)

            @block.scalar
            def _(act):
                act.wait_ge(sem["xin"], 64)
                act.activation(scond[:, :, :], condT[:, :, :], ACT.Silu).then_inc(*counts("cond_ready"))
                act.wait_ge(*counted("cond_ready"))

        def clear_counts():
            for s in list(sem.values()) + w_loaded + psum_full + psum_free:
                nc.sync.sem_clear(s)
            nc.all_engine_barrier()
            for d in (count, waited, job, last_use):
                d.clear()
            for b in range(8):
                uses[b] = 0

        clear_counts()

        m_flat = mT[:, :, :].rearrange("p k t -> p (k t)")
        q_tok = carve(0, NT, H_A, QK)
        k_tok = carve(4608, NKT, H_A, QK)
        v_a = carve(10752, NKT, H_A, V_A)
        q_b = carve(14848, NT, H_B, DK)
        k_b = carve(16384, NT, H_B, DK)
        v_b = carve(17920, NT, H_B, DV)
        cqT = carve(20992, QL // P, T)
        ckvT = carve(22528, KVL // P, T + P)
        kr = carve(23552, NKT, ROPE)
        cache_tok = carve(23680, KVL)
        ckv_out = carve(23936, KVL)
        stat = carve(24192, 2, NKT * H_A)
        sq_heads = carve(24320, H_A, QK)
        rope_tmp = carve(20992, 4, H_A, ROPE // 2)
        sq_x = carve(17920, KD, T)
        sq4 = m_flat[:, 0:QL // P * T].rearrange("p (a b) -> p a b", b=T)
        sq2 = m_flat[:, 1536:1536 + KVL // P * T].rearrange("p (a b) -> p a b", b=T)
        o_tok = m_flat.rearrange("p (t d) -> p t d", d=D)
        head_qT = carve(20992, 2, T)
        head_kT = carve(21760, 2, T + P)
        probs = carve(22784, 3, T)
        probsT = carve(23936, 2, T)
        nmax = carve(24704, 4)
        rsum = carve(24720, NT, H_A)
        gT = carve(0, KD, T)
        oT = carve(4608, KD, T)

        with nc.Fori(0, DEPTH) as l:
            with nc.Block() as block:
                @block.tensor
                def _(pe):
                    square_sum(pe, "n1", sq_x, KD)
                    for n in range(ADA_FIRST):
                        modulation_pe(pe, n)
                    pe.wait_ge(*following(pe, "h_ready"))
                    feature_major(pe, W_CQ, "cq", hT)
                    feature_major(pe, W_CKV, "ckv", hT, 2)
                    pe.wait_ge(*following(pe, "params_in", 64))
                    out = claim(pe, "krdt")
                    for t in range(NT):
                        ins = matmuls(pe, out[:, 64 * t:64 * t + 64],
                                      [(hT[:, k, tok(t)], wsm[:, k, 0:64]) for k in range(KD)])
                    ins.then_inc(*makes("krdt"))
                    out = claim(pe, "low")
                    matmuls(pe, out[0:2 * RANK, 0:T], [(wsm[:, k, 64:96], hT[:, k, :]) for k in range(KD)]
                            ).then_inc(*makes("low"))
                    pe.wait_ge(*following(pe, "cache_in", 32))
                    transposed(pe, "cache", [cache_tok[:, 0:P], cache_tok[:, P:2 * P]])
                    square_sum(pe, "ncq", sq4, QL // P, [("cq", j) for j in range(QL // P)])
                    square_sum(pe, "nckv", sq2, KVL // P, [("ckv", j) for j in range(KVL // P)])
                    token_major(pe, W_BQ, "bq")
                    pe.wait_ge(*following(pe, "cqn_ready"))
                    for c in range(2):
                        w = weights(pe, W_WQ + c, QL // P, 768)
                        for t in range(NT):
                            for h in range(2):
                                matmuls(pe, claim(pe, ("q", c, t, h))[:, 0:384],
                                        [(cqT[:, k, tok(t)], w[:, k, 384 * h:384 * h + 384])
                                         for k in range(QL // P)]).then_inc(*makes(("q", c, t, h)))
                        last_use[W_WQ + c] = ("q", c, NT - 1, 1)
                    token_major(pe, W_BK, "bk")
                    pe.wait_ge(*following(pe, "ckvn_ready"))
                    pe.wait_ge(*read("cache"))
                    transposed(pe, "ckv_out", [ckvT[:, 0, 0:P], ckvT[:, 1, 0:P]])
                    w = weights(pe, W_WKV, KVL // P, 2048)
                    for t in range(NKT):
                        for h in range(4):
                            matmuls(pe, claim(pe, ("kv", t, h)),
                                    [(ckvT[:, k, tok(t)], w[:, k, 512 * h:512 * h + 512])
                                     for k in range(KVL // P)]).then_inc(*makes(("kv", t, h)))
                    last_use[W_WKV] = ("kv", NKT - 1, 3)
                    for i in range(2):
                        token_major(pe, W_BV + i, ("bv", i))

                @block.sync
                def _(sp):
                    load_weights(sp, l, 0, RING)
                    for dst, src in ((vec[:, :], vecs), (row[:, :], rows)):
                        sp.dma_start(dst, src[bass.ds(l, 1)].rearrange("a p n -> p (a n)")).then_inc(sem["params_in"], 16)
                    sp.dma_start(wsm[:, :, :], kpn(w_small, l)).then_inc(sem["params_in"], 16)
                    sp.dma_start(wgl[:, :, :], w_gate_low[bass.ds(l, 1)].rearrange("a r d n -> r (a d) n")
                                 ).then_inc(sem["params_in"], 16)
                    sp.dma_start(cache_tok, cache_ckv[bass.ds(l, 1)].rearrange("a p n -> p (a n)")
                                 ).then_inc(sem["cache_in"], 16)
                    sp.dma_start(kr[:, NT, :], cache_krope[bass.ds(l, 1)].rearrange("a p n -> p (a n)")
                                 ).then_inc(sem["cache_in"], 16)
                    load_weights(sp, l, RING, W_ADA + RING)
                    sp.wait_ge(*read("krdt"))
                    sp.dma_start(new_krope[bass.ds(l, 1)].rearrange("a p n -> p (a n)"), kr[:, 0, :]
                                 ).then_inc(sem["stored"], 16)
                    sp.wait_ge(*read("ckv_out"))
                    sp.dma_start(new_ckv[bass.ds(l, 1)].rearrange("a p n -> p (a n)"), ckv_out
                                 ).then_inc(sem["stored"], 16)
                    sp.wait_ge(*following(sp, "stored", 32))

                @block.scalar
                def _(act):
                    norm_act(act, 0, "n1", sq_x)
                    for j in range(QL // P):
                        act.wait_ge(*made(("cq", j)))
                        s = bank(("cq", j))
                        act.activation(cqT[:, j, :], s[:, 0:T], ACT.Copy).then_inc(*counts("act_step"))
                        act.wait_ge(*counted("act_step"))
                        act.activation(sq4[:, j, :], s[:, 0:T], ACT.Square).then_inc(*reads(("cq", j)))
                        act.wait_ge(*read(("cq", j)))
                    for j in range(KVL // P):
                        act.wait_ge(*made(("ckv", j)))
                        s = bank(("ckv", j))
                        act.activation(ckvT[:, j, 0:T], s[:, 0:T], ACT.Copy).then_inc(*counts("act_step"))
                        act.wait_ge(*counted("act_step"))
                        act.activation(sq2[:, j, :], s[:, 0:T], ACT.Square).then_inc(*reads(("ckv", j)))
                        act.wait_ge(*read(("ckv", j)))
                    root(act, "ncq")
                    root(act, "nckv")

                    def evacuate(key, dst, scale=1.0):
                        act.wait_ge(*made(key))
                        act.activation(dst, bank(key).rearrange("p (h d) -> p h d", h=dst.shape[1]), ACT.Copy, scale=scale
                                       ).then_inc(*reads(key))
                        act.wait_ge(*read(key))

                    for t in range(NT):
                        evacuate(("bq", t), q_b[:, t, :, :], float(DK) ** -0.5)

                    def squares(x, i, t):
                        if (i, t) != (0, 0):
                            act.wait_ge(*following(act, "summed"))
                        act.activation(sq_heads, x[:, t, :, :], ACT.Square).then_inc(*counts("sq_ready"))

                    for t in range(NT):
                        for c in range(2):
                            for h in range(2):
                                act.wait_ge(*read(("q", c, t, h)))
                        squares(q_tok, 0, t)
                    act.wait_ge(*following(act, "stat_ready"))
                    act.activation(stat[:, 0, 0:NT * H_A], stat[:, 0, 0:NT * H_A], ACT.Sqrt).then_inc(*counts("head_root"))
                    for t in range(NT):
                        evacuate(("bk", t), k_b[:, t, :, :])
                    act.wait_ge(*made("ckv_out"))
                    act.activation(ckv_out, bank("ckv_out")[:, 0:KVL], ACT.Copy).then_inc(*reads("ckv_out"))
                    act.wait_ge(*read("ckv_out"))
                    act.wait_ge(*following(act, "rotary_in"))
                    for t in range(NKT):
                        for h in range(4):
                            act.wait_ge(*made(("kv", t, h)))
                            s = bank(("kv", t, h)).rearrange("p (h d) -> p h d", h=4)
                            act.activation(v_a[:, t, 4 * h:4 * h + 4, :], s[:, :, NOPE:], ACT.Copy
                                           ).then_inc(*counts("act_step"))
                            act.activation(k_tok[:, t, 4 * h:4 * h + 4, 0:NOPE], s[:, :, 0:NOPE], ACT.Copy
                                           ).then_inc(*reads(("kv", t, h)))
                            act.wait_ge(*read(("kv", t, h)))
                        squares(k_tok, 1, t)
                    for i in range(2):
                        for t in range(NT):
                            if (i, t) == (0, 1):
                                act.wait_ge(*following(act, "summed"))
                                act.wait_ge(*following(act, "stat_ready"))
                                act.activation(stat[:, 1, :], stat[:, 1, :], ACT.Sqrt).then_inc(*counts("head_root"))
                            evacuate((("bv", i), t), v_b[:, t, 2 * i:2 * i + 2, :])

                @block.gpsimd
                def _(pool):
                    pool.wait_ge(*following(pool, "cache_in", 32))
                    pool.wait_ge(*read("krdt"))
                    for t in range(NKT):
                        ins = pool.tensor_copy(k_tok[:, t, :, NOPE:], each(kr[:, t, :], H_A))
                    ins.then_inc(*counts("rotary_in"))

                @block.vector
                def _(dve):
                    dve.wait_ge(*following(dve, "params_in", 64))
                    for n in range(ADA_FIRST):
                        modulation_dve(dve, n)
                    amplitude(dve, 0, V_N1)
                    norm_dve(dve, "n1")
                    dve.wait_ge(*made("krdt"))
                    s = bank("krdt")[:, 0:NT * 64].rearrange("p (t c) -> p t c", c=64)
                    dve.tensor_copy(dtraw[:, :, :], s[:, :, 32:64]).then_inc(*counts("dve_step"))
                    dve.wait_ge(*counted("dve_step"))
                    dve.tensor_copy(kr[:, 0:NT, :], s[:, :, 0:32]).then_inc(*reads("krdt"))
                    dve.wait_ge(*read("krdt"))
                    dve.wait_ge(*made("low"))
                    dve.tensor_copy(lowT[0:2 * RANK, :], bank("low")[0:2 * RANK, 0:T]).then_inc(*reads("low"))
                    dve.wait_ge(*read("low"))
                    dve.wait_ge(*made("cache"))
                    dve.tensor_copy(ckvT[:, :, T:], quad(bank("cache")[:, 0:2 * P])).then_inc(*reads("cache"))
                    dve.wait_ge(*read("cache"))
                    root_mean(dve, "ncq", QL)
                    for j in range(QL // P):
                        ins = dve.scalar_tensor_tensor(out=cqT[:, j, :], in0=cqT[:, j, :], scalar=vec[:, V_QN + j:V_QN + j + 1],
                                                       in1=rstd[:, :], op0=ALU.mult, op1=ALU.mult)
                    ins.then_inc(*counts("cqn_ready"))
                    dve.wait_ge(*counted("cqn_ready"))
                    root_mean(dve, "nckv", KVL)
                    for j in range(KVL // P):
                        ins = dve.scalar_tensor_tensor(out=ckvT[:, j, 0:T], in0=ckvT[:, j, 0:T],
                                                       scalar=vec[:, V_KVN + j:V_KVN + j + 1],
                                                       in1=rstd[:, :], op0=ALU.mult, op1=ALU.mult)
                    ins.then_inc(*counts("ckvn_ready"))
                    dve.wait_ge(*counted("ckvn_ready"))
                    for c in range(2):
                        for t in range(NT):
                            for h in range(2):
                                dve.wait_ge(*made(("q", c, t, h)))
                                h0 = 8 * c + 4 * h
                                dve.tensor_copy(q_tok[:, t, h0:h0 + 4, :],
                                                bank(("q", c, t, h))[:, 0:384].rearrange("p (h d) -> p h d", d=QK)
                                                ).then_inc(*reads(("q", c, t, h)))
                                dve.wait_ge(*read(("q", c, t, h)))

                    def head_norm(x, tiles, i, scale, w):
                        n = tiles * H_A
                        heads = x.rearrange("p t h d -> p (t h) d")
                        st = stat[:, i, 0:n]
                        for t in range(tiles):
                            dve.wait_ge(*following(dve, "sq_ready"))
                            dve.tensor_reduce(stat[:, i, H_A * t:H_A * t + H_A], sq_heads, AX_X, ALU.add
                                              ).then_inc(*counts("summed"))
                            dve.wait_ge(*counted("summed"))
                        dve.tensor_scalar(st, st, 1.0 / QK, EPS, ALU.mult, ALU.add).then_inc(*counts("stat_ready"))
                        dve.wait_ge(*counted("stat_ready"))
                        dve.wait_ge(*following(dve, "head_root"))
                        dve.reciprocal(st, st).then_inc(*counts("dve_step"))
                        dve.wait_ge(*counted("dve_step"))
                        dve.tensor_tensor(heads, heads, over(st, QK), ALU.mult).then_inc(*counts("dve_step"))
                        dve.wait_ge(*counted("dve_step"))
                        dve.scalar_tensor_tensor(out=heads, in0=heads, scalar=scale, in1=each(row[:, w:w + QK], n),
                                                 op0=ALU.mult, op1=ALU.mult).then_inc(*counts("dve_step"))
                        dve.wait_ge(*counted("dve_step"))

                    def rotate(x):
                        for t in (1, 2):
                            pairs = x[:, t, :, NOPE:].rearrange("p h (m two) -> p h two m", two=2)
                            x1, x2 = pairs[:, :, 0, :], pairs[:, :, 1, :]
                            cos = each(cst[:, C_COS + 16 * (t - 1):C_COS + 16 * t], H_A)
                            sin = each(cst[:, C_SIN + 16 * (t - 1):C_SIN + 16 * t], H_A)
                            for i, (a, b) in enumerate(((x1, cos), (x2, sin), (x1, sin), (x2, cos))):
                                ins = dve.tensor_tensor(rope_tmp[:, i, :, :], a, b, ALU.mult)
                            ins.then_inc(*counts("dve_step"))
                            dve.wait_ge(*counted("dve_step"))
                            dve.tensor_tensor(x1, rope_tmp[:, 0], rope_tmp[:, 1], ALU.subtract)
                            dve.tensor_tensor(x2, rope_tmp[:, 2], rope_tmp[:, 3], ALU.add).then_inc(*counts("dve_step"))
                            dve.wait_ge(*counted("dve_step"))

                    head_norm(q_tok, NT, 0, float(QK) ** -0.5, R_QW)
                    rotate(q_tok)
                    head_norm(k_tok, NKT, 1, 1.0, R_KW)
                    rotate(k_tok)

            STEPS = [(h, t) for h in range(H_A) for t in range(NT)]
            KEYS = ((0, 1), (1, NKT), (1, NKT))
            AHEAD = 2
            ADA_AT = {5 * n + 2: ADA_FIRST + n for n in range(N_ADA - ADA_FIRST)}
            B_PV, N_ROT = 5, 5
            with nc.Block() as block:
                def next_head(i):
                    return (i + 1) // NT + 1 if i % NT == NT - 1 and (i + 1) // NT + 1 < H_A else None

                @block.tensor
                def _(pe):
                    turns = [0]

                    def rotating(key):
                        turns[0] += 1
                        return claim(pe, key, turns[0] % N_ROT)

                    def head(h):
                        for key, x, tiles in ((("qT", h), q_tok, NT), (("kT", h), k_tok, NKT)):
                            out = rotating(key)
                            for t in range(tiles):
                                ins = pe.transpose(out[0:QK, tok(t)], x[:, t, h, :], ident)
                            ins.then_inc(*makes(key))

                    def scores(i):
                        h, t = STEPS[i]
                        k0, k1 = KEYS[t]
                        if t == 0:
                            pe.wait_ge(*read(("qT", h)))
                            pe.wait_ge(*read(("kT", h)))
                        out = rotating(("s", i))
                        pe.matmul(out[:, 0:P * (k1 - k0)], head_qT[0:QK, h % 2, tok(t)],
                                  head_kT[0:QK, h % 2, P * k0:P * k1], start=True, stop=True).then_inc(*makes(("s", i)))

                    def turn_probs(i):
                        h, t = STEPS[i]
                        k0, k1 = KEYS[t]
                        pe.wait_ge(*read(("s", i)))
                        out = rotating(("pt", i))
                        for k in range(k1 - k0):
                            ins = pe.transpose(out[:, P * k:P * k + P], probs[:, i % 3, P * k:P * k + P], ident)
                        ins.then_inc(*makes(("pt", i)))

                    def weigh_values(i):
                        h, t = STEPS[i]
                        k0, k1 = KEYS[t]
                        if h % 8 == 0:
                            claim(pe, ("pv", t, h // 8), B_PV + t)
                        pe.wait_ge(*read(("pt", i)))
                        c = V_A * (h % 8)
                        ins = matmuls(pe, ps[:, B_PV + t, c:c + V_A],
                                      [(probsT[:, i % 2, P * k:P * k + P], v_a[:, k0 + k, h, :]) for k in range(k1 - k0)])
                        if h % 8 == 7:
                            ins.then_inc(*makes(("pv", t, h // 8)))

                    head(0)
                    head(1)
                    for i in range(-AHEAD, len(STEPS) + 1):
                        if i + AHEAD < len(STEPS):
                            scores(i + AHEAD)
                        if i >= 0 and next_head(i):
                            head(next_head(i))
                        if 0 <= i < len(STEPS):
                            turn_probs(i)
                        if i >= 1:
                            weigh_values(i - 1)
                        if i in ADA_AT:
                            n = ADA_AT[i]
                            turns[0] += 1
                            turn[0] = turns[0] % N_ROT
                            modulation_pe(pe, n)

                @block.scalar
                def _(act):
                    def queries(h):
                        act.wait_ge(*made(("qT", h)))
                        act.activation(head_qT[0:QK, h % 2, :], bank(("qT", h))[0:QK, 0:T], ACT.Copy).then_inc(*reads(("qT", h)))
                        act.wait_ge(*read(("qT", h)))

                    queries(0)
                    queries(1)
                    for j in range(-AHEAD, len(STEPS)):
                        i = j + AHEAD
                        if i < len(STEPS):
                            h, t = STEPS[i]
                            n = P * (KEYS[t][1] - KEYS[t][0])
                            if i >= 3:
                                act.wait_ge(*made(("pt", i - 3)))
                            act.wait_ge(*following(act, "nmax_ready"))
                            act.wait_ge(*made(("s", i)))
                            s = bank(("s", i))
                            act.activation(probs[:, i % 3, 0:n], s[:, 0:n], ACT.Exp, bias=nmax[:, i % 4:i % 4 + 1],
                                           accum_out=rsum[:, t, h:h + 1]).then_inc(*reads(("s", i)))
                            act.wait_ge(*read(("s", i)))
                        if j >= 0 and next_head(j):
                            queries(next_head(j))

                @block.vector
                def _(dve):
                    def keys(h):
                        dve.wait_ge(*made(("kT", h)))
                        dve.tensor_copy(head_kT[0:QK, h % 2, :], bank(("kT", h))[0:QK, :]).then_inc(*reads(("kT", h)))
                        dve.wait_ge(*read(("kT", h)))

                    def turned(i):
                        h, t = STEPS[i]
                        n = P * (KEYS[t][1] - KEYS[t][0])
                        dve.wait_ge(*made(("pt", i)))
                        dve.tensor_copy(probsT[:, i % 2, 0:n], bank(("pt", i))[:, 0:n]).then_inc(*reads(("pt", i)))
                        dve.wait_ge(*read(("pt", i)))

                    def heads_out(t, g):
                        dve.wait_ge(*made(("pv", t, g)))
                        s = bank(("pv", t, g)).rearrange("p (h d) -> p h d", d=V_A)
                        r = rsum[:, t, 8 * g:8 * g + 8]
                        dve.reciprocal(r, r).then_inc(*counts("dve_step"))
                        dve.wait_ge(*counted("dve_step"))
                        dve.tensor_tensor(o_tok[:, t, 512 * g:512 * g + 512].rearrange("p (h d) -> p h d", d=V_A),
                                          s, over(r, V_A), ALU.mult).then_inc(*reads(("pv", t, g)))
                        dve.wait_ge(*read(("pv", t, g)))

                    keys(0)
                    keys(1)
                    for j in range(-AHEAD, len(STEPS) + 2):
                        i = j + AHEAD
                        if i < len(STEPS):
                            h, t = STEPS[i]
                            n = P * (KEYS[t][1] - KEYS[t][0])
                            dve.wait_ge(*made(("s", i)))
                            s = bank(("s", i))
                            dve.tensor_reduce(nmax[:, i % 4:i % 4 + 1], s[:, 0:n], AX_X, ALU.max, negate=True
                                              ).then_inc(*counts("nmax_ready"))
                        if j >= 0 and next_head(j):
                            keys(next_head(j))
                        if 0 <= j < len(STEPS):
                            turned(j)
                        if j >= 2:
                            h, t = STEPS[j - 2]
                            if h % 8 == 7:
                                heads_out(t, h // 8)
                        if j in ADA_AT:
                            modulation_dve(dve, ADA_AT[j])
                    amplitude(dve, 1, V_N2)

                @block.sync
                def _(sp):
                    load_weights(sp, l, W_ADA + RING, W_GA + RING)

            with nc.Block() as block:
                @block.tensor
                def _(pe):
                    for i in range(2):
                        feature_major(pe, W_GA + i, ("ga", i), hT)
                    to_features(pe, "oa", o_tok)
                    project_pe(pe, W_AO, "ao", oT, "oa")

                @block.scalar
                def _(act):
                    gate_act(act, "ga", gT)

                @block.vector
                def _(dve):
                    features_dve(dve, "oa", oT)
                    gated_sum(dve, "ao", "ga", gT, True)

                @block.sync
                def _(sp):
                    load_weights(sp, l, W_GA + RING, W_OG + RING)

            og = carve(0, NT, D)
            logdec = carve(3072, 2, NT, H_B * DK)
            o_b = carve(6144, NT, D)
            soft = carve(6144, 2, NT, H_B * DK)
            sq_b = carve(3072, NT * H_B, DV)
            gla_s = carve(9216, 2, H_B, DV)
            gla_p = carve(11264, 2, H_B, DV)
            clamped = carve(13312, 512)
            up = carve(13824, H_B * DK)
            down = carve(14336, H_B * DK)
            qt = carve(20992, H_B, DK)
            kt = carve(21504, H_B, DK)
            qtT = carve(22016, H_B, P)
            ktT = carve(22528, H_B, P)
            att = carve(23040, H_B, P)
            ecol = carve(23552, 2, H_B, 2)
            stat_b = carve(23568, NT * H_B)
            SCAN = ((0, 0), (1, 0), (0, 1), (1, 2), (0, 2), (1, 1))
            FIRST = (0, 2, 3)
            LAST = (4, 5)
            with nc.Block() as block:
                @block.tensor
                def _(pe):
                    for t in range(NT):
                        for d in range(2):
                            pe.matmul(claim(pe, ("lg", t, d)), lowT[:, tok(t)], wgl[:, d, :], start=True, stop=True).then_inc(*makes(("lg", t, d)))
                    for i in range(2):
                        token_major(pe, W_OG + i, ("og", i))
                    pe.wait_ge(*following(pe, "logdecay_ready"))
                    for s, (d, t) in enumerate(SCAN):
                        pe.matmul(claim(pe, ("b", s)), rel(d), logdec[:, d, t, :], start=True, stop=True).then_inc(*makes(("b", s)))
                        out = claim(pe, ("ec", s))
                        for h in range(H_B):
                            ins = pe.matmul(out[:, 2 * h:2 * h + 2], logdec[:, d, t, DK * h:DK * h + DK],
                                            cst[:, C_SEL:C_SEL + 2], start=True, stop=True)
                        ins.then_inc(*makes(("ec", s)))
                        pe.wait_ge(*following(pe, "qk_ready"))
                        transposed(pe, ("qtT", s), [qt[:, h, :] for h in range(H_B)])
                        transposed(pe, ("ktT", s), [kt[:, h, :] for h in range(H_B)])
                        pe.wait_ge(*read(("qtT", s)))
                        pe.wait_ge(*read(("ktT", s)))
                        out = claim(pe, ("att", s))
                        for h in range(H_B):
                            ins = pe.matmul(out[:, P * h:P * h + P], ktT[:, h, :], qtT[:, h, :], start=True, stop=True)
                        ins.then_inc(*makes(("att", s)))
                        if s not in LAST:
                            for g in range(2):
                                out = claim(pe, ("ds", s, g))
                                for h in (2 * g, 2 * g + 1):
                                    c = DV * (h % 2)
                                    ins = pe.matmul(out[:, c:c + DV], kt[:, h, :], v_b[:, t, h, :], start=True, stop=True)
                                ins.then_inc(*makes(("ds", s, g)))
                        pe.wait_ge(*read(("att", s)))
                        if t:
                            pe.wait_ge(*following(pe, "scaled_state"))
                        for g in range(2):
                            out = claim(pe, ("o", s, g))
                            for h in (2 * g, 2 * g + 1):
                                c = DV * (h % 2)
                                pairs = [(att[:, h, :], v_b[:, t, h, :])]
                                if t:
                                    pairs.append((qtT[:, h, :], gla_s[:, d, h, :]))
                                ins = matmuls(pe, out[:, c:c + DV], pairs)
                            ins.then_inc(*makes(("o", s, g)))

                @block.scalar
                def _(act):
                    for i in range(2):
                        for t in range(NT):
                            act.wait_ge(*made((("og", i), t)))
                            s = bank((("og", i), t))
                            act.activation(og[:, t, 512 * i:512 * i + 512], s, ACT.Silu).then_inc(*reads((("og", i), t)))
                            act.wait_ge(*read((("og", i), t)))
                    act.wait_ge(*following(act, "abs_ready"))
                    act.activation(soft, soft, ACT.Exp, scale=-1.0).then_inc(*counts("act_step"))
                    act.wait_ge(*counted("act_step"))
                    act.activation(soft, soft, ACT.Ln, bias=1.0).then_inc(*counts("soft_ready"))
                    for s in range(len(SCAN)):
                        act.wait_ge(*following(act, "clamped_ready"))
                        act.activation(up, clamped, ACT.Exp).then_inc(*counts("act_step"))
                        act.wait_ge(*counted("act_step"))
                        act.activation(down, clamped, ACT.Exp, scale=-1.0).then_inc(*counts("decay_ready"))
                        act.wait_ge(*made(("ec", s)))
                        act.activation(ecol[:, s % 2, :, :],
                                       bank(("ec", s))[:, 0:2 * H_B].rearrange("p (h e) -> p h e", e=2),
                                       ACT.Exp).then_inc(*reads(("ec", s)))
                        act.wait_ge(*read(("ec", s)))
                        act.wait_ge(*made(("qtT", s)))
                        act.activation(qtT, quad(bank(("qtT", s))), ACT.Copy).then_inc(*reads(("qtT", s)))
                        act.wait_ge(*read(("qtT", s)))
                    act.wait_ge(*following(act, "o_ready"))
                    act.activation(sq_b, o_b.rearrange("p t (h d) -> p (t h) d", d=DV), ACT.Square).then_inc(*counts("sq_ready"))
                    act.wait_ge(*following(act, "stat_ready"))
                    act.activation(stat_b, stat_b, ACT.Sqrt).then_inc(*counts("head_root"))

                @block.gpsimd
                def _(pool):
                    pool.wait_ge(*following(pool, "gla_state_in", 32))
                    for s, (d, t) in enumerate(SCAN):
                        if t:
                            pool.wait_ge(*read(("ec", s)))
                            if s in LAST:
                                pool.wait_ge(*following(pool, "state_ready", 1))
                            ins = pool.tensor_tensor(gla_s[:, d, :, :], gla_s[:, d, :, :],
                                                     over(ecol[:, s % 2, :, d], DV), ALU.mult)
                            ins.then_inc(*counts("scaled_state"))

                @block.vector
                def _(dve):
                    for t in range(NT):
                        for d in range(2):
                            dve.wait_ge(*made(("lg", t, d)))
                            s = bank(("lg", t, d))
                            dve.tensor_copy(logdec[:, d, t, :], s).then_inc(*reads(("lg", t, d)))
                            dve.wait_ge(*read(("lg", t, d)))
                    dve.scalar_tensor_tensor(out=soft, in0=logdec, scalar=-1.0, in1=logdec,
                                             op0=ALU.mult, op1=ALU.max).then_inc(*counts("abs_ready"))
                    dve.wait_ge(*counted("abs_ready"))
                    dve.tensor_scalar(logdec, logdec, 0.0, 1.0 / GATE_NORM, ALU.min, ALU.mult).then_inc(*counts("dve_step"))
                    dve.wait_ge(*counted("dve_step"))
                    dve.wait_ge(*following(dve, "soft_ready"))
                    dve.scalar_tensor_tensor(out=logdec, in0=soft, scalar=-1.0 / GATE_NORM, in1=logdec,
                                             op0=ALU.mult, op1=ALU.add).then_inc(*counts("logdecay_ready"))
                    dve.wait_ge(*counted("logdecay_ready"))
                    for s, (d, t) in enumerate(SCAN):
                        dve.wait_ge(*made(("b", s)))
                        dve.tensor_scalar(clamped, bank(("b", s)), CLAMP, -CLAMP, ALU.min, ALU.max).then_inc(*reads(("b", s)))
                        dve.wait_ge(*read(("b", s)))
                        dve.tensor_copy(stat_b[:, 0:1], cst[:, 0:1]).then_inc(*counts("clamped_ready"))
                        dve.wait_ge(*following(dve, "decay_ready"))
                        dve.tensor_tensor(qt, q_b[:, t, :, :], up.rearrange("p (h d) -> p h d", d=DK), ALU.mult).then_inc(*counts("dve_step"))
                        dve.wait_ge(*counted("dve_step"))
                        dve.tensor_tensor(kt, k_b[:, t, :, :], down.rearrange("p (h d) -> p h d", d=DK), ALU.mult).then_inc(*counts("qk_ready"))
                        dve.wait_ge(*counted("qk_ready"))
                        dve.wait_ge(*made(("ktT", s)))
                        dve.tensor_copy(ktT, quad(bank(("ktT", s)))).then_inc(*reads(("ktT", s)))
                        dve.wait_ge(*read(("ktT", s)))
                        dve.wait_ge(*made(("att", s)))
                        dve.tensor_tensor(att, quad(bank(("att", s))), each(cum(d), H_B), ALU.mult).then_inc(*reads(("att", s)))
                        dve.wait_ge(*read(("att", s)))
                        for g in range(2):
                            out = o_b[:, t, 512 * g:512 * g + 512]
                            dve.wait_ge(*made(("o", s, g)))
                            p = bank(("o", s, g))
                            if s in FIRST:
                                dve.tensor_copy(out, p).then_inc(*reads(("o", s, g)))
                                dve.wait_ge(*read(("o", s, g)))
                            else:
                                dve.tensor_tensor(out, p, out, ALU.add).then_inc(*reads(("o", s, g)))
                                dve.wait_ge(*read(("o", s, g)))
                        if s not in LAST:
                            dve.wait_ge(*read(("ec", s)))
                            for g in range(2):
                                dve.wait_ge(*made(("ds", s, g)))
                                p = bank(("ds", s, g)).rearrange("p (h d) -> p h d", d=DV)
                                e = over(ecol[:, s % 2, 2 * g:2 * g + 2, 1 - d], DV)
                                if t == 0:
                                    dve.tensor_tensor(gla_p[:, d, 2 * g:2 * g + 2, :], p, e, ALU.mult).then_inc(*reads(("ds", s, g)))
                                    dve.wait_ge(*read(("ds", s, g)))
                                else:
                                    st = gla_s[:, d, 2 * g:2 * g + 2, :]
                                    dve.tensor_tensor(st, p, st, ALU.add).then_inc(*reads(("ds", s, g)))
                                    dve.wait_ge(*read(("ds", s, g)))
                                    ins = dve.tensor_tensor(st, st, e, ALU.mult)
                                    if g:
                                        ins.then_inc(*counts("state_ready"))
                                        dve.wait_ge(*counted("state_ready"))
                                    else:
                                        ins.then_inc(*counts("dve_step"))
                                        dve.wait_ge(*counted("dve_step"))
                    dve.tensor_copy(stat_b[:, 0:1], cst[:, 0:1]).then_inc(*counts("o_ready"))
                    dve.wait_ge(*counted("o_ready"))
                    dve.wait_ge(*following(dve, "sq_ready"))
                    dve.tensor_reduce(stat_b, sq_b, AX_X, ALU.add).then_inc(*counts("dve_step"))
                    dve.wait_ge(*counted("dve_step"))
                    dve.tensor_scalar(stat_b, stat_b, 1.0 / DV, EPS, ALU.mult, ALU.add).then_inc(*counts("stat_ready"))
                    dve.wait_ge(*counted("stat_ready"))
                    dve.wait_ge(*following(dve, "head_root"))
                    dve.reciprocal(stat_b, stat_b).then_inc(*counts("dve_step"))
                    dve.wait_ge(*counted("dve_step"))
                    heads = o_b.rearrange("p t (h d) -> p (t h) d", d=DV)
                    dve.tensor_tensor(heads, heads, over(stat_b, DV), ALU.mult).then_inc(*counts("dve_step"))
                    dve.wait_ge(*counted("dve_step"))
                    for i in range(2):
                        for t in range(NT):
                            dve.wait_ge(*read((("og", i), t)))
                    dve.tensor_tensor(o_b, o_b, og, ALU.mult).then_inc(*counts("dve_step"))
                    dve.wait_ge(*counted("dve_step"))

                @block.sync
                def _(sp):
                    for d in range(2):
                        sp.dma_start(gla_s[:, d, :, :], state_gla[bass.ds(l, 1), d].rearrange("a h k v -> k (a h) v")
                                     ).then_inc(sem["gla_state_in"], 16)
                    load_weights(sp, l, W_OG + RING, W_GB + RING)
                    for d in range(2):
                        for g in range(2):
                            sp.wait_ge(*read(("ds", d, g)))
                        sp.dma_start(new_gla[bass.ds(l, 1), d].rearrange("a h k v -> k (a h) v"), gla_p[:, d, :, :]
                                     ).then_inc(sem["stored"], 16)
                    sp.wait_ge(*following(sp, "stored", 32))

            gT_b = carve(0, KD, T)
            oT_b = carve(3072, KD, T)
            with nc.Block() as block:
                @block.tensor
                def _(pe):
                    for i in range(2):
                        feature_major(pe, W_GB + i, ("gb", i), hT)
                    to_features(pe, "ob", o_b)
                    project_pe(pe, W_BO, "bo", oT_b, "ob")

                @block.scalar
                def _(act):
                    gate_act(act, "gb", gT_b)

                @block.vector
                def _(dve):
                    features_dve(dve, "ob", oT_b, V_BON)
                    gated_sum(dve, "bo", "gb", gT_b, False)

                @block.sync
                def _(sp):
                    load_weights(sp, l, W_GB + RING, W_Z + RING)

            z_c = carve(0, NT, D)
            xpad = carve(3072, NX, XW)
            xbc = carve(7776, NX, YW)
            xs = carve(12432, NT, D)
            b_tok = carve(15504, NT, G_C, N_ST)
            y_c = carve(16272, NT, D)
            xdt = carve(19344, H_C, HP)
            xw = carve(20368, H_C, HP)
            diff = carve(21392, 2, 512)
            decayed = carve(22416, H_C, P)
            cbm = carve(24464, G_C, P)
            dt = carve(24720, NT, 32)
            dta = carve(24816, NT, 32)
            dtt = carve(24912, NT, 32)
            aexp = carve(25008, 32)
            ex2 = carve(25040, 2, 4, H_C)
            stat_c = carve(25170, NT)
            ssd_in = carve(3072, 2, KD, P)
            ssd_s = carve(5120, 2, H_C * HP)
            ssd_p = carve(7168, H_C * HP)
            ssd_out = (carve(8192, KD, P), carve(25200, KD, P))
            ssd_tmp = carve(9216, 512)
            OUT_COL = (0, X_S - X_P, X_S - X_P + P)
            with nc.Block() as block:
                @block.tensor
                def _(pe):
                    for i in range(2):
                        token_major(pe, W_Z + i, ("z", i))
                    for i in range(3):
                        feature_major(pe, W_CX + i, ("cx", i), hT)
                    for q in range(2):
                        for j in range(4 * q, 4 * q + 4):
                            pe.wait_ge(*following(pe, "xbc_ready"))
                        for t in range(NT):
                            transposed(pe, ("xs", t, q), [xbc[:, j, OUT_COL[t]:OUT_COL[t] + P] for j in range(4 * q, 4 * q + 4)])
                    for j in range(8, NX):
                        pe.wait_ge(*following(pe, "xbc_ready"))
                    for t in range(NT):
                        transposed(pe, ("bt", t), [xbc[:, 8 + g, OUT_COL[t]:OUT_COL[t] + P] for g in range(G_C)])

                @block.scalar
                def _(act):
                    for i in range(2):
                        for t in range(NT):
                            act.wait_ge(*made((("z", i), t)))
                            s = bank((("z", i), t))
                            act.activation(z_c[:, t, 512 * i:512 * i + 512], s, ACT.Silu).then_inc(*reads((("z", i), t)))
                            act.wait_ge(*read((("z", i), t)))
                    for i in range(3):
                        for j in range(4):
                            act.wait_ge(*made((("cx", i), j)))
                            s = bank((("cx", i), j))
                            act.activation(xpad[:, 4 * i + j, X_P:X_P + P], s[:, 0:P], ACT.Copy).then_inc(*counts("act_step"))
                            act.wait_ge(*counted("act_step"))
                            act.activation(xpad[:, 4 * i + j, X_S:X_S + 2 * P], s[:, P:T], ACT.Copy).then_inc(*reads((("cx", i), j)))
                            act.wait_ge(*read((("cx", i), j)))
                    for j in range(NX):
                        act.wait_ge(*following(act, "conv_ready"))
                        act.activation(xbc[:, j, :], xbc[:, j, :], ACT.Silu, bias=vec[:, V_CB + j:V_CB + j + 1]).then_inc(*counts("xbc_ready"))
                    act.wait_ge(*following(act, "abs_ready"))
                    act.activation(dtt, dtt, ACT.Exp, scale=-1.0).then_inc(*counts("act_step"))
                    act.wait_ge(*counted("act_step"))
                    act.activation(dtt, dtt, ACT.Ln, bias=1.0).then_inc(*counts("act_step"))
                    act.wait_ge(*counted("act_step"))
                    act.activation(aexp, row[:, R_ALOG:R_ALOG + 32], ACT.Exp).then_inc(*counts("soft_ready"))

                @block.vector
                def _(dve):
                    for a, b in ((0, X_P), (X_P + P, X_S), (XW - PAD, XW)):
                        dve.memset(xpad[:, :, a:b], 0.0).then_inc(*counts("dve_step"))
                        dve.wait_ge(*counted("dve_step"))
                    dve.tensor_tensor(dt, dtraw[:, :, :], each(row[:, R_DTB:R_DTB + 32], NT), ALU.add).then_inc(*counts("dve_step"))
                    dve.wait_ge(*counted("dve_step"))
                    dve.scalar_tensor_tensor(out=dtt, in0=dt, scalar=-1.0, in1=dt, op0=ALU.mult, op1=ALU.max).then_inc(*counts("abs_ready"))
                    dve.wait_ge(*counted("abs_ready"))
                    dve.tensor_scalar(dt, dt, 0.0, None, ALU.max).then_inc(*counts("dve_step"))
                    dve.wait_ge(*counted("dve_step"))
                    for j in range(NX):
                        dve.wait_ge(*read((("cx", j // 4), j % 4)))
                        for k in range(TAPS):
                            w = vec[:, V_CW + NX * k + j:V_CW + NX * k + j + 1]
                            src = xpad[:, j, k:k + YW]
                            if k == 0:
                                ins = dve.tensor_scalar(xbc[:, j, :], src, w, None, ALU.mult)
                            else:
                                ins = dve.scalar_tensor_tensor(out=xbc[:, j, :], in0=src, scalar=w, in1=xbc[:, j, :],
                                                               op0=ALU.mult, op1=ALU.add)
                            ins.then_inc(*counts("conv_ready" if k == TAPS - 1 else "dve_step"))
                            dve.wait_ge(*counted("conv_ready" if k == TAPS - 1 else "dve_step"))
                    for q in range(2):
                        for t in range(NT):
                            dve.wait_ge(*made(("xs", t, q)))
                            dve.tensor_copy(xs[:, t, 512 * q:512 * q + 512], bank(("xs", t, q))).then_inc(*reads(("xs", t, q)))
                            dve.wait_ge(*read(("xs", t, q)))
                    for t in range(NT):
                        dve.wait_ge(*made(("bt", t)))
                        dve.tensor_copy(b_tok[:, t, :, :], quad(bank(("bt", t))[:, 0:G_C * P])).then_inc(*reads(("bt", t)))
                        dve.wait_ge(*read(("bt", t)))
                    dve.wait_ge(*following(dve, "soft_ready"))
                    dve.tensor_tensor(dt, dt, dtt, ALU.add).then_inc(*counts("dve_step"))
                    dve.wait_ge(*counted("dve_step"))
                    dve.scalar_tensor_tensor(out=dta, in0=dt, scalar=-1.0, in1=each(aexp, NT),
                                             op0=ALU.mult, op1=ALU.mult).then_inc(*counts("dve_step"))
                    dve.wait_ge(*counted("dve_step"))

                @block.sync
                def _(sp):
                    load_weights(sp, l, W_Z + RING, W_GC + RING)

            with nc.Block() as block:
                @block.tensor
                def _(pe):
                    pe.wait_ge(*following(pe, "ssd_state_in", 32))
                    for d in range(2):
                        for q in range(2):
                            transposed(pe, ("si", d, q), [ssd_in[:, d, 4 * q + i, :] for i in range(4)])
                    for s, (d, t) in enumerate(SCAN):
                        col = slice(OUT_COL[t], OUT_COL[t] + P)
                        a = dta[:, t, H_C * d:H_C * d + H_C]
                        out = claim(pe, ("sc", s))
                        for i, m in enumerate((rel(d), cum(d), aft(d), ones)):
                            ins = pe.matmul(out[:, H_C * i:H_C * i + H_C], m, a, start=True, stop=True)
                        ins.then_inc(*makes(("sc", s)))
                        out = claim(pe, ("cb", s))
                        for g in range(G_C):
                            ins = pe.matmul(out[:, P * g:P * g + P], xbc[:, 8 + g, col], xbc[:, 10 + g, col],
                                            start=True, stop=True)
                        ins.then_inc(*makes(("cb", s)))
                        for q in range(4):
                            out = claim(pe, ("ai", s, q))
                            for i in range(4):
                                h = H_C * d + 4 * q + i
                                ins = pe.matmul(out[:, P * i:P * i + P], dta[:, t, h:h + 1].broadcast_to([P, P]), rel(d),
                                                start=True, stop=True)
                            ins.then_inc(*makes(("ai", s, q)))
                        if t:
                            for g in range(G_C):
                                if s in FIRST:
                                    pe.wait_ge(*read(("si", d, g)))
                                else:
                                    pe.wait_ge(*read(("ds", s - 2, g)))
                                if s not in FIRST and g == 0:
                                    pe.wait_ge(*following(pe, "state_ready"))
                                pe.matmul(claim(pe, ("yo", s, g)), xbc[:, 10 + g, col],
                                          ssd_s[:, d, 512 * g:512 * g + 512], start=True, stop=True).then_inc(*makes(("yo", s, g)))
                        pe.wait_ge(*following(pe, "xw_ready"))
                        if s not in LAST:
                            for g in range(G_C):
                                pe.matmul(claim(pe, ("ds", s, g)), b_tok[:, t, g, :],
                                          xw.rearrange("p h d -> p (h d)")[:, 512 * g:512 * g + 512],
                                          start=True, stop=True).then_inc(*makes(("ds", s, g)))
                        for g in range(G_C):
                            pe.wait_ge(*following(pe, "mask_ready", 2))
                            out = claim(pe, ("yd", s, g))
                            for i in range(8):
                                h = 8 * g + i
                                ins = pe.matmul(out[:, HP * i:HP * i + HP], decayed[:, h, :], xdt[:, h, :],
                                                start=True, stop=True)
                            ins.then_inc(*makes(("yd", s, g)))
                        if t == 0:
                            for g in range(G_C):
                                pe.wait_ge(*read(("ds", s, g)))
                            for q in range(2):
                                transposed(pe, ("so", d, q), [ssd_p[:, 512 * q + P * i:512 * q + P * i + P] for i in range(4)])

                @block.scalar
                def _(act):
                    for s, (d, t) in enumerate(SCAN):
                        act.wait_ge(*made(("sc", s)))
                        p = bank(("sc", s)).rearrange("p (a h) -> p a h", h=H_C)
                        act.activation(ex2[:, s % 2, 0, :], p[:, 0, :], ACT.Copy).then_inc(*counts("act_step"))
                        act.wait_ge(*counted("act_step"))
                        act.activation(ex2[:, s % 2, 1:4, :], p[:, 1:4, :], ACT.Exp).then_inc(*reads(("sc", s)))
                        act.wait_ge(*read(("sc", s)))
                        for q in range(4):
                            act.wait_ge(*following(act, "diff_ready"))
                            act.activation(diff[:, q % 2, :], diff[:, q % 2, :], ACT.Exp).then_inc(*counts("decayed_ready"))
                    for t in range(NT):
                        act.wait_ge(*following(act, "y_ready"))
                        act.activation(xs[:, t, :], y_c[:, t, :], ACT.Square, accum_out=stat_c[:, t:t + 1]).then_inc(*counts("sq_ready"))
                    act.wait_ge(*following(act, "stat_ready"))
                    act.activation(stat_c, stat_c, ACT.Sqrt).then_inc(*counts("head_root"))

                @block.gpsimd
                def _(pool):
                    for t in range(NT):
                        ins = pool.tensor_tensor(y_c[:, t, :].rearrange("p (h d) -> p h d", d=HP),
                                                 xs[:, t, :].rearrange("p (h d) -> p h d", d=HP),
                                                 over(row[:, R_D:R_D + H_C], HP), ALU.mult)
                    ins.then_inc(*counts("yoff_ready"))
                    for s, (d, t) in enumerate(SCAN):
                        pool.wait_ge(*read(("sc", s)))
                        if s:
                            pool.wait_ge(*made(("yd", s - 1, 1)))
                        pool.tensor_tensor(xdt, xs[:, t, :].rearrange("p (h d) -> p h d", d=HP),
                                            over(dt[:, t, H_C * d:H_C * d + H_C], HP), ALU.mult).then_inc(*counts("pool_step"))
                        pool.wait_ge(*counted("pool_step"))
                        pool.tensor_tensor(xw, xdt, over(ex2[:, s % 2, 2, :], HP), ALU.mult).then_inc(*counts("xw_ready"))

                @block.vector
                def _(dve):
                    dve.wait_ge(*following(dve, "yoff_ready"))
                    for d in range(2):
                        for q in range(2):
                            dve.wait_ge(*made(("si", d, q)))
                            dve.tensor_copy(ssd_s[:, d, 512 * q:512 * q + 512], bank(("si", d, q))).then_inc(*reads(("si", d, q)))
                            dve.wait_ge(*read(("si", d, q)))
                    for s, (d, t) in enumerate(SCAN):
                        dve.wait_ge(*made(("cb", s)))
                        dve.tensor_tensor(cbm, quad(bank(("cb", s))[:, 0:G_C * P]), each(cum(d), G_C), ALU.mult).then_inc(*reads(("cb", s)))
                        dve.wait_ge(*read(("cb", s)))
                        dve.wait_ge(*read(("sc", s)))
                        for q in range(5):
                            if q < 4:
                                dve.wait_ge(*made(("ai", s, q)))
                                dve.tensor_tensor(quad(diff[:, q % 2, :]), quad(bank(("ai", s, q))),
                                                  over(ex2[:, s % 2, 0, 4 * q:4 * q + 4], P), ALU.subtract).then_inc(*reads(("ai", s, q)))
                                dve.wait_ge(*read(("ai", s, q)))
                                dve.tensor_scalar(diff[:, q % 2, :], diff[:, q % 2, :], 0.0, None, ALU.min).then_inc(*counts("diff_ready"))
                            if q:
                                r = q - 1
                                dve.wait_ge(*following(dve, "decayed_ready"))
                                dve.tensor_tensor(decayed[:, 4 * r:4 * r + 4, :], quad(diff[:, r % 2, :]),
                                                  each(cbm[:, r // 2, :], 4), ALU.mult).then_inc(*counts("mask_ready"))
                                dve.wait_ge(*counted("mask_ready"))
                        for g in range(G_C):
                            out = y_c[:, t, 512 * g:512 * g + 512]
                            if t:
                                dve.wait_ge(*made(("yo", s, g)))
                                dve.tensor_tensor(ssd_tmp.rearrange("p (h d) -> p h d", d=HP),
                                                  bank(("yo", s, g)).rearrange("p (h d) -> p h d", d=HP),
                                                  over(ex2[:, s % 2, 1, 8 * g:8 * g + 8], HP), ALU.mult).then_inc(*counts("dve_step"))
                                dve.wait_ge(*counted("dve_step"))
                                dve.tensor_tensor(out, ssd_tmp, out, ALU.add).then_inc(*reads(("yo", s, g)))
                                dve.wait_ge(*read(("yo", s, g)))
                            dve.wait_ge(*made(("yd", s, g)))
                            dve.tensor_tensor(out, bank(("yd", s, g)), out, ALU.add).then_inc(*reads(("yd", s, g)))
                            dve.wait_ge(*read(("yd", s, g)))
                        if s not in LAST:
                            for g in range(G_C):
                                dve.wait_ge(*made(("ds", s, g)))
                                p = bank(("ds", s, g))
                                if t == 0:
                                    dve.tensor_copy(ssd_p[:, 512 * g:512 * g + 512], p).then_inc(*reads(("ds", s, g)))
                                    dve.wait_ge(*read(("ds", s, g)))
                                else:
                                    st = ssd_s[:, d, 512 * g:512 * g + 512]
                                    sv = st.rearrange("p (h d) -> p h d", d=HP)
                                    dve.tensor_tensor(sv, sv, over(ex2[:, s % 2, 3, 8 * g:8 * g + 8], HP), ALU.mult).then_inc(*counts("dve_step"))
                                    dve.wait_ge(*counted("dve_step"))
                                    dve.tensor_tensor(st, p, st, ALU.add).then_inc(*reads(("ds", s, g)))
                                    dve.wait_ge(*read(("ds", s, g)))
                            if t:
                                dve.tensor_copy(stat_c[:, 0:1], cst[:, 0:1]).then_inc(*counts("state_ready"))
                                dve.wait_ge(*counted("state_ready"))
                        if t == 0:
                            for q in range(2):
                                dve.wait_ge(*made(("so", d, q)))
                                dve.tensor_copy(ssd_out[d][:, 4 * q:4 * q + 4, :], quad(bank(("so", d, q)))).then_inc(*reads(("so", d, q)))
                                dve.wait_ge(*read(("so", d, q)))
                    for t in range(NT):
                        dve.tensor_tensor(y_c[:, t, :], y_c[:, t, :], z_c[:, t, :], ALU.mult).then_inc(*counts("y_ready"))
                        dve.wait_ge(*counted("y_ready"))
                    for t in range(NT):
                        dve.wait_ge(*following(dve, "sq_ready"))
                    dve.tensor_scalar(stat_c, stat_c, 1.0 / D, EPS, ALU.mult, ALU.add).then_inc(*counts("stat_ready"))
                    dve.wait_ge(*counted("stat_ready"))
                    dve.wait_ge(*following(dve, "head_root"))
                    dve.reciprocal(stat_c, stat_c).then_inc(*counts("dve_step"))
                    dve.wait_ge(*counted("dve_step"))
                    for t in range(NT):
                        dve.tensor_scalar(y_c[:, t, :], y_c[:, t, :], stat_c[:, t:t + 1], None, ALU.mult).then_inc(*counts("dve_step"))
                        dve.wait_ge(*counted("dve_step"))

                @block.sync
                def _(sp):
                    for d in range(2):
                        sp.dma_start(ssd_in[:, d, :, :], state_ssd[bass.ds(l, 1), d].rearrange("a (j q) n -> q (a j) n", q=P)
                                     ).then_inc(sem["ssd_state_in"], 16)
                    for d in range(2):
                        for q in range(2):
                            sp.wait_ge(*read(("so", d, q)))
                        sp.dma_start(new_ssd[bass.ds(l, 1), d].rearrange("a (j q) n -> q (a j) n", q=P), ssd_out[d]
                                     ).then_inc(sem["stored"], 16)
                    sp.wait_ge(*following(sp, "stored", 32))

            gT_c = carve(0, KD, T)
            oT_c = carve(3072, KD, T)
            with nc.Block() as block:
                @block.tensor
                def _(pe):
                    for i in range(2):
                        feature_major(pe, W_GC + i, ("gc", i), hT)
                    to_features(pe, "oc", y_c)
                    project_pe(pe, W_CO, "co", oT_c, "oc")
                    pe.wait_ge(*following(pe, "merged_ready"))
                    for i in range(2):
                        feature_major(pe, W_OUT + i, ("out", i), mT)

                @block.scalar
                def _(act):
                    gate_act(act, "gc", gT_c)

                @block.vector
                def _(dve):
                    features_dve(dve, "oc", oT_c, V_CN)
                    gated_sum(dve, "co", "gc", gT_c, False)
                    dve.tensor_copy(stat_c[:, 0:1], cst[:, 0:1]).then_inc(*counts("merged_ready"))
                    dve.wait_ge(*counted("merged_ready"))
                    for i in range(2):
                        for j in range(4):
                            dve.wait_ge(*made((("out", i), j)))
                            s = bank((("out", i), j))
                            k = 4 * i + j
                            for ts, c in COND:
                                ins = dve.scalar_tensor_tensor(out=xT[:, k, ts], in0=s[:, ts], scalar=mod[:, 2, k, c:c + 1],
                                                               in1=xT[:, k, ts], op0=ALU.mult, op1=ALU.add)
                                if c == 0:
                                    ins.then_inc(*counts("dve_step"))
                                    dve.wait_ge(*counted("dve_step"))
                            ins.then_inc(*reads((("out", i), j)))
                            dve.wait_ge(*read((("out", i), j)))

                @block.sync
                def _(sp):
                    load_weights(sp, l, W_GC + RING, W_MOE + RING)

            outs = carve(0, NE, D)
            spread = carve(16384, NE + 1, T)
            hc = carve(22912, KD, SLOTS)
            hidden = carve(23680, DE // P, SLOTS)
            silc = carve(24064, DE // P, SLOTS)
            pick = carve(24448, NT, SLOTS)
            pick_w = carve(24736, NT, SLOTS)
            h_tok = mT[:, :, :].rearrange("p k t -> p (k t)").rearrange("p (t d) -> p t d", d=D)
            score = carve(25600, NT, NE)
            sel = carve(25648, NT, NE)
            pairs6 = carve(25696, NT * NG, 6)
            gsum = carve(25768, NT, NG)
            gmax = carve(25780, NT)
            genc = carve(25784, NT, NG)
            gone = carve(25796, NT, NG)
            enc = carve(25808, NT, NE)
            one = carve(25856, NT, NE)
            chosen = carve(25904, NT, NE)
            gate = carve(25952, NT, NE + 2)
            place = carve(26008, NT, NE + 2)
            load = carve(26064, NE)
            gate_over = carve(26088, NT, NE)
            B_PICK, B_GATH, B_W1, B_W3, B_W2 = 0, 1, 3, 4, 5
            with nc.Block() as block:
                base = {}

                @block.tensor
                def _(pe):
                    square_sum(pe, "n2", sq_x, KD)
                    pe.wait_ge(*following(pe, "h_ready"))
                    out = claim(pe, "route")
                    for t in range(NT):
                        ins = matmuls(pe, out[:, NE * t:NE * t + NE], [(hT[:, k, tok(t)], rw[:, k, :]) for k in range(KD)])
                    ins.then_inc(*makes("route"))
                    for t in range(NT):
                        for q in range(2):
                            transposed(pe, ("ht", t, q), [hT[:, 4 * q + i, tok(t)] for i in range(4)])
                    pe.wait_ge(*following(pe, "chosen_ready"))
                    out = claim(pe, "place")
                    for t in range(NT):
                        matmuls(pe, out[:, NE * t:NE * t + NE], [(ones, chosen[:, u, :]) for u in range(t)]
                                + [(aft(1), chosen[:, t, :])])
                    ins = matmuls(pe, out[:, NE * NT:NE * NT + NE], [(ones, chosen[:, u, :]) for u in range(NT)])
                    ins.then_inc(*makes("place"))
                    base.update({b: uses[b] for b in range(8)})

                    def gather(e):
                        pe.wait_ge(sem["picked"], e + 1)
                        pe.wait_ge(psum_free[B_PICK], e + base[B_PICK])
                        for t in range(NT):
                            ins = pe.transpose(ps[0:SLOTS, B_PICK, tok(t)], pick_w[:, t, :], ident)
                        ins.then_inc(psum_full[B_PICK], 1)
                        for g in range(2):
                            pe.wait_ge(psum_free[B_GATH + g], e + base[B_GATH + g])
                            for i in range(4):
                                d = 4 * g + i
                                ins = matmuls(pe, ps[:, B_GATH + g, SLOTS * i:SLOTS * i + SLOTS],
                                              [(h_tok[:, t, P * d:P * d + P], pick[:, t, :]) for t in range(NT)])
                            ins.then_inc(psum_full[B_GATH + g], 1)

                    gather(0)
                    with pe.Fori(0, NE) as e:
                        pe.wait_ge(psum_free[B_GATH + 1], e + (base[B_GATH + 1] + 1))
                        for i, b in ((0, B_W1), (1, B_W3)):
                            pe.wait_ge(w_loaded[i], e * 16 + 16 * (W_MOE // RING + 1))
                            pe.wait_ge(psum_free[b], e + base[b])
                            w = chunk(i, KD, DE)
                            for f in range(DE // P):
                                ins = matmuls(pe, ps[:, b, SLOTS * f:SLOTS * f + SLOTS],
                                              [(w[:, k, P * f:P * f + P], hc[:, k, :]) for k in range(KD)])
                            ins.then_inc(psum_full[b], 1)
                        gather(e + 1)
                        w2 = chunk(2, DE // P, D)
                        pe.wait_ge(w_loaded[2], e * 16 + 16 * (W_MOE // RING + 1))
                        pe.wait_ge(psum_free[B_W3], e + (base[B_W3] + 1))
                        for g in range(2):
                            pe.wait_ge(psum_free[B_W2 + g], e + base[B_W2 + g])
                            matmuls(pe, ps[0:SLOTS, B_W2 + g, :], [(hidden[:, k, :], w2[:, k, 512 * g:512 * g + 512])
                                                                   for k in range(DE // P)]).then_inc(psum_full[B_W2 + g], 1)
                    for b, n in ((B_PICK, NE + 1), (B_GATH, NE + 1), (B_GATH + 1, NE + 1), (B_W1, NE), (B_W3, NE),
                                 (B_W2, NE), (B_W2 + 1, NE)):
                        uses[b] += n
                    for b in (B_PICK, B_W2, B_W2 + 1):
                        pe.wait_ge(psum_free[b], uses[b])
                    for d in range(KD):
                        ins = matmuls(pe, claim(pe, ("moe", d))[:, 0:T],
                                      [(outs[0:SLOTS, e, P * d:P * d + P], spread[0:SLOTS, e, :]) for e in range(NE)])
                        ins.then_inc(*makes(("moe", d)))

                @block.sync
                def _(sp):
                    with sp.Fori(1, NE) as e:
                        for i, b in ((0, B_W1), (1, B_W3), (2, B_W2 + 1)):
                            sp.wait_ge(psum_full[b], e + base[b])
                            src, k, w = expert_source(i, l, e)
                            sp.dma_start(chunk(i, k, w), src).then_inc(w_loaded[i], 16)

                @block.scalar
                def _(act):
                    norm_act(act, 1, "n2", sq_x)
                    act.wait_ge(*made("route"))
                    act.activation(score, bank("route")[:, 0:NT * NE].rearrange("p (t e) -> p t e", e=NE),
                                   ACT.Sigmoid).then_inc(*reads("route"))
                    for t in range(NT):
                        for q in range(2):
                            act.wait_ge(*made(("ht", t, q)))
                            act.activation(h_tok[:, t, 512 * q:512 * q + 512], bank(("ht", t, q)),
                                           ACT.Copy).then_inc(*reads(("ht", t, q)))
                            act.wait_ge(*read(("ht", t, q)))
                    with act.Fori(0, NE) as e:
                        act.wait_ge(psum_full[B_W1], e + (base[B_W1] + 1))
                        act.activation(silc, ps[:, B_W1, 0:DE // P * SLOTS].rearrange("p (f s) -> p f s", s=SLOTS),
                                       ACT.Silu).then_inc(psum_free[B_W1], 1)
                        for g in range(2):
                            act.wait_ge(psum_full[B_W2 + g], e + (base[B_W2 + g] + 1))
                            act.activation(outs[0:SLOTS, bass.ds(e, 1), 512 * g:512 * g + 512].rearrange("s a n -> s (a n)"),
                                           ps[0:SLOTS, B_W2 + g, :], ACT.Copy).then_inc(psum_free[B_W2 + g], 1)

                @block.vector
                def _(dve):
                    norm_dve(dve, "n2")
                    dve.wait_ge(*read("route"))

                    def step(ins):
                        ins.then_inc(*counts("dve_step"))
                        dve.wait_ge(*counted("dve_step"))

                    flat = sel.rearrange("p t (g e) -> p (t g) e", e=EG)
                    step(dve.tensor_tensor(sel, score, each(row[:, R_RB:R_RB + NE], NT), ALU.add))
                    for c, a, b, w in ((0, 0, 2, 2), (2, 0, 3, 1), (3, 1, 2, 1), (4, 0, 1, 1), (5, 2, 3, 1)):
                        step(dve.tensor_tensor(pairs6[:, :, c:c + w], flat[:, :, a:a + w], flat[:, :, b:b + w], ALU.add))
                    step(dve.tensor_reduce(gsum.rearrange("p t g -> p (t g)"), pairs6, AX_X, ALU.max))

                    def first_max(x, n, e, o):
                        rank = each(cst[:, C_RANK:C_RANK + n], NT)
                        step(dve.tensor_reduce(gmax, x, AX_X, ALU.max))
                        step(dve.tensor_tensor(e, x, over(gmax, n), ALU.is_ge))
                        step(dve.tensor_tensor(e, e, rank, ALU.mult))
                        step(dve.tensor_reduce(gmax, e, AX_X, ALU.max))
                        step(dve.tensor_tensor(o, e, over(gmax, n), ALU.is_equal))

                    first_max(gsum, NG, genc, gone)
                    inside = gone.rearrange("p t g -> p (t g)")
                    step(dve.tensor_tensor(flat, flat, over(inside, EG), ALU.mult))
                    step(dve.tensor_scalar(genc, gone, -1.0, BIG, ALU.add, ALU.mult))
                    step(dve.tensor_tensor(flat, flat, over(genc.rearrange("p t g -> p (t g)"), EG), ALU.add))
                    first_max(sel, NE, enc, chosen)
                    step(dve.scalar_tensor_tensor(out=sel, in0=chosen, scalar=-2.0 * BIG, in1=sel, op0=ALU.mult, op1=ALU.add))
                    first_max(sel, NE, enc, one)
                    dve.tensor_tensor(chosen, chosen, one, ALU.add).then_inc(*counts("chosen_ready"))
                    dve.wait_ge(*counted("chosen_ready"))
                    g = gate[:, :, 0:NE]
                    step(dve.tensor_tensor(g, score, chosen, ALU.mult))
                    step(dve.tensor_reduce(gmax, g, AX_X, ALU.add))
                    step(dve.reciprocal(gmax, gmax))
                    step(dve.tensor_tensor(g, g, over(gmax, NE), ALU.mult))
                    step(dve.memset(gate[:, :, NE:], 0.0))
                    dve.wait_ge(*made("place"))
                    p = bank("place")
                    step(dve.memset(place[:, :, NE:], -1.0))
                    step(dve.scalar_tensor_tensor(out=place[:, :, 0:NE], in0=p[:, 0:NT * NE].rearrange("p (t e) -> p t e", e=NE),
                                                  scalar=1.0, in1=chosen, op0=ALU.add, op1=ALU.mult))
                    dve.tensor_copy(load, p[:, NT * NE:NT * NE + NE]).then_inc(*reads("place"))
                    dve.wait_ge(*read("place"))
                    step(dve.tensor_scalar(place[:, :, 0:NE], place[:, :, 0:NE], -1.0, None, ALU.add))
                    step(dve.scalar_tensor_tensor(out=gate_over, in0=place[:, :, 0:NE], scalar=float(SLOTS), in1=g,
                                                  op0=ALU.is_ge, op1=ALU.mult))
                    step(dve.tensor_reduce(gmax[:, 0:1], load, AX_X, ALU.max))
                    step(dve.tensor_scalar(gmax[:, 1:2], gmax[:, 0:1], float(SLOTS), None, ALU.is_gt))
                    step(dve.tensor_copy(overflow[:, :], gmax[0:1, 1:2]))

                    def choose(e):
                        iota = cst[:, C_IOTA:C_IOTA + SLOTS]
                        for t in range(NT):
                            at = place[:, t, bass.ds(e, 1)]
                            dve.tensor_scalar(pick[:, t, :], iota, at, None, ALU.is_equal)
                            ins = dve.tensor_scalar(pick_w[:, t, :], iota, at, gate[:, t, bass.ds(e, 1)],
                                                    ALU.is_equal, ALU.mult)
                        ins.then_inc(sem["picked"], 1)

                    def gathered(e):
                        dve.wait_ge(psum_full[B_PICK], e + (base[B_PICK] + 1))
                        dve.tensor_copy(spread[0:SLOTS, bass.ds(e, 1), :].rearrange("s a n -> s (a n)"),
                                        ps[0:SLOTS, B_PICK, 0:T]).then_inc(psum_free[B_PICK], 1)
                        for g in range(2):
                            dve.wait_ge(psum_full[B_GATH + g], e + (base[B_GATH + g] + 1))
                            dve.tensor_copy(hc[:, 4 * g:4 * g + 4, :],
                                            ps[:, B_GATH + g, 0:4 * SLOTS].rearrange("p (d s) -> p d s", s=SLOTS)
                                            ).then_inc(psum_free[B_GATH + g], 1)

                    dve.wait_ge(*read(("ht", NT - 1, 1)))
                    choose(0)
                    gathered(0)
                    choose(1)
                    with dve.Fori(0, NE) as e:
                        dve.wait_ge(psum_full[B_W3], e + (base[B_W3] + 1))
                        dve.wait_ge(psum_free[B_W1], e + (base[B_W1] + 1))
                        dve.tensor_tensor(hidden, ps[:, B_W3, 0:DE // P * SLOTS].rearrange("p (f s) -> p f s", s=SLOTS),
                                          silc, ALU.mult).then_inc(psum_free[B_W3], 1)
                        gathered(e + 1)
                        choose(e + 2)
                    for d in range(KD):
                        dve.wait_ge(*made(("moe", d)))
                        s = bank(("moe", d))
                        for ts, c in COND:
                            ins = dve.scalar_tensor_tensor(out=xT[:, d, ts], in0=s[:, ts], scalar=mod[:, 5, d, c:c + 1],
                                                           in1=xT[:, d, ts], op0=ALU.mult, op1=ALU.add)
                        ins.then_inc(*reads(("moe", d)))
                        dve.wait_ge(*read(("moe", d)))

            clear_counts()

            acc = carve(0, NT, D)
            hid = carve(3072, DE // P, T)
            sil = carve(4608, DE // P, T)
            moved = carve(6600, 512)
            B_HID, B_OUT, N_OUT = 0, 4, 3
            BANKS = B_OUT + N_OUT
            with nc.Block() as block:
                @block.tensor
                def _(pe):
                    with pe.If(pe.value_load(overflow[0:1, 0:1], min_val=0, max_val=1) > 0):
                        for b in range(BANKS):
                            claim(pe, ("first", b), b)
                            pe.matmul(ps[0:2, b, 0:2], ident[:, 0:2], ident[:, 0:2], start=True, stop=True
                                      ).then_inc(*makes(("first", b)))
                        with pe.Fori(0, NE) as e:
                            def slot(i):
                                pe.wait_ge(w_loaded[i], e * 16 + 16)
                                k = (KD, KD, DE // P)[i]
                                return chunk(i, k, 4096 // k)

                            w1 = slot(0)
                            w3 = slot(1)
                            for f in range(DE // P):
                                for i, w in ((0, w1), (1, w3)):
                                    b = B_HID + 2 * (f % 2) + i
                                    pe.wait_ge(psum_free[b], e * 2 + (1 + f // 2))
                                    matmuls(pe, ps[:, b, 0:T], [(w[:, k, P * f:P * f + P], hT[:, k, :]) for k in range(KD)]
                                            ).then_inc(psum_full[b], 1)
                            w2 = slot(2)
                            pe.wait_ge(sem["hidden_ready"], e * 4 + 4)
                            for n in range(2 * NT):
                                b = B_OUT + n % N_OUT
                                pe.wait_ge(psum_free[b], e * 2 + (1 + n // N_OUT))
                                matmuls(pe, ps[:, b, :], [(hid[:, k, tok(n // 2)], w2[:, k, 512 * (n % 2):512 * (n % 2) + 512])
                                                          for k in range(DE // P)]).then_inc(psum_full[b], 1)
                        for b in range(BANKS):
                            uses[b] += 2 * NE
                        pe.wait_ge(*following(pe, "moe_ready"))
                        to_features(pe, "mo", acc)

                @block.sync
                def _(sp):
                    with sp.If(sp.value_load(overflow[0:1, 0:1], min_val=0, max_val=1) > 0):
                        for i in range(3):
                            src, k, w = expert_source(i, l, 0)
                            sp.dma_start(chunk(i, k, w), src).then_inc(w_loaded[i], 16)
                        with sp.Fori(1, NE) as e:
                            for i, b in enumerate((B_HID + 2, B_HID + 3, B_OUT + N_OUT - 1)):
                                sp.wait_ge(psum_full[b], e * 2 + 1)
                                src, k, w = expert_source(i, l, e)
                                sp.dma_start(chunk(i, k, w), src).then_inc(w_loaded[i], 16)

                @block.scalar
                def _(act):
                    with act.If(act.value_load(overflow[0:1, 0:1], min_val=0, max_val=1) > 0):
                        with act.Fori(0, NE) as e:
                            for f in range(DE // P):
                                b = B_HID + 2 * (f % 2)
                                act.wait_ge(psum_full[b], e * 2 + (1 + f // 2 + 1))
                                act.activation(sil[:, f, :], ps[:, b, 0:T], ACT.Silu).then_inc(psum_free[b], 1)

                @block.vector
                def _(dve):
                    with dve.If(dve.value_load(overflow[0:1, 0:1], min_val=0, max_val=1) > 0):
                        for b in range(BANKS):
                            dve.wait_ge(*made(("first", b)))
                            dve.tensor_copy(moved[0:2, 0:2], ps[0:2, b, 0:2]).then_inc(*reads(("first", b)))
                            dve.wait_ge(*read(("first", b)))
                        dve.memset(acc, 0.0).then_inc(*counts("dve_step"))
                        dve.wait_ge(*counted("dve_step"))
                        with dve.Fori(0, NE) as e:
                            for f in range(DE // P):
                                a = B_HID + 2 * (f % 2)
                                dve.wait_ge(psum_full[a + 1], e * 2 + (1 + f // 2 + 1))
                                dve.wait_ge(psum_free[a], e * 2 + (1 + f // 2 + 1))
                                dve.tensor_tensor(hid[:, f, :], ps[:, a + 1, 0:T], sil[:, f, :], ALU.mult
                                                  ).then_inc(sem["hidden_ready"], 1)
                                dve.wait_ge(sem["hidden_ready"], e * 4 + (f + 1))
                                dve.tensor_copy(moved[:, 0:1], cst[:, 0:1]).then_inc(psum_free[a + 1], 1)
                            for n in range(2 * NT):
                                b = B_OUT + n % N_OUT
                                t = n // 2
                                out = acc[:, t, 512 * (n % 2):512 * (n % 2) + 512]
                                dve.wait_ge(psum_full[b], e * 2 + (1 + n // N_OUT + 1))
                                dve.scalar_tensor_tensor(out=out, in0=ps[:, b, :], scalar=gate_over[:, t, bass.ds(e, 1)],
                                                         in1=out, op0=ALU.mult, op1=ALU.add).then_inc(psum_free[b], 1)
                                dve.wait_ge(psum_free[b], e * 2 + (1 + n // N_OUT + 1))
                        dve.tensor_copy(moved[:, 0:1], cst[:, 0:1]).then_inc(*counts("moe_ready"))
                        dve.wait_ge(*counted("moe_ready"))
                        for t in range(NT):
                            c = 0 if t == 0 else 1
                            for q in range(2):
                                dve.wait_ge(*made(("mo", t, q)))
                                s = quad(bank(("mo", t, q)))
                                dve.tensor_tensor(quad(moved), s, over(mod[:, 5, 4 * q:4 * q + 4, c], P), ALU.mult
                                                  ).then_inc(*reads(("mo", t, q)))
                                dve.wait_ge(*read(("mo", t, q)))
                                out = xT[:, 4 * q:4 * q + 4, tok(t)]
                                dve.tensor_tensor(out, out, quad(moved), ALU.add).then_inc(*counts("dve_step"))
                                dve.wait_ge(*counted("dve_step"))

            clear_counts()

        y_out = carve(0, NT, D)
        with nc.Block() as block:
            @block.tensor
            def _(pe):
                for t in range(NT):
                    for q in range(2):
                        transposed(pe, ("y", t, q), [xT[:, 4 * q + i, tok(t)] for i in range(4)])

            @block.vector
            def _(dve):
                for t in range(NT):
                    for q in range(2):
                        dve.wait_ge(*made(("y", t, q)))
                        dve.tensor_copy(y_out[:, t, 512 * q:512 * q + 512], bank(("y", t, q))).then_inc(*reads(("y", t, q)))
                        dve.wait_ge(*read(("y", t, q)))

            @block.sync
            def _(sp):
                for t in range(NT):
                    for q in range(2):
                        sp.wait_ge(*read(("y", t, q)))
                sp.dma_start(y.rearrange("(t p) d -> p t d", p=P), y_out).then_inc(sem["stored"], 16)
                sp.wait_ge(sem["stored"], 16)


_OUTS = [(NT * P, D), (DEPTH, P, KVL), (DEPTH, P, ROPE), (DEPTH, 2, H_B, DK, DV), (DEPTH, 2, H_C * HP, N_ST)]


def _constants():
    import numpy as np
    s, i = np.arange(P)[:, None], np.arange(P)[None, :]
    half = P // 2
    f = np.float32
    c = np.zeros((P, N_CONST), f)
    c[:, C_ID:C_ID + P] = s == i
    c[:, C_REL:C_REL + P] = (s <= i).astype(f) - (s < half).astype(f)
    c[:, C_REL + P:C_REL + 2 * P] = (s >= i).astype(f) - (s >= half).astype(f)
    c[:, C_CUM:C_CUM + P] = s <= i
    c[:, C_CUM + P:C_CUM + 2 * P] = s >= i
    c[:, C_AFT:C_AFT + P] = s > i
    c[:, C_AFT + P:C_AFT + 2 * P] = s < i
    c[:, C_ONE:C_ONE + P] = 1
    c[:, C_SEL] = (s < half)[:, 0]
    c[:, C_SEL + 1] = (s >= half)[:, 0]
    grid_w, n_freq = 64, ROPE // 4
    tok = np.arange(2 * P)
    inv = (1.0 / (np.float32(10000.0) ** (np.arange(n_freq, dtype=f) / f(n_freq)))).astype(f)
    ang = np.concatenate([(tok // grid_w).astype(f)[:, None] * inv, (tok % grid_w).astype(f)[:, None] * inv], 1)
    for t in range(2):
        c[:, C_COS + 16 * t:C_COS + 16 * t + 16] = np.cos(ang[P * t:P * t + P])
        c[:, C_SIN + 16 * t:C_SIN + 16 * t + 16] = np.sin(ang[P * t:P * t + P])
    c[:, C_RANK:C_RANK + 16] = 16 - np.arange(16)
    c[:, C_IOTA:C_IOTA + SLOTS] = np.arange(SLOTS)
    return c


def kernel(**inputs):
    import numpy as np
    import concourse.bacc as _bacc
    from concourse import mybir as _mybir
    from concourse.bass_utils import run_bass_kernel_spmd as _run

    a = {k: np.asarray(v) for k, v in inputs.items()}
    f = np.float32

    def features(v):
        return v.reshape(DEPTH, -1, P).transpose(0, 2, 1)

    def rows_of(v):
        return np.broadcast_to(v.reshape(DEPTH, 1, -1), (DEPTH, P, v[0].size))

    w_in = a['w_in']
    gates = np.zeros((DEPTH, 2 * RANK + 1, 2, H_B * DK), f)
    for d in range(2):
        gates[:, RANK * d:RANK * d + RANK, d] = a['b_wg'][:, d]
        gates[:, 2 * RANK, d] = a['b_bg'][:, d]
    vecs = np.concatenate(
        [features(a[n]) for n in ('norm1', 'norm2', 'b_ada', 'a_q_norm', 'a_kv_norm', 'c_norm')]
        + [features(np.tile(a['b_onorm'], (1, H_B))),
           a['c_conv_w'].reshape(DEPTH, TAPS * NX, P).transpose(0, 2, 1), features(a['c_conv_b'])], axis=2)
    rows = np.concatenate(
        [rows_of(a[n]) for n in ('a_qk_qnorm', 'a_qk_knorm', 'c_dt_bias', 'c_A_log', 'c_D')]
        + [np.broadcast_to(a['router_bias'], (DEPTH, P, NE))], axis=2)
    named = [
        ('x', np.concatenate([a['x_prompt'][0], a['x_sample'][0]], 0)),
        ('cond', np.stack([a['c_ctx'], a['c'][0]], 0).reshape(2, KD, P).transpose(2, 1, 0)),
        ('consts', _constants()), ('vecs', vecs), ('rows', rows),
        ('w_small', np.concatenate([w_in[:, :, KROPE:KROPE + ROPE], w_in[:, :, DTC:DTC + 32],
                                    w_in[:, :, GLOW:GLOW + 32]], 2)),
        ('w_gate_low', gates), ('router_w', a['router_w']), ('cache_ckv', a['cache_ckv'][0]),
        ('cache_krope', a['cache_krope'][0]), ('state_gla', a['state_gla'][0]),
        ('state_ssd', a['state_ssd'][0].reshape(DEPTH, 2, H_C * HP, N_ST)),
        ('w_ada', a['w_ada']), ('w_in', w_in), ('a_wq', a['a_wq']), ('a_wkv', a['a_wkv']), ('a_wo', a['a_wo']),
        ('b_wo', a['b_wo']), ('c_wo', a['c_wo']), ('w_out', a['w_out']),
        ('e_w1', a['e_w1'].reshape(DEPTH * NE, D, DE)), ('e_w3', a['e_w3'].reshape(DEPTH * NE, D, DE)),
        ('e_w2', a['e_w2'].reshape(DEPTH * NE, DE, D))]
    nc = _bacc.Bacc("TRN2", target_bir_lowering=False, num_devices=1)
    arrays, args = {}, []
    for name, v in named:
        v = np.ascontiguousarray(v)
        arrays[f"in_{name}"] = v
        args.append(nc.dram_tensor(f"in_{name}", v.shape, _mybir.dt.from_np(v.dtype), kind="ExternalInput").ap())
    for i, shape in enumerate(_OUTS):
        args.append(nc.dram_tensor(f"out_{i}", shape, _mybir.dt.from_np(np.dtype(f)), kind="ExternalOutput").ap())
    trunk_kernel(nc, *args)
    r = _run(nc, [arrays], core_ids=[0]).results[0]
    o = [r[f"out_{i}"] for i in range(len(_OUTS))]
    return (o[0][0:P][None], o[0][P:][None], o[1][None], o[2][None], o[3][None],
            o[4].reshape(1, DEPTH, 2, H_C, HP, N_ST))
```

```python
from contextlib import ExitStack

import concourse.bass as bass
from concourse import mybir

F32 = mybir.dt.float32
ALU = mybir.AluOpType
ACT = mybir.ActivationFunctionType
AX_X = mybir.AxisListType.X

P = 128
D = 1024
DEPTH = 2
NT = 3
T = NT * P
KD = D // P
EPS = 1e-6
H_A, NOPE, ROPE, V_A = 16, 64, 32, 64
QK = NOPE + ROPE
QL, KVL = 512, 256
NKT = NT + 1
H_B, DK, DV = 4, 128, 256
RANK = 16
GATE_NORM = 16.0
H_C, HP, N_ST, G_C = 16, 64, 128, 2
XBC = H_C * HP + 2 * G_C * N_ST
NX = XBC // P
TAPS = 5
PAD = TAPS // 2
X_P, X_S = PAD, 3 * PAD + P
XW = X_S + 2 * P + PAD
YW = XW - 2 * PAD
NE, NG = 16, 4
EG = NE // NG
DE = 512
BIG = 1e30
SLOTS = 96
PAIRS = 2 * T
CC = PAIRS // P
CLAMP = 80.0

CQ, CKV, KROPE, BQ, BK, BV, OG, GLOW, Z, CX, DTC, GATES = (
    0, 512, 768, 800, 1312, 1824, 2848, 3872, 3904, 4928, 6464, 6496)

C_ID, C_REL, C_CUM, C_AFT, C_ONE, C_SEL, C_COS, C_SIN, C_RANK = (
    0, 128, 384, 640, 896, 1024, 1026, 1058, 1090)
N_CONST = 1106
V_N1, V_N2, V_BADA, V_QN, V_KVN, V_CN, V_BON, V_CW, V_CB = 0, 8, 16, 64, 68, 70, 78, 86, 146
N_VEC = 158
R_QW, R_KW, R_DTB, R_ALOG, R_D, R_RB = 0, 96, 192, 224, 256, 272
N_ROW = 288

N_ADA = 12
ADA_FIRST = 4
ADA_LATE = 10
W_CQ, W_CKV, W_BQ, W_WQ, W_BK, W_WKV, W_BV = 4, 5, 6, 7, 9, 10, 11
W_GA, W_AO, W_OG, W_GB, W_BO = (13, 15), (17, 19), 20, 22, 24
W_Z, W_CX, W_GC, W_CO, W_OUT, W_LATE, W_MOE = (26, 28), (30, 32, 33), 34, 36, 38, 40, 42
W_ADA = (0, 1, 2, 3, 14, 16, 18, 27, 29, 31, 40, 41)
RING = 3


def trunk_kernel(nc, x, cond, consts, iota, vecs, rows, w_small, w_gate_low, router_w, cache_ckv, cache_krope,
                 state_gla, state_ssd, w_ada, w_in, a_wq, a_wkv, a_wo, b_wo, c_wo, w_out, e_w1, e_w3, e_w2,
                 y, new_ckv, new_krope, new_gla, new_ssd):
    with ExitStack() as ctx:
        def sb(name, shape):
            return ctx.enter_context(nc.sbuf_tensor(name, shape, F32))

        ring = sb("ring", [P, RING, 4096])
        xT = sb("xT", [P, KD, T])
        hT = sb("hT", [P, KD, T])
        mT = sb("mT", [P, KD, T])
        cst = sb("cst", [P, N_CONST])
        vec = sb("vec", [P, N_VEC])
        row = sb("row", [P, N_ROW])
        wsm = sb("wsm", [P, KD, 96])
        wgl = sb("wgl", [2 * RANK + 1, 2, 512])
        rw = sb("rw", [P, KD, NE])
        condT = sb("condT", [P, KD, 2])
        scond = sb("scond", [P, KD, 2])
        mod = sb("mod", [P, 6, KD, 2])
        amp = sb("amp", [P, 2, KD, 2])
        dtraw = sb("dtraw", [P, NT, 32])
        lowT = sb("lowT", [2 * RANK + 1, T])
        rstd = sb("rstd", [P, T])
        arena = sb("arena", [P, 26656])
        starts = ctx.enter_context(nc.sbuf_tensor("starts", [1, NE + 1], mybir.dt.int32))
        overflow = ctx.enter_context(nc.sbuf_tensor("overflow", [1, 1], mybir.dt.int32))
        ps = ctx.enter_context(nc.psum_tensor("ps", [P, 8, 512], F32))

        names = (
            "xin", "cond_ready", "params_in", "cache_in", "squares_ready", "root_ready", "weighted",
            "h_ready", "cqn_ready", "ckvn_ready", "sq_ready", "summed", "stat_ready", "head_root", "rotary_in",
            "nmax_ready", "abs_ready", "soft_ready", "logdecay_ready", "clamped_ready", "decay_ready",
            "qk_ready", "gla_state_in", "scaled_state", "state_ready", "o_ready", "conv_ready",
            "xbc_ready", "ssd_state_in", "diff_ready", "decayed_ready", "mask_ready", "xw_ready",
            "yoff_ready", "y_ready", "merged_ready", "chosen_ready", "iota_in", "sums_ready", "cleared", "starts_ready", "picked", "tokens_in", "hidden_ready", "moe_ready", "stored",
            "act_step", "dve_step", "pool_step")
        sem = {n: ctx.enter_context(nc.semaphore(n)) for n in names}
        over_loaded = [ctx.enter_context(nc.semaphore(f"over_loaded{i}")) for i in range(3)]
        w_loaded = [ctx.enter_context(nc.semaphore(f"w_loaded{i}")) for i in range(RING)]
        psum_full = [ctx.enter_context(nc.semaphore(f"psum_full{i}")) for i in range(8)]
        psum_free = [ctx.enter_context(nc.semaphore(f"psum_free{i}")) for i in range(8)]

        count, waited = {}, {}
        job = {}
        uses = [0] * 8
        turn = [0]
        last_use = {}

        def counts(name):
            count[name] = count.get(name, 0) + 1
            return sem[name], 1

        def counted(name):
            return sem[name], count[name]

        def following(eng, name, by=1):
            key = (str(eng.engine), name)
            waited[key] = waited.get(key, 0) + by
            return sem[name], waited[key]

        def claim(pe, key, bank=None):
            if bank is None:
                bank = turn[0] % 8
                turn[0] += 1
            job[key] = (bank, uses[bank])
            if uses[bank]:
                pe.wait_ge(psum_free[bank], uses[bank])
            uses[bank] += 1
            return ps[:, bank, :]

        def bank(key):
            return ps[:, job[key][0], :]

        def makes(key):
            return psum_full[job[key][0]], 1

        def made(key):
            return psum_full[job[key][0]], job[key][1] + 1

        def reads(key):
            return psum_free[job[key][0]], 1

        def read(key):
            return psum_free[job[key][0]], job[key][1] + 1

        def carve(off, *shape):
            n = 1
            for s in shape:
                n *= s
            v = arena[:, off:off + n]
            if len(shape) == 2:
                return v.rearrange("p (a b) -> p a b", b=shape[1])
            if len(shape) == 3:
                return v.rearrange("p (a b c) -> p a b c", b=shape[1], c=shape[2])
            if len(shape) == 4:
                return v.rearrange("p (a b c d) -> p a b c d", b=shape[1], c=shape[2], d=shape[3])
            return v

        ident = cst[:, C_ID:C_ID + P]
        ones = cst[:, C_ONE:C_ONE + P]

        def rel(d):
            return cst[:, C_REL + P * d:C_REL + P * d + P]

        def cum(d):
            return cst[:, C_CUM + P * d:C_CUM + P * d + P]

        def aft(d):
            return cst[:, C_AFT + P * d:C_AFT + P * d + P]

        COND = ((slice(0, P), 0), (slice(P, T), 1))

        def tok(t):
            return slice(t * P, t * P + P)

        def quad(ap):
            return ap.rearrange("p (a b) -> p a b", b=P)

        def over(ap, n):
            return ap.unsqueeze(2).broadcast_to([ap.shape[0], ap.shape[1], n])

        def each(ap, n):
            return ap.unsqueeze(1).broadcast_to([ap.shape[0], n, ap.shape[1]])

        def chunk(n, k, w):
            return ring[:, n % RING, 0:k * w].rearrange("p (k w) -> p k w", k=k)

        def kpn(ap, i):
            return ap[bass.ds(i, 1)].rearrange("a (k p) n -> p (a k) n", p=P)

        def weight_source(n, l):
            cols = {W_CQ: (CQ, 512), W_CKV: (CKV, KVL), W_BQ: (BQ, 512), W_BK: (BK, 512)}
            for chunks, col in ((W_GA, GATES), (W_Z, Z), (W_CX, CX)):
                for i, c in enumerate(chunks):
                    cols[c] = (col + 512 * i, 512)
            for base, col, m in ((W_GB, GATES + D, 2), (W_GC, GATES + 2 * D, 2), (W_BV, BV, 2), (W_OG, OG, 2)):
                for i in range(m):
                    cols[base + i] = (col + 512 * i, 512)
            if n in W_ADA:
                c = 512 * W_ADA.index(n)
                return kpn(w_ada, l)[:, :, c:c + 512], KD, 512
            if n in cols:
                c, w = cols[n]
                return kpn(w_in, l)[:, :, c:c + w], KD, w
            if n in (W_WQ, W_WQ + 1):
                i = n - W_WQ
                return kpn(a_wq, l)[:, :, 768 * i:768 * i + 768], QL // P, 768
            if n == W_WKV:
                return kpn(a_wkv, l), KVL // P, 2048
            for chunks, ap in ((W_AO, a_wo), ((W_BO, W_BO + 1), b_wo), ((W_CO, W_CO + 1), c_wo), ((W_OUT, W_OUT + 1), w_out)):
                if n in chunks:
                    c = 512 * chunks.index(n)
                    return kpn(ap, l)[:, :, c:c + 512], KD, 512
            raise AssertionError(n)

        def expert_source(i, l, e):
            k = (KD, KD, DE // P)[i]
            return kpn((e_w1, e_w3, e_w2)[i], l * NE + e), k, 4096 // k

        def load_weights(sp, l, n0, n1):
            for n in range(n0, n1):
                if n >= RING:
                    sp.wait_ge(*made(last_use[n - RING]))
                src, k, w = weight_source(n, l) if n < W_MOE else expert_source(n - W_MOE, l, 0)
                sp.dma_start(chunk(n, k, w), src).then_inc(w_loaded[n % RING], 16)

        def weights(pe, n, k, w):
            pe.wait_ge(w_loaded[n % RING], 16 * (n // RING + 1))
            return chunk(n, k, w)

        def matmuls(pe, out, pairs):
            for i, (a, b) in enumerate(pairs):
                ins = pe.matmul(out, a, b, start=(i == 0), stop=(i == len(pairs) - 1))
            return ins

        def feature_major(pe, n, key, src, m=4):
            w = weights(pe, n, KD, P * m)
            for j in range(m):
                matmuls(pe, claim(pe, (key, j))[:, 0:T],
                        [(w[:, k, P * j:P * j + P], src[:, k, :]) for k in range(KD)]).then_inc(*makes((key, j)))
            last_use[n] = (key, m - 1)

        def token_major(pe, n, key):
            w = weights(pe, n, KD, 512)
            for t in range(NT):
                matmuls(pe, claim(pe, (key, t)), [(hT[:, k, tok(t)], w[:, k, :]) for k in range(KD)]).then_inc(*makes((key, t)))
            last_use[n] = (key, NT - 1)

        def square_sum(pe, key, sq, kd, made_from=()):
            out = claim(pe, key)
            if not made_from:
                pe.wait_ge(*following(pe, "squares_ready"))
            for k in made_from:
                pe.wait_ge(*read(k))
            matmuls(pe, out[:, 0:T], [(ones, sq[:, k, :]) for k in range(kd)]).then_inc(*makes(key))

        def transposed(pe, key, srcs, bank=None):
            out = claim(pe, key, bank)
            for i, s in enumerate(srcs):
                ins = pe.transpose(out[0:s.shape[1], i * P:i * P + P], s, ident)
            ins.then_inc(*makes(key))

        def root_mean(dve, key, n):
            dve.wait_ge(*made(key))
            s = bank(key)
            dve.tensor_scalar(rstd[:, :], s[:, 0:T], 1.0 / n, EPS, ALU.mult, ALU.add).then_inc(*reads(key))
            dve.wait_ge(*read(key))
            dve.wait_ge(*following(dve, "root_ready"))
            dve.reciprocal(rstd[:, :], rstd[:, :]).then_inc(*counts("dve_step"))
            dve.wait_ge(*counted("dve_step"))

        def root(act, key):
            act.wait_ge(*read(key))
            act.activation(rstd[:, :], rstd[:, :], ACT.Sqrt).then_inc(*counts("root_ready"))

        NORM_ACT = 5

        def norm_dve(dve, i):
            dve.tensor_tensor(hT[:, 0:2, :], xT[:, 0:2, :], each(rstd[:, :], 2), ALU.mult).then_inc(*counts("weighted"))
            dve.tensor_tensor(hT[:, 2:NORM_ACT, :], xT[:, 2:NORM_ACT, :], each(rstd[:, :], NORM_ACT - 2), ALU.mult
                              ).then_inc(*counts("weighted"))
            dve.tensor_tensor(hT[:, NORM_ACT:, :], xT[:, NORM_ACT:, :], each(rstd[:, :], KD - NORM_ACT), ALU.mult
                              ).then_inc(*counts("dve_step"))
            dve.wait_ge(*counted("dve_step"))
            for k in range(NORM_ACT, KD):
                for ts, c in COND:
                    ins = dve.tensor_scalar(hT[:, k, ts], hT[:, k, ts], amp[:, i, k, c:c + 1],
                                            mod[:, 3 * i, k, c:c + 1], ALU.mult, ALU.add)
            ins.then_inc(*counts("h_ready"))

        def modulation_pe(pe, n, bank=None):
            c = W_ADA[n]
            w = weights(pe, c, KD, 512)
            matmuls(pe, claim(pe, ("mr", n), bank)[0:2, :], [(scond[:, k, :], w[:, k, :]) for k in range(KD)]
                    ).then_inc(*makes(("mr", n)))
            last_use[c] = ("mr", n)

        def modulation_sums(dve, n, sums):
            c = W_ADA[n]
            w = chunk(c, KD, 512)
            dve.wait_ge(w_loaded[c % RING], 16 * (c // RING + 1))
            for k in range(KD):
                for v in range(2):
                    if k == 0:
                        ins = dve.tensor_scalar(sums[:, v, :], w[:, k, :], scond[:, k, v:v + 1], None, ALU.mult)
                    else:
                        ins = dve.scalar_tensor_tensor(out=sums[:, v, :], in0=w[:, k, :], scalar=scond[:, k, v:v + 1],
                                                       in1=sums[:, v, :], op0=ALU.mult, op1=ALU.add)
                ins.then_inc(*counts("dve_step" if k < KD - 1 else "sums_ready"))
                dve.wait_ge(*counted("dve_step" if k < KD - 1 else "sums_ready"))

        def modulation_sums_pe(pe, n, sums):
            pe.wait_ge(*following(pe, "sums_ready"))
            m = claim(pe, ("mod", n))
            for j in range(4):
                for v in range(2):
                    ins = pe.matmul(m[:, 2 * j + v:2 * j + v + 1], sums[:, v, P * j:P * j + P], ones[:, 0:1],
                                    start=True, stop=True)
            ins.then_inc(*makes(("mod", n)))
            last_use[W_ADA[n]] = ("mod", n)

        def modulation_features_pe(pe, n, rows, bank=None):
            pe.wait_ge(*read(("mr", n)))
            m = claim(pe, ("mod", n), bank)
            for j in range(4):
                ins = pe.transpose(m[:, 2 * j:2 * j + 2], rows[0:2, P * j:P * j + P], ident[0:2, 0:2])
            ins.then_inc(*makes(("mod", n)))

        def modulation_rows_dve(dve, n, rows):
            dve.wait_ge(*made(("mr", n)))
            dve.tensor_copy(rows[0:2, :], bank(("mr", n))[0:2, :]).then_inc(*reads(("mr", n)))
            dve.wait_ge(*read(("mr", n)))

        def modulation_dve(dve, n):
            dve.wait_ge(*made(("mod", n)))
            s = bank(("mod", n))
            modc = mod.rearrange("p s k c -> p (s k) c")
            dve.tensor_tensor(modc[:, 4 * n:4 * n + 4, :], s[:, 0:8].rearrange("p (a b) -> p a b", b=2),
                              over(vec[:, V_BADA + 4 * n:V_BADA + 4 * n + 4], 2), ALU.add).then_inc(*reads(("mod", n)))
            dve.wait_ge(*read(("mod", n)))

        def amplitude(dve, i, w):
            dve.scalar_tensor_tensor(out=amp[:, i, :, :], in0=mod[:, 3 * i + 1, :, :], scalar=1.0,
                                     in1=over(vec[:, w:w + KD], 2), op0=ALU.add, op1=ALU.mult
                                     ).then_inc(*counts("dve_step"))
            dve.wait_ge(*counted("dve_step"))

        def norm_act(act, i, key, sq):
            act.activation(sq, xT[:, :, :], ACT.Square).then_inc(*counts("squares_ready"))
            root(act, key)
            for k in range(NORM_ACT):
                if k in (0, 2):
                    act.wait_ge(*following(act, "weighted"))
                for ts, c in COND:
                    ins = act.activation(hT[:, k, ts], hT[:, k, ts], ACT.Identity,
                                         bias=mod[:, 3 * i, k, c:c + 1], scale=amp[:, i, k, c:c + 1])
            ins.then_inc(*counts("h_ready"))

        def gate_act(act, key, gT):
            for i in range(2):
                for j in range(4):
                    act.wait_ge(*made(((key, i), j)))
                    s = bank(((key, i), j))
                    act.activation(gT[4 * i + j], s[:, 0:T], ACT.Sigmoid).then_inc(*reads(((key, i), j)))
                    act.wait_ge(*read(((key, i), j)))

        def gate_pe(pe, n, key, g):
            i, j = divmod(g, 4)
            w = weights(pe, n + i, KD, 512)
            matmuls(pe, claim(pe, ((key, i), j))[:, 0:T],
                    [(w[:, k, P * j:P * j + P], hT[:, k, :]) for k in range(KD)]).then_inc(*makes(((key, i), j)))
            last_use[n + i] = ((key, i), j)

        def gate_tile_act(act, key, gT, g):
            i, j = divmod(g, 4)
            act.wait_ge(*made(((key, i), j)))
            act.activation(gT[g], bank(((key, i), j))[:, 0:T], ACT.Sigmoid).then_inc(*reads(((key, i), j)))
            act.wait_ge(*read(((key, i), j)))

        def gated_sum(dve, key, gkey, gT, first):
            for i in range(2):
                for j in range(4):
                    d = 4 * i + j
                    dve.wait_ge(*made(((key, i), j)))
                    s = bank(((key, i), j))
                    if first:
                        dve.wait_ge(*read(((gkey, i), j)))
                        dve.tensor_tensor(mT[:, d, :], s[:, 0:T], gT[d], ALU.mult).then_inc(*reads(((key, i), j)))
                        dve.wait_ge(*read(((key, i), j)))
                    else:
                        dve.tensor_tensor(gT[d], s[:, 0:T], gT[d], ALU.mult).then_inc(*reads(((key, i), j)))
                        dve.wait_ge(*read(((key, i), j)))
                        ins = dve.tensor_tensor(mT[:, d, :], mT[:, d, :], gT[d], ALU.add)
                        ins.then_inc(*counts("dve_step"))
                        dve.wait_ge(*counted("dve_step"))

        def to_features(pe, key, src):
            for t in range(NT):
                for q in range(2):
                    transposed(pe, (key, t, q), [src[:, t, 512 * q + P * i:512 * q + P * i + P] for i in range(4)])

        def features_dve(dve, key, dst, w=None):
            for t in range(NT):
                for q in range(2):
                    dve.wait_ge(*made((key, t, q)))
                    s = quad(bank((key, t, q)))
                    out = dst[:, 4 * q:4 * q + 4, tok(t)]
                    if w is None:
                        ins = dve.tensor_copy(out, s)
                    else:
                        ins = dve.tensor_tensor(out, s, over(vec[:, w + 4 * q:w + 4 * q + 4], P), ALU.mult)
                    ins.then_inc(*reads((key, t, q)))
                    dve.wait_ge(*read((key, t, q)))

        def project_pe(pe, chunks, key, src, tkey, between=None):
            for t in range(NT):
                for q in range(2):
                    pe.wait_ge(*read((tkey, t, q)))
            for i in range(2):
                feature_major(pe, chunks[i], (key, i), src)
                if between and i == 0:
                    between()

        x_in = carve(0, NT, D)
        with nc.Block() as block:
            @block.tensor
            def _(pe):
                pe.wait_ge(sem["xin"], 64)
                to_features(pe, "x", x_in)

            @block.sync
            def _(sp):
                sp.dma_start(x_in, x.rearrange("(t p) d -> p t d", p=P)).then_inc(sem["xin"], 16)
                sp.dma_start(cst[:, :], consts).then_inc(sem["xin"], 16)
                sp.dma_start(condT[:, :, :], cond).then_inc(sem["xin"], 16)
                sp.dma_start(rw[:, :, :], router_w.rearrange("(k p) e -> p k e", p=P)).then_inc(sem["xin"], 16)
                load_weights(sp, 0, 0, RING)
                sp.wait_ge(sem["xin"], 64)

            @block.vector
            def _(dve):
                dve.memset(lowT[2 * RANK:2 * RANK + 1, :], 1.0).then_inc(*counts("dve_step"))
                dve.wait_ge(*counted("dve_step"))
                features_dve(dve, "x", xT)

            @block.scalar
            def _(act):
                act.wait_ge(sem["xin"], 64)
                act.activation(scond[:, :, :], condT[:, :, :], ACT.Silu).then_inc(*counts("cond_ready"))
                act.wait_ge(*counted("cond_ready"))

        def clear_counts(loads=False):
            for s in list(sem.values()) + over_loaded + psum_full + psum_free + (w_loaded if loads else []):
                nc.sync.sem_clear(s)
            nc.all_engine_barrier()
            for d in (count, waited, job, last_use):
                d.clear()
            for b in range(8):
                uses[b] = 0

        clear_counts()

        m_flat = mT[:, :, :].rearrange("p k t -> p (k t)")
        q_tok = carve(0, NT, H_A, QK)
        k_tok = carve(4608, NKT, H_A, QK)
        v_a = carve(10752, NKT, H_A, V_A)
        q_b = carve(14848, NT, H_B, DK)
        k_b = carve(16384, NT, H_B, DK)
        v_b = carve(17920, NT, H_B, DV)
        cqT = carve(20992, QL // P, T)
        ckvT = carve(22528, KVL // P, T + P)
        kr = carve(23552, NKT, ROPE)
        cache_tok = carve(23680, KVL)
        ckv_out = carve(23936, KVL)
        stat = carve(24192, 2, NKT * H_A)
        sq_heads = carve(24320, H_A, QK)
        rope_tmp = carve(20992, 4, H_A, ROPE // 2)
        mod_sums_n = carve(2048, 2, 512)
        mod_rows = carve(0, ADA_FIRST, 512)
        sq_x = carve(17920, KD, T)
        sq4 = m_flat[:, 0:QL // P * T].rearrange("p (a b) -> p a b", b=T)
        sq2 = m_flat[:, 1536:1536 + KVL // P * T].rearrange("p (a b) -> p a b", b=T)
        o_tok = m_flat.rearrange("p (t d) -> p t d", d=D)
        head_qT = carve(20992, 2, T)
        head_kT = carve(21760, 2, T + P)
        probs = carve(22784, 3, T)
        probsT = carve(23936, 2, T)
        nmax = carve(24704, 4)
        rsum = carve(24720, NT, H_A)
        mod_sums = carve(24768, 2, 512)
        gT = [carve(T * k, T) for k in range(KD)]
        oT = carve(4608, KD, T)

        with nc.Fori(0, DEPTH) as l:
            with nc.Block() as block:
                @block.tensor
                def _(pe):
                    for n in (0, 2, 3):
                        if n == 2:
                            square_sum(pe, "n1", sq_x, KD)
                        if n == 3:
                            modulation_sums_pe(pe, 1, mod_sums_n)
                        modulation_pe(pe, n)
                    for n in (0, 2, 3):
                        modulation_features_pe(pe, n, mod_rows[:, n, :])
                    pe.wait_ge(*following(pe, "h_ready", 2))
                    feature_major(pe, W_CQ, "cq", hT)
                    feature_major(pe, W_CKV, "ckv", hT, 2)
                    pe.wait_ge(*following(pe, "params_in", 64))
                    out = claim(pe, "krdt")
                    for t in range(NT):
                        ins = matmuls(pe, out[:, 64 * t:64 * t + 64],
                                      [(hT[:, k, tok(t)], wsm[:, k, 0:64]) for k in range(KD)])
                    ins.then_inc(*makes("krdt"))
                    out = claim(pe, "low")
                    matmuls(pe, out[0:2 * RANK, 0:T], [(wsm[:, k, 64:96], hT[:, k, :]) for k in range(KD)]
                            ).then_inc(*makes("low"))
                    pe.wait_ge(*following(pe, "cache_in", 32))
                    transposed(pe, "cache", [cache_tok[:, 0:P], cache_tok[:, P:2 * P]])
                    square_sum(pe, "ncq", sq4, QL // P, [("cq", j) for j in range(QL // P)])
                    square_sum(pe, "nckv", sq2, KVL // P, [("ckv", j) for j in range(KVL // P)])
                    token_major(pe, W_BQ, "bq")
                    pe.wait_ge(*following(pe, "cqn_ready"))
                    for c in range(2):
                        w = weights(pe, W_WQ + c, QL // P, 768)
                        for t in range(NT):
                            for h in range(2):
                                matmuls(pe, claim(pe, ("q", c, t, h))[:, 0:384],
                                        [(cqT[:, k, tok(t)], w[:, k, 384 * h:384 * h + 384])
                                         for k in range(QL // P)]).then_inc(*makes(("q", c, t, h)))
                        last_use[W_WQ + c] = ("q", c, NT - 1, 1)
                    token_major(pe, W_BK, "bk")
                    pe.wait_ge(*following(pe, "ckvn_ready"))
                    pe.wait_ge(*read("cache"))
                    transposed(pe, "ckv_out", [ckvT[:, 0, 0:P], ckvT[:, 1, 0:P]])
                    w = weights(pe, W_WKV, KVL // P, 2048)
                    for t in range(NKT):
                        for h in range(4):
                            matmuls(pe, claim(pe, ("kv", t, h)),
                                    [(ckvT[:, k, tok(t)], w[:, k, 512 * h:512 * h + 512])
                                     for k in range(KVL // P)]).then_inc(*makes(("kv", t, h)))
                    last_use[W_WKV] = ("kv", NKT - 1, 3)
                    for i in range(2):
                        token_major(pe, W_BV + i, ("bv", i))

                @block.sync
                def _(sp):
                    for dst, src in ((vec[:, :], vecs), (row[:, :], rows)):
                        sp.dma_start(dst, src[bass.ds(l, 1)].rearrange("a p n -> p (a n)")).then_inc(sem["params_in"], 16)
                    sp.dma_start(wsm[:, :, :], kpn(w_small, l)).then_inc(sem["params_in"], 16)
                    sp.dma_start(wgl[:, :, :], w_gate_low[bass.ds(l, 1)].rearrange("a r d n -> r (a d) n")
                                 ).then_inc(sem["params_in"], 16)
                    sp.dma_start(cache_tok, cache_ckv[bass.ds(l, 1)].rearrange("a p n -> p (a n)")
                                 ).then_inc(sem["cache_in"], 16)
                    sp.dma_start(kr[:, NT, :], cache_krope[bass.ds(l, 1)].rearrange("a p n -> p (a n)")
                                 ).then_inc(sem["cache_in"], 16)
                    load_weights(sp, l, RING, W_BV + 2)
                    sp.wait_ge(*read("krdt"))
                    sp.dma_start(new_krope[bass.ds(l, 1)].rearrange("a p n -> p (a n)"), kr[:, 0, :]
                                 ).then_inc(sem["stored"], 16)
                    sp.wait_ge(*read("ckv_out"))
                    sp.dma_start(new_ckv[bass.ds(l, 1)].rearrange("a p n -> p (a n)"), ckv_out
                                 ).then_inc(sem["stored"], 16)
                    load_weights(sp, l, W_BV + 2, W_GA[0] + RING)
                    sp.wait_ge(*following(sp, "stored", 32))

                @block.scalar
                def _(act):
                    norm_act(act, 0, "n1", sq_x)
                    for j in range(QL // P):
                        act.wait_ge(*made(("cq", j)))
                        s = bank(("cq", j))
                        act.activation(cqT[:, j, :], s[:, 0:T], ACT.Copy).then_inc(*counts("act_step"))
                        act.wait_ge(*counted("act_step"))
                        act.activation(sq4[:, j, :], s[:, 0:T], ACT.Square).then_inc(*reads(("cq", j)))
                        act.wait_ge(*read(("cq", j)))
                    for j in range(KVL // P):
                        act.wait_ge(*made(("ckv", j)))
                        s = bank(("ckv", j))
                        act.activation(ckvT[:, j, 0:T], s[:, 0:T], ACT.Copy).then_inc(*counts("act_step"))
                        act.wait_ge(*counted("act_step"))
                        act.activation(sq2[:, j, :], s[:, 0:T], ACT.Square).then_inc(*reads(("ckv", j)))
                        act.wait_ge(*read(("ckv", j)))
                    root(act, "ncq")
                    root(act, "nckv")

                    def evacuate(key, dst, scale=1.0):
                        act.wait_ge(*made(key))
                        act.activation(dst, bank(key).rearrange("p (h d) -> p h d", h=dst.shape[1]), ACT.Copy, scale=scale
                                       ).then_inc(*reads(key))
                        act.wait_ge(*read(key))

                    for t in range(NT):
                        evacuate(("bq", t), q_b[:, t, :, :], float(DK) ** -0.5)

                    def squares(x, i, t):
                        if (i, t) != (0, 0):
                            act.wait_ge(*following(act, "summed"))
                        act.activation(sq_heads, x[:, t, :, :], ACT.Square).then_inc(*counts("sq_ready"))

                    for t in range(NT):
                        for c in range(2):
                            for h in range(2):
                                act.wait_ge(*read(("q", c, t, h)))
                        squares(q_tok, 0, t)
                    act.wait_ge(*following(act, "stat_ready"))
                    act.activation(stat[:, 0, 0:NT * H_A], stat[:, 0, 0:NT * H_A], ACT.Sqrt).then_inc(*counts("head_root"))
                    for t in range(NT):
                        evacuate(("bk", t), k_b[:, t, :, :])
                    act.wait_ge(*made("ckv_out"))
                    act.activation(ckv_out, bank("ckv_out")[:, 0:KVL], ACT.Copy).then_inc(*reads("ckv_out"))
                    act.wait_ge(*read("ckv_out"))
                    act.wait_ge(*following(act, "rotary_in"))
                    for t in range(NKT):
                        for h in range(4):
                            act.wait_ge(*made(("kv", t, h)))
                            s = bank(("kv", t, h)).rearrange("p (h d) -> p h d", h=4)
                            act.activation(v_a[:, t, 4 * h:4 * h + 4, :], s[:, :, NOPE:], ACT.Copy
                                           ).then_inc(*counts("act_step"))
                            act.activation(k_tok[:, t, 4 * h:4 * h + 4, 0:NOPE], s[:, :, 0:NOPE], ACT.Copy
                                           ).then_inc(*reads(("kv", t, h)))
                            act.wait_ge(*read(("kv", t, h)))
                        squares(k_tok, 1, t)
                    for i in range(2):
                        for t in range(NT):
                            if (i, t) == (0, 1):
                                act.wait_ge(*following(act, "summed"))
                                act.wait_ge(*following(act, "stat_ready"))
                                act.activation(stat[:, 1, :], stat[:, 1, :], ACT.Sqrt).then_inc(*counts("head_root"))
                            evacuate((("bv", i), t), v_b[:, t, 2 * i:2 * i + 2, :])

                @block.gpsimd
                def _(pool):
                    pool.wait_ge(*following(pool, "cache_in", 32))
                    pool.wait_ge(*read("krdt"))
                    for t in range(NKT):
                        ins = pool.tensor_copy(k_tok[:, t, :, NOPE:], each(kr[:, t, :], H_A))
                    ins.then_inc(*counts("rotary_in"))

                @block.vector
                def _(dve):
                    modulation_sums(dve, 1, mod_sums_n)
                    dve.wait_ge(*following(dve, "params_in", 64))
                    modulation_rows_dve(dve, 0, mod_rows[:, 0, :])
                    root_mean(dve, "n1", D)
                    for n in (2, 3):
                        modulation_rows_dve(dve, n, mod_rows[:, n, :])
                    for n in range(ADA_FIRST):
                        modulation_dve(dve, n)
                    amplitude(dve, 0, V_N1)
                    norm_dve(dve, 0)
                    dve.wait_ge(*made("krdt"))
                    s = bank("krdt")[:, 0:NT * 64].rearrange("p (t c) -> p t c", c=64)
                    dve.tensor_copy(dtraw[:, :, :], s[:, :, 32:64]).then_inc(*counts("dve_step"))
                    dve.wait_ge(*counted("dve_step"))
                    dve.tensor_copy(kr[:, 0:NT, :], s[:, :, 0:32]).then_inc(*reads("krdt"))
                    dve.wait_ge(*read("krdt"))
                    dve.wait_ge(*made("low"))
                    dve.tensor_copy(lowT[0:2 * RANK, :], bank("low")[0:2 * RANK, 0:T]).then_inc(*reads("low"))
                    dve.wait_ge(*read("low"))
                    dve.wait_ge(*made("cache"))
                    dve.tensor_copy(ckvT[:, :, T:], quad(bank("cache")[:, 0:2 * P])).then_inc(*reads("cache"))
                    dve.wait_ge(*read("cache"))
                    root_mean(dve, "ncq", QL)
                    for j in range(QL // P):
                        ins = dve.scalar_tensor_tensor(out=cqT[:, j, :], in0=cqT[:, j, :], scalar=vec[:, V_QN + j:V_QN + j + 1],
                                                       in1=rstd[:, :], op0=ALU.mult, op1=ALU.mult)
                    ins.then_inc(*counts("cqn_ready"))
                    dve.wait_ge(*counted("cqn_ready"))
                    root_mean(dve, "nckv", KVL)
                    for j in range(KVL // P):
                        ins = dve.scalar_tensor_tensor(out=ckvT[:, j, 0:T], in0=ckvT[:, j, 0:T],
                                                       scalar=vec[:, V_KVN + j:V_KVN + j + 1],
                                                       in1=rstd[:, :], op0=ALU.mult, op1=ALU.mult)
                    ins.then_inc(*counts("ckvn_ready"))
                    dve.wait_ge(*counted("ckvn_ready"))
                    for c in range(2):
                        for t in range(NT):
                            for h in range(2):
                                dve.wait_ge(*made(("q", c, t, h)))
                                h0 = 8 * c + 4 * h
                                dve.tensor_copy(q_tok[:, t, h0:h0 + 4, :],
                                                bank(("q", c, t, h))[:, 0:384].rearrange("p (h d) -> p h d", d=QK)
                                                ).then_inc(*reads(("q", c, t, h)))
                                dve.wait_ge(*read(("q", c, t, h)))

                    def head_norm(x, tiles, i, scale, w):
                        n = tiles * H_A
                        heads = x.rearrange("p t h d -> p (t h) d")
                        st = stat[:, i, 0:n]
                        for t in range(tiles):
                            dve.wait_ge(*following(dve, "sq_ready"))
                            dve.tensor_reduce(stat[:, i, H_A * t:H_A * t + H_A], sq_heads, AX_X, ALU.add
                                              ).then_inc(*counts("summed"))
                            dve.wait_ge(*counted("summed"))
                        dve.tensor_scalar(st, st, 1.0 / QK, EPS, ALU.mult, ALU.add).then_inc(*counts("stat_ready"))
                        dve.wait_ge(*counted("stat_ready"))
                        dve.wait_ge(*following(dve, "head_root"))
                        dve.reciprocal(st, st).then_inc(*counts("dve_step"))
                        dve.wait_ge(*counted("dve_step"))
                        dve.tensor_tensor(heads, heads, over(st, QK), ALU.mult).then_inc(*counts("dve_step"))
                        dve.wait_ge(*counted("dve_step"))
                        dve.scalar_tensor_tensor(out=heads, in0=heads, scalar=scale, in1=each(row[:, w:w + QK], n),
                                                 op0=ALU.mult, op1=ALU.mult).then_inc(*counts("dve_step"))
                        dve.wait_ge(*counted("dve_step"))

                    def rotate(x):
                        for t in (1, 2):
                            pairs = x[:, t, :, NOPE:].rearrange("p h (m two) -> p h two m", two=2)
                            x1, x2 = pairs[:, :, 0, :], pairs[:, :, 1, :]
                            cos = each(cst[:, C_COS + 16 * (t - 1):C_COS + 16 * t], H_A)
                            sin = each(cst[:, C_SIN + 16 * (t - 1):C_SIN + 16 * t], H_A)
                            for i, (a, b) in enumerate(((x1, cos), (x2, sin), (x1, sin), (x2, cos))):
                                ins = dve.tensor_tensor(rope_tmp[:, i, :, :], a, b, ALU.mult)
                            ins.then_inc(*counts("dve_step"))
                            dve.wait_ge(*counted("dve_step"))
                            dve.tensor_tensor(x1, rope_tmp[:, 0], rope_tmp[:, 1], ALU.subtract)
                            dve.tensor_tensor(x2, rope_tmp[:, 2], rope_tmp[:, 3], ALU.add).then_inc(*counts("dve_step"))
                            dve.wait_ge(*counted("dve_step"))

                    head_norm(q_tok, NT, 0, float(QK) ** -0.5, R_QW)
                    rotate(q_tok)
                    head_norm(k_tok, NKT, 1, 1.0, R_KW)
                    rotate(k_tok)

            STEPS = [(h, t) for h in range(H_A) for t in range(NT)]
            KEYS = ((0, 1), (1, NKT), (1, NKT))
            AHEAD = 2
            B_PV, N_ROT = 5, 5
            with nc.Block() as block:
                def next_head(i):
                    return (i + 1) // NT + 1 if i % NT == NT - 1 and (i + 1) // NT + 1 < H_A else None

                @block.tensor
                def _(pe):
                    turns = [0]

                    def rotating(key):
                        turns[0] += 1
                        return claim(pe, key, turns[0] % N_ROT)

                    def head(h):
                        for key, x, tiles in ((("qT", h), q_tok, NT), (("kT", h), k_tok, NKT)):
                            out = rotating(key)
                            for t in range(tiles):
                                ins = pe.transpose(out[0:QK, tok(t)], x[:, t, h, :], ident)
                            ins.then_inc(*makes(key))

                    def scores(i):
                        h, t = STEPS[i]
                        k0, k1 = KEYS[t]
                        if t == 0:
                            pe.wait_ge(*read(("qT", h)))
                            pe.wait_ge(*read(("kT", h)))
                        out = rotating(("s", i))
                        pe.matmul(out[:, 0:P * (k1 - k0)], head_qT[0:QK, h % 2, tok(t)],
                                  head_kT[0:QK, h % 2, P * k0:P * k1], start=True, stop=True).then_inc(*makes(("s", i)))

                    def turn_probs(i):
                        h, t = STEPS[i]
                        k0, k1 = KEYS[t]
                        pe.wait_ge(*read(("s", i)))
                        out = rotating(("pt", i))
                        for k in range(k1 - k0):
                            ins = pe.transpose(out[:, P * k:P * k + P], probs[:, i % 3, P * k:P * k + P], ident)
                        ins.then_inc(*makes(("pt", i)))

                    def weigh_values(i):
                        h, t = STEPS[i]
                        k0, k1 = KEYS[t]
                        if h % 8 == 0:
                            claim(pe, ("pv", t, h // 8), B_PV + t)
                        pe.wait_ge(*read(("pt", i)))
                        c = V_A * (h % 8)
                        ins = matmuls(pe, ps[:, B_PV + t, c:c + V_A],
                                      [(probsT[:, i % 2, P * k:P * k + P], v_a[:, k0 + k, h, :]) for k in range(k1 - k0)])
                        if h % 8 == 7:
                            ins.then_inc(*makes(("pv", t, h // 8)))

                    head(0)
                    head(1)
                    for i in range(-AHEAD, len(STEPS) + 1):
                        if i + AHEAD < len(STEPS):
                            scores(i + AHEAD)
                        if i >= 0 and next_head(i):
                            head(next_head(i))
                        if 0 <= i < len(STEPS):
                            turn_probs(i)
                        if i >= 1:
                            weigh_values(i - 1)

                @block.scalar
                def _(act):
                    def queries(h):
                        act.wait_ge(*made(("qT", h)))
                        act.activation(head_qT[0:QK, h % 2, :], bank(("qT", h))[0:QK, 0:T], ACT.Copy).then_inc(*reads(("qT", h)))
                        act.wait_ge(*read(("qT", h)))

                    queries(0)
                    queries(1)
                    for j in range(-AHEAD, len(STEPS)):
                        i = j + AHEAD
                        if i < len(STEPS):
                            h, t = STEPS[i]
                            n = P * (KEYS[t][1] - KEYS[t][0])
                            if i >= 3:
                                act.wait_ge(*made(("pt", i - 3)))
                            act.wait_ge(*following(act, "nmax_ready"))
                            act.wait_ge(*made(("s", i)))
                            s = bank(("s", i))
                            act.activation(probs[:, i % 3, 0:n], s[:, 0:n], ACT.Exp, bias=nmax[:, i % 4:i % 4 + 1],
                                           accum_out=rsum[:, t, h:h + 1]).then_inc(*reads(("s", i)))
                            act.wait_ge(*read(("s", i)))
                        if j >= 0 and next_head(j):
                            queries(next_head(j))

                @block.vector
                def _(dve):
                    def keys(h):
                        dve.wait_ge(*made(("kT", h)))
                        dve.tensor_copy(head_kT[0:QK, h % 2, :], bank(("kT", h))[0:QK, :]).then_inc(*reads(("kT", h)))
                        dve.wait_ge(*read(("kT", h)))

                    def turned(i):
                        h, t = STEPS[i]
                        n = P * (KEYS[t][1] - KEYS[t][0])
                        dve.wait_ge(*made(("pt", i)))
                        dve.tensor_copy(probsT[:, i % 2, 0:n], bank(("pt", i))[:, 0:n]).then_inc(*reads(("pt", i)))
                        dve.wait_ge(*read(("pt", i)))

                    def heads_out(t, g):
                        dve.wait_ge(*made(("pv", t, g)))
                        s = bank(("pv", t, g)).rearrange("p (h d) -> p h d", d=V_A)
                        r = rsum[:, t, 8 * g:8 * g + 8]
                        dve.reciprocal(r, r).then_inc(*counts("dve_step"))
                        dve.wait_ge(*counted("dve_step"))
                        dve.tensor_tensor(o_tok[:, t, 512 * g:512 * g + 512].rearrange("p (h d) -> p h d", d=V_A),
                                          s, over(r, V_A), ALU.mult).then_inc(*reads(("pv", t, g)))
                        dve.wait_ge(*read(("pv", t, g)))

                    keys(0)
                    keys(1)
                    for j in range(-AHEAD, len(STEPS) + 2):
                        i = j + AHEAD
                        if i < len(STEPS):
                            h, t = STEPS[i]
                            n = P * (KEYS[t][1] - KEYS[t][0])
                            dve.wait_ge(*made(("s", i)))
                            s = bank(("s", i))
                            dve.tensor_reduce(nmax[:, i % 4:i % 4 + 1], s[:, 0:n], AX_X, ALU.max, negate=True
                                              ).then_inc(*counts("nmax_ready"))
                        if j >= 0 and next_head(j):
                            keys(next_head(j))
                        if 0 <= j < len(STEPS):
                            turned(j)
                        if j >= 2:
                            h, t = STEPS[j - 2]
                            if h % 8 == 7:
                                heads_out(t, h // 8)

            with nc.Block() as block:
                @block.tensor
                def _(pe):
                    for i in range(2):
                        feature_major(pe, W_GA[i], ("ga", i), hT)
                        modulation_sums_pe(pe, ADA_FIRST + i, mod_sums)
                    to_features(pe, "oa", o_tok)
                    project_pe(pe, W_AO, "ao", oT, "oa", lambda: modulation_sums_pe(pe, ADA_FIRST + 2, mod_sums))

                @block.scalar
                def _(act):
                    gate_act(act, "ga", gT)

                @block.vector
                def _(dve):
                    modulation_sums(dve, ADA_FIRST, mod_sums)
                    modulation_dve(dve, ADA_FIRST)
                    modulation_sums(dve, ADA_FIRST + 1, mod_sums)
                    modulation_dve(dve, ADA_FIRST + 1)
                    features_dve(dve, "oa", oT)
                    modulation_sums(dve, ADA_FIRST + 2, mod_sums)
                    gated_sum(dve, "ao", "ga", gT, True)
                    modulation_dve(dve, ADA_FIRST + 2)

                @block.sync
                def _(sp):
                    load_weights(sp, l, W_GA[0] + RING, W_AO[1] + RING)

            og = carve(0, NT, D)
            logdec = carve(3072, 2, NT, H_B * DK)
            o_b = carve(6144, NT, D)
            soft = carve(6144, 2, NT, H_B * DK)
            sq_b = carve(3072, NT * H_B, DV)
            gla_s = carve(9216, 2, H_B, DV)
            gla_p = carve(11264, 2, H_B, DV)
            clamped = carve(13312, 512)
            up = carve(13824, H_B * DK)
            down = carve(14336, H_B * DK)
            qt = carve(20992, H_B, DK)
            kt = carve(21504, H_B, DK)
            qtT = carve(22016, H_B, P)
            ktT = carve(22528, H_B, P)
            att = carve(23040, H_B, P)
            ecol = carve(23552, 2, H_B, 2)
            stat_b = carve(23568, NT * H_B)
            gT_b = [carve(23584 + T * k, T) for k in range(KD)]
            SCAN = ((0, 0), (1, 0), (0, 1), (1, 2), (0, 2), (1, 1))
            FIRST = (0, 2, 3)
            LAST = (4, 5)
            with nc.Block() as block:
                @block.tensor
                def _(pe):
                    for t in range(NT):
                        for d in range(2):
                            pe.matmul(claim(pe, ("lg", t, d)), lowT[:, tok(t)], wgl[:, d, :], start=True, stop=True).then_inc(*makes(("lg", t, d)))
                    for i in range(2):
                        token_major(pe, W_OG + i, ("og", i))
                    pe.wait_ge(*following(pe, "logdecay_ready"))
                    for s, (d, t) in enumerate(SCAN):
                        pe.matmul(claim(pe, ("b", s)), rel(d), logdec[:, d, t, :], start=True, stop=True).then_inc(*makes(("b", s)))
                        out = claim(pe, ("ec", s))
                        for h in range(H_B):
                            ins = pe.matmul(out[:, 2 * h:2 * h + 2], logdec[:, d, t, DK * h:DK * h + DK],
                                            cst[:, C_SEL:C_SEL + 2], start=True, stop=True)
                        ins.then_inc(*makes(("ec", s)))
                        gate_pe(pe, W_GB, "gb", s)
                        pe.wait_ge(*following(pe, "qk_ready"))
                        transposed(pe, ("qtT", s), [qt[:, h, :] for h in range(H_B)])
                        transposed(pe, ("ktT", s), [kt[:, h, :] for h in range(H_B)])
                        pe.wait_ge(*read(("qtT", s)))
                        pe.wait_ge(*read(("ktT", s)))
                        out = claim(pe, ("att", s))
                        for h in range(H_B):
                            ins = pe.matmul(out[:, P * h:P * h + P], ktT[:, h, :], qtT[:, h, :], start=True, stop=True)
                        ins.then_inc(*makes(("att", s)))
                        if s not in LAST:
                            for g in range(2):
                                out = claim(pe, ("ds", s, g))
                                for h in (2 * g, 2 * g + 1):
                                    c = DV * (h % 2)
                                    ins = pe.matmul(out[:, c:c + DV], kt[:, h, :], v_b[:, t, h, :], start=True, stop=True)
                                ins.then_inc(*makes(("ds", s, g)))
                        pe.wait_ge(*read(("att", s)))
                        if t:
                            pe.wait_ge(*following(pe, "scaled_state"))
                        for g in range(2):
                            out = claim(pe, ("o", s, g))
                            for h in (2 * g, 2 * g + 1):
                                c = DV * (h % 2)
                                pairs = [(att[:, h, :], v_b[:, t, h, :])]
                                if t:
                                    pairs.append((qtT[:, h, :], gla_s[:, d, h, :]))
                                ins = matmuls(pe, out[:, c:c + DV], pairs)
                            ins.then_inc(*makes(("o", s, g)))
                    for g in range(len(SCAN), KD):
                        gate_pe(pe, W_GB, "gb", g)

                @block.scalar
                def _(act):
                    act.wait_ge(*following(act, "abs_ready"))
                    act.activation(soft, soft, ACT.Exp, scale=-1.0).then_inc(*counts("act_step"))
                    act.wait_ge(*counted("act_step"))
                    act.activation(soft, soft, ACT.Ln, bias=1.0).then_inc(*counts("soft_ready"))
                    for i in range(2):
                        for t in range(NT):
                            act.wait_ge(*made((("og", i), t)))
                            s = bank((("og", i), t))
                            act.activation(og[:, t, 512 * i:512 * i + 512], s, ACT.Silu).then_inc(*reads((("og", i), t)))
                            act.wait_ge(*read((("og", i), t)))
                    for s in range(len(SCAN)):
                        act.wait_ge(*following(act, "clamped_ready"))
                        act.activation(up, clamped, ACT.Exp).then_inc(*counts("act_step"))
                        act.wait_ge(*counted("act_step"))
                        act.activation(down, clamped, ACT.Exp, scale=-1.0).then_inc(*counts("decay_ready"))
                        act.wait_ge(*made(("ec", s)))
                        act.activation(ecol[:, s % 2, :, :],
                                       bank(("ec", s))[:, 0:2 * H_B].rearrange("p (h e) -> p h e", e=2),
                                       ACT.Exp).then_inc(*reads(("ec", s)))
                        act.wait_ge(*read(("ec", s)))
                        gate_tile_act(act, "gb", gT_b, s)
                        act.wait_ge(*made(("qtT", s)))
                        act.activation(qtT, quad(bank(("qtT", s))), ACT.Copy).then_inc(*reads(("qtT", s)))
                        act.wait_ge(*read(("qtT", s)))
                    act.wait_ge(*following(act, "o_ready"))
                    act.activation(sq_b, o_b.rearrange("p t (h d) -> p (t h) d", d=DV), ACT.Square).then_inc(*counts("sq_ready"))
                    act.wait_ge(*following(act, "stat_ready"))
                    act.activation(stat_b, stat_b, ACT.Sqrt).then_inc(*counts("head_root"))
                    for g in range(len(SCAN), KD):
                        gate_tile_act(act, "gb", gT_b, g)

                @block.gpsimd
                def _(pool):
                    pool.wait_ge(*following(pool, "gla_state_in", 32))
                    for s, (d, t) in enumerate(SCAN):
                        if t:
                            pool.wait_ge(*read(("ec", s)))
                            if s in LAST:
                                pool.wait_ge(*following(pool, "state_ready", 1))
                            ins = pool.tensor_tensor(gla_s[:, d, :, :], gla_s[:, d, :, :],
                                                     over(ecol[:, s % 2, :, d], DV), ALU.mult)
                            ins.then_inc(*counts("scaled_state"))

                @block.vector
                def _(dve):
                    for t in range(NT):
                        for d in range(2):
                            dve.wait_ge(*made(("lg", t, d)))
                            s = bank(("lg", t, d))
                            dve.tensor_copy(logdec[:, d, t, :], s).then_inc(*reads(("lg", t, d)))
                            dve.wait_ge(*read(("lg", t, d)))
                    dve.scalar_tensor_tensor(out=soft, in0=logdec, scalar=-1.0, in1=logdec,
                                             op0=ALU.mult, op1=ALU.max).then_inc(*counts("abs_ready"))
                    dve.wait_ge(*counted("abs_ready"))
                    dve.tensor_scalar(logdec, logdec, 0.0, 1.0 / GATE_NORM, ALU.min, ALU.mult).then_inc(*counts("dve_step"))
                    dve.wait_ge(*counted("dve_step"))
                    dve.wait_ge(*following(dve, "soft_ready"))
                    dve.scalar_tensor_tensor(out=logdec, in0=soft, scalar=-1.0 / GATE_NORM, in1=logdec,
                                             op0=ALU.mult, op1=ALU.add).then_inc(*counts("logdecay_ready"))
                    dve.wait_ge(*counted("logdecay_ready"))
                    for s, (d, t) in enumerate(SCAN):
                        dve.wait_ge(*made(("b", s)))
                        dve.tensor_scalar(clamped, bank(("b", s)), CLAMP, -CLAMP, ALU.min, ALU.max).then_inc(*reads(("b", s)))
                        dve.wait_ge(*read(("b", s)))
                        dve.tensor_copy(stat_b[:, 0:1], cst[:, 0:1]).then_inc(*counts("clamped_ready"))
                        dve.wait_ge(*following(dve, "decay_ready"))
                        dve.tensor_tensor(qt, q_b[:, t, :, :], up.rearrange("p (h d) -> p h d", d=DK), ALU.mult).then_inc(*counts("dve_step"))
                        dve.wait_ge(*counted("dve_step"))
                        dve.tensor_tensor(kt, k_b[:, t, :, :], down.rearrange("p (h d) -> p h d", d=DK), ALU.mult).then_inc(*counts("qk_ready"))
                        dve.wait_ge(*counted("qk_ready"))
                        dve.wait_ge(*made(("ktT", s)))
                        dve.tensor_copy(ktT, quad(bank(("ktT", s)))).then_inc(*reads(("ktT", s)))
                        dve.wait_ge(*read(("ktT", s)))
                        dve.wait_ge(*made(("att", s)))
                        dve.tensor_tensor(att, quad(bank(("att", s))), each(cum(d), H_B), ALU.mult).then_inc(*reads(("att", s)))
                        dve.wait_ge(*read(("att", s)))
                        for g in range(2):
                            out = o_b[:, t, 512 * g:512 * g + 512]
                            dve.wait_ge(*made(("o", s, g)))
                            p = bank(("o", s, g))
                            if s in FIRST:
                                dve.tensor_copy(out, p).then_inc(*reads(("o", s, g)))
                                dve.wait_ge(*read(("o", s, g)))
                            else:
                                dve.tensor_tensor(out, p, out, ALU.add).then_inc(*reads(("o", s, g)))
                                dve.wait_ge(*read(("o", s, g)))
                        if s not in LAST:
                            dve.wait_ge(*read(("ec", s)))
                            for g in range(2):
                                dve.wait_ge(*made(("ds", s, g)))
                                p = bank(("ds", s, g)).rearrange("p (h d) -> p h d", d=DV)
                                e = over(ecol[:, s % 2, 2 * g:2 * g + 2, 1 - d], DV)
                                if t == 0:
                                    dve.tensor_tensor(gla_p[:, d, 2 * g:2 * g + 2, :], p, e, ALU.mult).then_inc(*reads(("ds", s, g)))
                                    dve.wait_ge(*read(("ds", s, g)))
                                else:
                                    st = gla_s[:, d, 2 * g:2 * g + 2, :]
                                    dve.tensor_tensor(st, p, st, ALU.add).then_inc(*reads(("ds", s, g)))
                                    dve.wait_ge(*read(("ds", s, g)))
                                    ins = dve.tensor_tensor(st, st, e, ALU.mult)
                                    if g:
                                        ins.then_inc(*counts("state_ready"))
                                        dve.wait_ge(*counted("state_ready"))
                                    else:
                                        ins.then_inc(*counts("dve_step"))
                                        dve.wait_ge(*counted("dve_step"))
                    dve.tensor_copy(stat_b[:, 0:1], cst[:, 0:1]).then_inc(*counts("o_ready"))
                    dve.wait_ge(*counted("o_ready"))
                    dve.wait_ge(*following(dve, "sq_ready"))
                    dve.tensor_reduce(stat_b, sq_b, AX_X, ALU.add).then_inc(*counts("dve_step"))
                    dve.wait_ge(*counted("dve_step"))
                    dve.tensor_scalar(stat_b, stat_b, 1.0 / DV, EPS, ALU.mult, ALU.add).then_inc(*counts("stat_ready"))
                    dve.wait_ge(*counted("stat_ready"))
                    dve.wait_ge(*following(dve, "head_root"))
                    dve.reciprocal(stat_b, stat_b).then_inc(*counts("dve_step"))
                    dve.wait_ge(*counted("dve_step"))
                    heads = o_b.rearrange("p t (h d) -> p (t h) d", d=DV)
                    dve.tensor_tensor(heads, heads, over(stat_b, DV), ALU.mult).then_inc(*counts("dve_step"))
                    dve.wait_ge(*counted("dve_step"))
                    for i in range(2):
                        for t in range(NT):
                            dve.wait_ge(*read((("og", i), t)))
                    dve.tensor_tensor(o_b, o_b, og, ALU.mult).then_inc(*counts("dve_step"))
                    dve.wait_ge(*counted("dve_step"))

                @block.sync
                def _(sp):
                    for d in range(2):
                        sp.dma_start(gla_s[:, d, :, :], state_gla[bass.ds(l, 1), d].rearrange("a h k v -> k (a h) v")
                                     ).then_inc(sem["gla_state_in"], 16)
                    load_weights(sp, l, W_AO[1] + RING, W_BO + 2)
                    for d in range(2):
                        for g in range(2):
                            sp.wait_ge(*read(("ds", d, g)))
                        sp.dma_start(new_gla[bass.ds(l, 1), d].rearrange("a h k v -> k (a h) v"), gla_p[:, d, :, :]
                                     ).then_inc(sem["stored"], 16)
                    load_weights(sp, l, W_BO + 2, W_BO + RING)
                    sp.wait_ge(*following(sp, "stored", 32))

            oT_b = carve(3072, KD, T)
            with nc.Block() as block:
                @block.tensor
                def _(pe):
                    to_features(pe, "ob", o_b)
                    project_pe(pe, (W_BO, W_BO + 1), "bo", oT_b, "ob")

                @block.vector
                def _(dve):
                    features_dve(dve, "ob", oT_b, V_BON)
                    gated_sum(dve, "bo", "gb", gT_b, False)

                @block.sync
                def _(sp):
                    load_weights(sp, l, W_BO + RING, W_Z[0] + RING)

            z_c = carve(0, NT, D)
            xpad = carve(3072, NX, XW)
            xbc = carve(7776, NX, YW)
            xs = carve(12432, NT, D)
            b_tok = carve(15504, NT, G_C, N_ST)
            y_c = carve(16272, NT, D)
            xdt = carve(19344, H_C, HP)
            xw = carve(20368, H_C, HP)
            diff = carve(21392, 2, 512)
            decayed = carve(22416, H_C, P)
            cbm = carve(24464, G_C, P)
            dt = carve(24720, NT, 32)
            dta = carve(24816, NT, 32)
            dtt = carve(24912, NT, 32)
            aexp = carve(25008, 32)
            ex2 = carve(25040, 2, 4, H_C)
            stat_c = carve(25170, NT)
            ssd_in = carve(3072, 2, KD, P)
            ssd_s = carve(5120, 2, H_C * HP)
            ssd_p = carve(7168, H_C * HP)
            ssd_out = (carve(8192, KD, P), carve(25200, KD, P))
            ssd_tmp = carve(9216, 512)
            gT_c = [carve(9728 + T * k, T) for k in range(3)] + [carve(3072 + T * k, T) for k in range(KD - 3)]
            mod_sums_c = carve(19344, 2, 512)
            OUT_COL = (0, X_S - X_P, X_S - X_P + P)
            with nc.Block() as block:
                @block.tensor
                def _(pe):
                    for i in range(2):
                        token_major(pe, W_Z[i], ("z", i))
                        modulation_sums_pe(pe, ADA_FIRST + 3 + i, mod_sums_c)
                    for i in range(3):
                        feature_major(pe, W_CX[i], ("cx", i), hT)
                        if i == 0:
                            modulation_sums_pe(pe, ADA_FIRST + 5, mod_sums_c)
                    for q in range(2):
                        for j in range(4 * q, 4 * q + 4):
                            pe.wait_ge(*following(pe, "xbc_ready"))
                        for t in range(NT):
                            transposed(pe, ("xs", t, q), [xbc[:, j, OUT_COL[t]:OUT_COL[t] + P] for j in range(4 * q, 4 * q + 4)])
                    for j in range(8, NX):
                        pe.wait_ge(*following(pe, "xbc_ready"))
                    for t in range(NT):
                        transposed(pe, ("bt", t), [xbc[:, 8 + g, OUT_COL[t]:OUT_COL[t] + P] for g in range(G_C)])

                @block.scalar
                def _(act):
                    for i in range(2):
                        for t in range(NT):
                            act.wait_ge(*made((("z", i), t)))
                            s = bank((("z", i), t))
                            act.activation(z_c[:, t, 512 * i:512 * i + 512], s, ACT.Silu).then_inc(*reads((("z", i), t)))
                            act.wait_ge(*read((("z", i), t)))
                    for i in range(3):
                        for j in range(4):
                            act.wait_ge(*made((("cx", i), j)))
                            s = bank((("cx", i), j))
                            act.activation(xpad[:, 4 * i + j, X_P:X_P + P], s[:, 0:P], ACT.Copy).then_inc(*counts("act_step"))
                            act.wait_ge(*counted("act_step"))
                            act.activation(xpad[:, 4 * i + j, X_S:X_S + 2 * P], s[:, P:T], ACT.Copy).then_inc(*reads((("cx", i), j)))
                            act.wait_ge(*read((("cx", i), j)))
                    for j in range(NX):
                        act.wait_ge(*following(act, "conv_ready"))
                        act.activation(xbc[:, j, :], xbc[:, j, :], ACT.Silu, bias=vec[:, V_CB + j:V_CB + j + 1]).then_inc(*counts("xbc_ready"))
                    act.wait_ge(*following(act, "abs_ready"))
                    act.activation(dtt, dtt, ACT.Exp, scale=-1.0).then_inc(*counts("act_step"))
                    act.wait_ge(*counted("act_step"))
                    act.activation(dtt, dtt, ACT.Ln, bias=1.0).then_inc(*counts("act_step"))
                    act.wait_ge(*counted("act_step"))
                    act.activation(aexp, row[:, R_ALOG:R_ALOG + 32], ACT.Exp).then_inc(*counts("soft_ready"))

                @block.vector
                def _(dve):
                    for a, b in ((0, X_P), (X_P + P, X_S), (XW - PAD, XW)):
                        dve.memset(xpad[:, :, a:b], 0.0).then_inc(*counts("dve_step"))
                        dve.wait_ge(*counted("dve_step"))
                    dve.tensor_tensor(dt, dtraw[:, :, :], each(row[:, R_DTB:R_DTB + 32], NT), ALU.add).then_inc(*counts("dve_step"))
                    dve.wait_ge(*counted("dve_step"))
                    dve.scalar_tensor_tensor(out=dtt, in0=dt, scalar=-1.0, in1=dt, op0=ALU.mult, op1=ALU.max).then_inc(*counts("abs_ready"))
                    dve.wait_ge(*counted("abs_ready"))
                    dve.tensor_scalar(dt, dt, 0.0, None, ALU.max).then_inc(*counts("dve_step"))
                    dve.wait_ge(*counted("dve_step"))
                    for n in range(ADA_FIRST + 3, ADA_LATE):
                        modulation_sums(dve, n, mod_sums_c)
                        if n < ADA_LATE - 1:
                            modulation_dve(dve, n)
                    for j in range(NX):
                        dve.wait_ge(*read((("cx", j // 4), j % 4)))
                        if j == 4:
                            modulation_dve(dve, ADA_LATE - 1)
                            amplitude(dve, 1, V_N2)
                        for k in range(TAPS):
                            w = vec[:, V_CW + NX * k + j:V_CW + NX * k + j + 1]
                            src = xpad[:, j, k:k + YW]
                            if k == 0:
                                ins = dve.tensor_scalar(xbc[:, j, :], src, w, None, ALU.mult)
                            else:
                                ins = dve.scalar_tensor_tensor(out=xbc[:, j, :], in0=src, scalar=w, in1=xbc[:, j, :],
                                                               op0=ALU.mult, op1=ALU.add)
                            ins.then_inc(*counts("conv_ready" if k == TAPS - 1 else "dve_step"))
                            dve.wait_ge(*counted("conv_ready" if k == TAPS - 1 else "dve_step"))
                    for q in range(2):
                        for t in range(NT):
                            dve.wait_ge(*made(("xs", t, q)))
                            dve.tensor_copy(xs[:, t, 512 * q:512 * q + 512], bank(("xs", t, q))).then_inc(*reads(("xs", t, q)))
                            dve.wait_ge(*read(("xs", t, q)))
                    for t in range(NT):
                        dve.wait_ge(*made(("bt", t)))
                        dve.tensor_copy(b_tok[:, t, :, :], quad(bank(("bt", t))[:, 0:G_C * P])).then_inc(*reads(("bt", t)))
                        dve.wait_ge(*read(("bt", t)))
                    dve.wait_ge(*following(dve, "soft_ready"))
                    dve.tensor_tensor(dt, dt, dtt, ALU.add).then_inc(*counts("dve_step"))
                    dve.wait_ge(*counted("dve_step"))
                    dve.scalar_tensor_tensor(out=dta, in0=dt, scalar=-1.0, in1=each(aexp, NT),
                                             op0=ALU.mult, op1=ALU.mult).then_inc(*counts("dve_step"))
                    dve.wait_ge(*counted("dve_step"))

                @block.sync
                def _(sp):
                    load_weights(sp, l, W_Z[0] + RING, W_GC + RING)

            with nc.Block() as block:
                @block.tensor
                def _(pe):
                    gate_pe(pe, W_GC, "gc", 0)
                    pe.wait_ge(*following(pe, "ssd_state_in", 32))
                    for d in range(2):
                        for q in range(2):
                            transposed(pe, ("si", d, q), [ssd_in[:, d, 4 * q + i, :] for i in range(4)])
                    for s, (d, t) in enumerate(SCAN):
                        col = slice(OUT_COL[t], OUT_COL[t] + P)
                        a = dta[:, t, H_C * d:H_C * d + H_C]
                        out = claim(pe, ("sc", s))
                        for i, m in enumerate((rel(d), cum(d), aft(d), ones)):
                            ins = pe.matmul(out[:, H_C * i:H_C * i + H_C], m, a, start=True, stop=True)
                        ins.then_inc(*makes(("sc", s)))
                        out = claim(pe, ("cb", s))
                        for g in range(G_C):
                            ins = pe.matmul(out[:, P * g:P * g + P], xbc[:, 8 + g, col], xbc[:, 10 + g, col],
                                            start=True, stop=True)
                        ins.then_inc(*makes(("cb", s)))
                        for q in range(4):
                            out = claim(pe, ("ai", s, q))
                            for i in range(4):
                                h = H_C * d + 4 * q + i
                                ins = pe.matmul(out[:, P * i:P * i + P], dta[:, t, h:h + 1].broadcast_to([P, P]), rel(d),
                                                start=True, stop=True)
                            ins.then_inc(*makes(("ai", s, q)))
                        if t:
                            for g in range(G_C):
                                if s in FIRST:
                                    pe.wait_ge(*read(("si", d, g)))
                                else:
                                    pe.wait_ge(*read(("ds", s - 2, g)))
                                if s not in FIRST and g == 0:
                                    pe.wait_ge(*following(pe, "state_ready"))
                                pe.matmul(claim(pe, ("yo", s, g)), xbc[:, 10 + g, col],
                                          ssd_s[:, d, 512 * g:512 * g + 512], start=True, stop=True).then_inc(*makes(("yo", s, g)))
                        if s + 1 < len(SCAN):
                            gate_pe(pe, W_GC, "gc", s + 1)
                        pe.wait_ge(*following(pe, "xw_ready"))
                        if s not in LAST:
                            for g in range(G_C):
                                pe.matmul(claim(pe, ("ds", s, g)), b_tok[:, t, g, :],
                                          xw.rearrange("p h d -> p (h d)")[:, 512 * g:512 * g + 512],
                                          start=True, stop=True).then_inc(*makes(("ds", s, g)))
                        for g in range(G_C):
                            pe.wait_ge(*following(pe, "mask_ready", 2))
                            out = claim(pe, ("yd", s, g))
                            for i in range(8):
                                h = 8 * g + i
                                ins = pe.matmul(out[:, HP * i:HP * i + HP], decayed[:, h, :], xdt[:, h, :],
                                                start=True, stop=True)
                            ins.then_inc(*makes(("yd", s, g)))
                        if t == 0:
                            for g in range(G_C):
                                pe.wait_ge(*read(("ds", s, g)))
                            for q in range(2):
                                transposed(pe, ("so", d, q), [ssd_p[:, 512 * q + P * i:512 * q + P * i + P] for i in range(4)])
                    for g in range(len(SCAN), KD):
                        gate_pe(pe, W_GC, "gc", g)

                @block.scalar
                def _(act):
                    gate_tile_act(act, "gc", gT_c, 0)
                    for s, (d, t) in enumerate(SCAN):
                        act.wait_ge(*made(("sc", s)))
                        p = bank(("sc", s)).rearrange("p (a h) -> p a h", h=H_C)
                        act.activation(ex2[:, s % 2, 0, :], p[:, 0, :], ACT.Copy).then_inc(*counts("act_step"))
                        act.wait_ge(*counted("act_step"))
                        act.activation(ex2[:, s % 2, 1:4, :], p[:, 1:4, :], ACT.Exp).then_inc(*reads(("sc", s)))
                        act.wait_ge(*read(("sc", s)))
                        for q in range(4):
                            act.wait_ge(*following(act, "diff_ready"))
                            act.activation(diff[:, q % 2, :], diff[:, q % 2, :], ACT.Exp).then_inc(*counts("decayed_ready"))
                        if s + 1 < len(SCAN):
                            if s == 2:
                                for i in range(4):
                                    act.wait_ge(*read(("si", i // 2, i % 2)))
                            gate_tile_act(act, "gc", gT_c, s + 1)
                    for t in range(NT):
                        act.wait_ge(*following(act, "y_ready"))
                        act.activation(xs[:, t, :], y_c[:, t, :], ACT.Square, accum_out=stat_c[:, t:t + 1]).then_inc(*counts("sq_ready"))
                    act.wait_ge(*following(act, "stat_ready"))
                    act.activation(stat_c, stat_c, ACT.Sqrt).then_inc(*counts("head_root"))
                    for g in range(len(SCAN), KD):
                        gate_tile_act(act, "gc", gT_c, g)

                @block.gpsimd
                def _(pool):
                    for t in range(NT):
                        ins = pool.tensor_tensor(y_c[:, t, :].rearrange("p (h d) -> p h d", d=HP),
                                                 xs[:, t, :].rearrange("p (h d) -> p h d", d=HP),
                                                 over(row[:, R_D:R_D + H_C], HP), ALU.mult)
                    ins.then_inc(*counts("yoff_ready"))
                    for s, (d, t) in enumerate(SCAN):
                        pool.wait_ge(*read(("sc", s)))
                        if s:
                            pool.wait_ge(*made(("yd", s - 1, 1)))
                        pool.tensor_tensor(xdt, xs[:, t, :].rearrange("p (h d) -> p h d", d=HP),
                                            over(dt[:, t, H_C * d:H_C * d + H_C], HP), ALU.mult).then_inc(*counts("pool_step"))
                        pool.wait_ge(*counted("pool_step"))
                        pool.tensor_tensor(xw, xdt, over(ex2[:, s % 2, 2, :], HP), ALU.mult).then_inc(*counts("xw_ready"))

                @block.vector
                def _(dve):
                    dve.wait_ge(*following(dve, "yoff_ready"))
                    for d in range(2):
                        for q in range(2):
                            dve.wait_ge(*made(("si", d, q)))
                            dve.tensor_copy(ssd_s[:, d, 512 * q:512 * q + 512], bank(("si", d, q))).then_inc(*reads(("si", d, q)))
                            dve.wait_ge(*read(("si", d, q)))
                    for s, (d, t) in enumerate(SCAN):
                        dve.wait_ge(*made(("cb", s)))
                        dve.tensor_tensor(cbm, quad(bank(("cb", s))[:, 0:G_C * P]), each(cum(d), G_C), ALU.mult).then_inc(*reads(("cb", s)))
                        dve.wait_ge(*read(("cb", s)))
                        dve.wait_ge(*read(("sc", s)))
                        for q in range(5):
                            if q < 4:
                                dve.wait_ge(*made(("ai", s, q)))
                                dve.tensor_tensor(quad(diff[:, q % 2, :]), quad(bank(("ai", s, q))),
                                                  over(ex2[:, s % 2, 0, 4 * q:4 * q + 4], P), ALU.subtract).then_inc(*reads(("ai", s, q)))
                                dve.wait_ge(*read(("ai", s, q)))
                                dve.tensor_scalar(diff[:, q % 2, :], diff[:, q % 2, :], 0.0, None, ALU.min).then_inc(*counts("diff_ready"))
                            if q:
                                r = q - 1
                                dve.wait_ge(*following(dve, "decayed_ready"))
                                dve.tensor_tensor(decayed[:, 4 * r:4 * r + 4, :], quad(diff[:, r % 2, :]),
                                                  each(cbm[:, r // 2, :], 4), ALU.mult).then_inc(*counts("mask_ready"))
                                dve.wait_ge(*counted("mask_ready"))
                        for g in range(G_C):
                            out = y_c[:, t, 512 * g:512 * g + 512]
                            if t:
                                dve.wait_ge(*made(("yo", s, g)))
                                dve.tensor_tensor(ssd_tmp.rearrange("p (h d) -> p h d", d=HP),
                                                  bank(("yo", s, g)).rearrange("p (h d) -> p h d", d=HP),
                                                  over(ex2[:, s % 2, 1, 8 * g:8 * g + 8], HP), ALU.mult).then_inc(*counts("dve_step"))
                                dve.wait_ge(*counted("dve_step"))
                                dve.tensor_tensor(out, ssd_tmp, out, ALU.add).then_inc(*reads(("yo", s, g)))
                                dve.wait_ge(*read(("yo", s, g)))
                            dve.wait_ge(*made(("yd", s, g)))
                            dve.tensor_tensor(out, bank(("yd", s, g)), out, ALU.add).then_inc(*reads(("yd", s, g)))
                            dve.wait_ge(*read(("yd", s, g)))
                        if s not in LAST:
                            for g in range(G_C):
                                dve.wait_ge(*made(("ds", s, g)))
                                p = bank(("ds", s, g))
                                if t == 0:
                                    dve.tensor_copy(ssd_p[:, 512 * g:512 * g + 512], p).then_inc(*reads(("ds", s, g)))
                                    dve.wait_ge(*read(("ds", s, g)))
                                else:
                                    st = ssd_s[:, d, 512 * g:512 * g + 512]
                                    sv = st.rearrange("p (h d) -> p h d", d=HP)
                                    dve.tensor_tensor(sv, sv, over(ex2[:, s % 2, 3, 8 * g:8 * g + 8], HP), ALU.mult).then_inc(*counts("dve_step"))
                                    dve.wait_ge(*counted("dve_step"))
                                    dve.tensor_tensor(st, p, st, ALU.add).then_inc(*reads(("ds", s, g)))
                                    dve.wait_ge(*read(("ds", s, g)))
                            if t:
                                dve.tensor_copy(stat_c[:, 0:1], cst[:, 0:1]).then_inc(*counts("state_ready"))
                                dve.wait_ge(*counted("state_ready"))
                        if t == 0:
                            for q in range(2):
                                dve.wait_ge(*made(("so", d, q)))
                                dve.tensor_copy(ssd_out[d][:, 4 * q:4 * q + 4, :], quad(bank(("so", d, q)))).then_inc(*reads(("so", d, q)))
                                dve.wait_ge(*read(("so", d, q)))
                    for t in range(NT):
                        dve.tensor_tensor(y_c[:, t, :], y_c[:, t, :], z_c[:, t, :], ALU.mult).then_inc(*counts("y_ready"))
                        dve.wait_ge(*counted("y_ready"))
                    for t in range(NT):
                        dve.wait_ge(*following(dve, "sq_ready"))
                    dve.tensor_scalar(stat_c, stat_c, 1.0 / D, EPS, ALU.mult, ALU.add).then_inc(*counts("stat_ready"))
                    dve.wait_ge(*counted("stat_ready"))
                    dve.wait_ge(*following(dve, "head_root"))
                    dve.reciprocal(stat_c, stat_c).then_inc(*counts("dve_step"))
                    dve.wait_ge(*counted("dve_step"))
                    for t in range(NT):
                        dve.tensor_scalar(y_c[:, t, :], y_c[:, t, :], stat_c[:, t:t + 1], None, ALU.mult).then_inc(*counts("dve_step"))
                        dve.wait_ge(*counted("dve_step"))

                @block.sync
                def _(sp):
                    for d in range(2):
                        sp.dma_start(ssd_in[:, d, :, :], state_ssd[bass.ds(l, 1), d].rearrange("a (j q) n -> q (a j) n", q=P)
                                     ).then_inc(sem["ssd_state_in"], 16)
                    load_weights(sp, l, W_GC + RING, W_CO + 2)
                    for d in range(2):
                        for q in range(2):
                            sp.wait_ge(*read(("so", d, q)))
                        sp.dma_start(new_ssd[bass.ds(l, 1), d].rearrange("a (j q) n -> q (a j) n", q=P), ssd_out[d]
                                     ).then_inc(sem["stored"], 16)
                    load_weights(sp, l, W_CO + 2, W_CO + RING)
                    sp.wait_ge(*following(sp, "stored", 32))

            oT_c = carve(5120, KD, T)
            with nc.Block() as block:
                @block.tensor
                def _(pe):
                    to_features(pe, "oc", y_c)
                    project_pe(pe, (W_CO, W_CO + 1), "co", oT_c, "oc")
                    pe.wait_ge(*following(pe, "merged_ready"))
                    for i in range(2):
                        feature_major(pe, W_OUT + i, ("out", i), mT)

                @block.vector
                def _(dve):
                    features_dve(dve, "oc", oT_c, V_CN)
                    gated_sum(dve, "co", "gc", gT_c, False)
                    dve.tensor_copy(stat_c[:, 0:1], cst[:, 0:1]).then_inc(*counts("merged_ready"))
                    dve.wait_ge(*counted("merged_ready"))
                    for i in range(2):
                        for j in range(4):
                            dve.wait_ge(*made((("out", i), j)))
                            s = bank((("out", i), j))
                            k = 4 * i + j
                            for ts, c in COND:
                                ins = dve.scalar_tensor_tensor(out=xT[:, k, ts], in0=s[:, ts], scalar=mod[:, 2, k, c:c + 1],
                                                               in1=xT[:, k, ts], op0=ALU.mult, op1=ALU.add)
                                if c == 0:
                                    ins.then_inc(*counts("dve_step"))
                                    dve.wait_ge(*counted("dve_step"))
                            ins.then_inc(*reads((("out", i), j)))
                            dve.wait_ge(*read((("out", i), j)))

                @block.sync
                def _(sp):
                    load_weights(sp, l, W_CO + RING, W_OUT + 2 + RING)

            srt = carve(0, KD, PAIRS + SLOTS)
            ys = carve(6912, KD, PAIRS + SLOTS)
            outs = carve(0, CC, D)
            pick = carve(13824, NT, PAIRS)
            pick_w = carve(16128, NT, PAIRS)
            spread = carve(18432, CC, T)
            hc = carve(20736, KD, SLOTS)
            hidden = carve(21504, DE // P, SLOTS)
            silc = carve(21888, DE // P, SLOTS)
            second = carve(22272, PAIRS)
            iota_sb = carve(23040, PAIRS)
            late_rows = carve(23808, N_ADA - ADA_LATE, 512)
            h_tok = mT[:, :, :].rearrange("p k t -> p (k t)").rearrange("p (t d) -> p t d", d=D)
            score = carve(25600, NT, NE)
            sel = carve(25648, NT, NE)
            pairs6 = carve(25696, NT * NG, 6)
            gsum = carve(25768, NT, NG)
            gmax = carve(25780, NT)
            genc = carve(25784, NT, NG)
            gone = carve(25796, NT, NG)
            enc = carve(25808, NT, NE)
            one = carve(25856, 2, NT, NE)
            chosen = carve(25952, NT, NE)
            below = carve(26000, NT, NE)
            gate = carve(26048, NT, NE)
            place = carve(26096, NT, NE)
            load = carve(26144, NE)
            gate_over = carve(26160, NT, NE)
            first_col = carve(26208, NE + 1)
            at = carve(26228, NT, 2)
            weight = carve(26234, NT, 2)
            B_W1, B_W3, B_Y = 0, 1, 2
            with nc.Block() as block:
                base = {}

                @block.tensor
                def _(pe):
                    modulation_pe(pe, ADA_LATE)
                    square_sum(pe, "n2", sq_x, KD)
                    modulation_pe(pe, ADA_LATE + 1)
                    pe.wait_ge(*following(pe, "h_ready", 2))
                    out = claim(pe, "route")
                    for t in range(NT):
                        ins = matmuls(pe, out[:, NE * t:NE * t + NE], [(hT[:, k, tok(t)], rw[:, k, :]) for k in range(KD)])
                    ins.then_inc(*makes("route"))
                    for t in range(NT):
                        for q in range(2):
                            transposed(pe, ("ht", t, q), [hT[:, 4 * q + i, tok(t)] for i in range(4)])
                    for n in range(ADA_LATE, N_ADA):
                        modulation_features_pe(pe, n, late_rows[:, n - ADA_LATE, :])
                    pe.wait_ge(*following(pe, "chosen_ready"))
                    out = claim(pe, "place")
                    for t in range(NT):
                        matmuls(pe, out[:, NE * t:NE * t + NE], [(ones, chosen[:, u, :]) for u in range(t)]
                                + [(aft(1), chosen[:, t, :])])
                    for i, x in enumerate((below, chosen)):
                        ins = matmuls(pe, out[:, NE * (NT + i):NE * (NT + i) + NE], [(ones, x[:, u, :]) for u in range(NT)])
                    ins.then_inc(*makes("place"))
                    for t in range(NT):
                        for q in range(2):
                            pe.wait_ge(*read(("ht", t, q)))
                    for g in range(2):
                        pe.wait_ge(*following(pe, "picked"))
                        for d in range(KD):
                            matmuls(pe, claim(pe, ("srt", d, g))[:, 0:PAIRS // 2],
                                    [(h_tok[:, t, P * d:P * d + P], pick[:, t, PAIRS // 2 * g:PAIRS // 2 * (g + 1)])
                                     for t in range(NT)]).then_inc(*makes(("srt", d, g)))
                    pe.wait_ge(*following(pe, "picked"))
                    for c in range(CC):
                        transposed(pe, ("spread", c), [pick_w[:, t, P * c:P * c + P] for t in range(NT)])
                    for b in (B_W1, B_W3, B_Y, B_Y + 1):
                        pe.wait_ge(psum_free[b], uses[b])
                    base.update({b: uses[b] for b in range(8)})

                    def hidden_pe(e):
                        pe.wait_ge(sem["tokens_in"], e + 1)
                        for i, b in ((0, B_W1), (1, B_W3)):
                            pe.wait_ge(w_loaded[i], e * 16 + 16 * (W_MOE // RING + 1))
                            pe.wait_ge(psum_free[b], e + base[b])
                            w = chunk(i, KD, DE)
                            for f in range(DE // P):
                                ins = matmuls(pe, ps[:, b, SLOTS * f:SLOTS * f + SLOTS],
                                              [(w[:, k, P * f:P * f + P], hc[:, k, :]) for k in range(KD)])
                            ins.then_inc(psum_full[b], 1)

                    def output_pe(n, place=2):
                        w2 = chunk(place, DE // P, D)
                        pe.wait_ge(w_loaded[place], n * 16 + 16 * (W_MOE // RING + (place != 2)))
                        pe.wait_ge(psum_free[B_W3], n + base[B_W3])
                        for g in range(2):
                            pe.wait_ge(psum_free[B_Y + g], n + (base[B_Y + g] - 1))
                            for i in range(4):
                                d = 4 * g + i
                                ins = matmuls(pe, ps[:, B_Y + g, SLOTS * i:SLOTS * i + SLOTS],
                                              [(w2[:, k, P * d:P * d + P], hidden[:, k, :]) for k in range(DE // P)])
                            ins.then_inc(psum_full[B_Y + g], 1)

                    hidden_pe(0)
                    with pe.Fori(1, NE) as e:
                        hidden_pe(e)
                        output_pe(e)
                    output_pe(NE, 0)
                    for b in (B_W1, B_W3, B_Y, B_Y + 1):
                        uses[b] += NE
                    for b in (B_Y, B_Y + 1):
                        pe.wait_ge(psum_free[b], uses[b])
                    for c in range(CC):
                        for q in range(2):
                            transposed(pe, ("outs", c, q), [ys[:, 4 * q + i, P * c:P * c + P] for i in range(4)])
                    for q in range(2):
                        for c in range(CC):
                            pe.wait_ge(*read(("outs", c, q)))
                        for i in range(4):
                            d = 4 * q + i
                            matmuls(pe, claim(pe, ("moe", d))[:, 0:T],
                                    [(outs[:, c, P * d:P * d + P], spread[:, c, :]) for c in range(CC)]
                                    ).then_inc(*makes(("moe", d)))

                @block.sync
                def _(sp):
                    sp.dma_start(iota_sb, iota).then_inc(sem["iota_in"], 16)
                    load_weights(sp, l, W_OUT + 2 + RING, W_MOE + RING)
                    def load_expert(i, b, e, used=None, place=None):
                        sp.wait_ge(psum_full[b], (e if used is None else used) + base[b])
                        src, k, w = expert_source(i, l, e)
                        place = i if place is None else place
                        sp.dma_start(chunk(place, k, w), src).then_inc(w_loaded[place], 16)

                    load_expert(0, B_W1, 1)
                    load_expert(1, B_W3, 1)
                    with sp.Fori(2, NE) as e:
                        load_expert(0, B_W1, e)
                        load_expert(1, B_W3, e)
                        load_expert(2, B_Y + 1, e - 1)
                    load_expert(2, B_W1, NE - 1, NE, 0)

                @block.gpsimd
                def _(pool):
                    pool.memset(ys, 0.0)
                    pool.memset(srt[:, :, PAIRS:], 0.0).then_inc(*counts("cleared"))

                @block.scalar
                def _(act):
                    norm_act(act, 1, "n2", sq_x)
                    act.wait_ge(*made("route"))
                    act.activation(score, bank("route")[:, 0:NT * NE].rearrange("p (t e) -> p t e", e=NE),
                                   ACT.Sigmoid).then_inc(*reads("route"))
                    for t in range(NT):
                        for q in range(2):
                            act.wait_ge(*made(("ht", t, q)))
                            act.activation(h_tok[:, t, 512 * q:512 * q + 512], bank(("ht", t, q)),
                                           ACT.Copy).then_inc(*reads(("ht", t, q)))
                            act.wait_ge(*read(("ht", t, q)))
                    for g in range(2):
                        for d in range(KD):
                            act.wait_ge(*made(("srt", d, g)))
                            act.activation(srt[:, d, PAIRS // 2 * g:PAIRS // 2 * (g + 1)],
                                           bank(("srt", d, g))[:, 0:PAIRS // 2], ACT.Copy).then_inc(*reads(("srt", d, g)))
                            act.wait_ge(*read(("srt", d, g)))
                    for c in range(CC):
                        act.wait_ge(*made(("spread", c)))
                        act.activation(spread[:, c, :], bank(("spread", c))[:, 0:T], ACT.Copy).then_inc(*reads(("spread", c)))
                        act.wait_ge(*read(("spread", c)))
                    act.wait_ge(*following(act, "cleared"))
                    act.wait_ge(*following(act, "starts_ready"))
                    def silu(e):
                        act.wait_ge(psum_full[B_W1], e + (base[B_W1] + 1))
                        act.wait_ge(psum_free[B_W3], e + base[B_W3])
                        act.activation(silc, ps[:, B_W1, 0:DE // P * SLOTS].rearrange("p (f s) -> p f s", s=SLOTS),
                                       ACT.Silu).then_inc(psum_free[B_W1], 1)

                    def output(e, n):
                        column = act.value_load(starts[0:1, e], min_val=0, max_val=PAIRS)
                        act.wait_ge(psum_free[B_Y + 1], n + (base[B_Y + 1] - 1))
                        for g in range(2):
                            act.wait_ge(psum_full[B_Y + g], n + base[B_Y + g])
                            act.activation(ys[:, 4 * g:4 * g + 4, bass.ds(column, SLOTS)],
                                           ps[:, B_Y + g, 0:4 * SLOTS].rearrange("p (d s) -> p d s", s=SLOTS),
                                           ACT.Copy).then_inc(psum_free[B_Y + g], 1)

                    silu(0)
                    with act.Fori(1, NE) as e:
                        silu(e)
                        output(bass.ds(e - 1, 1), e)
                    output(slice(NE - 1, NE), NE)
                    act.wait_ge(sem["tokens_in"], NE + 1)
                    for c in range(CC):
                        act.wait_ge(*made(("outs", c, 1)))
                        act.activation(outs[:, c, 512:1024], bank(("outs", c, 1)), ACT.Copy).then_inc(*reads(("outs", c, 1)))
                        act.wait_ge(*read(("outs", c, 1)))

                @block.vector
                def _(dve):
                    modulation_rows_dve(dve, ADA_LATE, late_rows[:, 0, :])
                    root_mean(dve, "n2", D)
                    norm_dve(dve, 1)
                    modulation_rows_dve(dve, ADA_LATE + 1, late_rows[:, 1, :])
                    dve.wait_ge(*read("route"))

                    def step(ins):
                        ins.then_inc(*counts("dve_step"))
                        dve.wait_ge(*counted("dve_step"))

                    flat = sel.rearrange("p t (g e) -> p (t g) e", e=EG)
                    step(dve.tensor_tensor(sel, score, each(row[:, R_RB:R_RB + NE], NT), ALU.add))
                    for c, a, b, w in ((0, 0, 2, 2), (2, 0, 3, 1), (3, 1, 2, 1), (4, 0, 1, 1), (5, 2, 3, 1)):
                        step(dve.tensor_tensor(pairs6[:, :, c:c + w], flat[:, :, a:a + w], flat[:, :, b:b + w], ALU.add))
                    step(dve.tensor_reduce(gsum.rearrange("p t g -> p (t g)"), pairs6, AX_X, ALU.max))

                    def first_max(x, n, e, o):
                        rank = each(cst[:, C_RANK:C_RANK + n], NT)
                        step(dve.tensor_reduce(gmax, x, AX_X, ALU.max))
                        step(dve.tensor_tensor(e, x, over(gmax, n), ALU.is_ge))
                        step(dve.tensor_tensor(e, e, rank, ALU.mult))
                        step(dve.tensor_reduce(gmax, e, AX_X, ALU.max))
                        step(dve.tensor_tensor(o, e, over(gmax, n), ALU.is_equal))

                    first_max(gsum, NG, genc, gone)
                    inside = gone.rearrange("p t g -> p (t g)")
                    step(dve.tensor_tensor(flat, flat, over(inside, EG), ALU.mult))
                    step(dve.tensor_scalar(genc, gone, -1.0, BIG, ALU.add, ALU.mult))
                    step(dve.tensor_tensor(flat, flat, over(genc.rearrange("p t g -> p (t g)"), EG), ALU.add))
                    rank = each(cst[:, C_RANK:C_RANK + NE], NT)
                    first_max(sel, NE, enc, one[:, 0, :, :])
                    step(dve.tensor_tensor(below, over(gmax, NE), rank, ALU.is_gt))
                    step(dve.scalar_tensor_tensor(out=sel, in0=one[:, 0, :, :], scalar=-2.0 * BIG, in1=sel,
                                                  op0=ALU.mult, op1=ALU.add))
                    first_max(sel, NE, enc, one[:, 1, :, :])
                    step(dve.tensor_tensor(enc, over(gmax, NE), rank, ALU.is_gt))
                    step(dve.tensor_tensor(below, below, enc, ALU.add))
                    dve.tensor_tensor(chosen, one[:, 0, :, :], one[:, 1, :, :], ALU.add).then_inc(*counts("chosen_ready"))
                    dve.wait_ge(*counted("chosen_ready"))
                    step(dve.tensor_tensor(gate, score, chosen, ALU.mult))
                    step(dve.tensor_reduce(gmax, gate, AX_X, ALU.add))
                    step(dve.reciprocal(gmax, gmax))
                    step(dve.tensor_tensor(gate, gate, over(gmax, NE), ALU.mult))
                    for n in range(ADA_LATE, N_ADA):
                        modulation_dve(dve, n)
                    dve.wait_ge(*made("place"))
                    p = bank("place")
                    step(dve.tensor_copy(first_col[:, 0:NE], p[:, NE * NT:NE * NT + NE]))
                    step(dve.tensor_copy(load, p[:, NE * (NT + 1):NE * (NT + 1) + NE]))
                    dve.tensor_copy(place, p[:, 0:NT * NE].rearrange("p (t e) -> p t e", e=NE)).then_inc(*reads("place"))
                    dve.wait_ge(*read("place"))
                    step(dve.tensor_tensor(sel, place, each(first_col[:, 0:NE], NT), ALU.add))
                    for j in range(2):
                        step(dve.tensor_tensor(enc, sel, one[:, j, :, :], ALU.mult))
                        step(dve.tensor_reduce(at[:, :, j], enc, AX_X, ALU.add))
                    dve.wait_ge(sem["iota_in"], 16)
                    for g in range(2):
                        half = slice(PAIRS // 2 * g, PAIRS // 2 * (g + 1))
                        for t in range(NT):
                            step(dve.tensor_scalar(pick[:, t, half], iota_sb[:, half], at[:, t, 0:1], None, ALU.is_equal))
                            ins = dve.scalar_tensor_tensor(out=pick[:, t, half], in0=iota_sb[:, half], scalar=at[:, t, 1:2],
                                                           in1=pick[:, t, half], op0=ALU.is_equal, op1=ALU.add)
                        ins.then_inc(*counts("picked"))
                    step(dve.scalar_tensor_tensor(out=gate_over, in0=place, scalar=float(SLOTS), in1=gate,
                                                  op0=ALU.is_ge, op1=ALU.mult))
                    step(dve.tensor_tensor(gate, gate, gate_over, ALU.subtract))
                    for j in range(2):
                        step(dve.tensor_tensor(enc, gate, one[:, j, :, :], ALU.mult))
                        step(dve.tensor_reduce(weight[:, :, j], enc, AX_X, ALU.add))
                    step(dve.tensor_reduce(gmax[:, 0:1], load, AX_X, ALU.max))
                    step(dve.tensor_scalar(gmax[:, 1:2], gmax[:, 0:1], float(SLOTS), None, ALU.is_gt))
                    step(dve.tensor_copy(overflow[:, :], gmax[0:1, 1:2]))
                    step(dve.memset(first_col[:, NE:NE + 1], 0.0))
                    dve.tensor_copy(starts[:, :], first_col[0:1, :]).then_inc(*counts("starts_ready"))
                    dve.wait_ge(*counted("starts_ready"))
                    for t in range(NT):
                        step(dve.tensor_scalar(pick_w[:, t, :], iota_sb, at[:, t, 0:1], weight[:, t, 0:1],
                                               ALU.is_equal, ALU.mult))
                        step(dve.tensor_scalar(second, iota_sb, at[:, t, 1:2], weight[:, t, 1:2], ALU.is_equal, ALU.mult))
                        step(dve.tensor_tensor(pick_w[:, t, :], pick_w[:, t, :], second, ALU.add))
                    dve.tensor_copy(second[:, 0:1], cst[:, 0:1]).then_inc(*counts("picked"))

                    def tokens(e):
                        column = dve.value_load(starts[0:1, bass.ds(e, 1)], min_val=0, max_val=PAIRS)
                        dve.tensor_copy(hc, srt[:, :, bass.ds(column, SLOTS)]).then_inc(sem["tokens_in"], 1)

                    dve.wait_ge(*read(("srt", KD - 1, 1)))
                    dve.wait_ge(*following(dve, "cleared"))
                    tokens(0)
                    def hidden_dve(e):
                        dve.wait_ge(psum_free[B_W1], e + (base[B_W1] + 1))
                        dve.tensor_tensor(hidden, ps[:, B_W3, 0:DE // P * SLOTS].rearrange("p (f s) -> p f s", s=SLOTS),
                                          silc, ALU.mult).then_inc(psum_free[B_W3], 1)

                    dve.wait_ge(psum_full[B_W3], base[B_W3] + 1)
                    tokens(1)
                    hidden_dve(0)
                    with dve.Fori(1, NE) as e:
                        dve.wait_ge(psum_full[B_W3], e + (base[B_W3] + 1))
                        tokens(e + 1)
                        dve.wait_ge(psum_full[B_Y + 1], e + base[B_Y + 1])
                        hidden_dve(e)
                    dve.wait_ge(sem["tokens_in"], NE + 1)
                    for c in range(CC):
                        dve.wait_ge(*made(("outs", c, 0)))
                        dve.tensor_copy(outs[:, c, 0:512], bank(("outs", c, 0))).then_inc(*reads(("outs", c, 0)))
                        dve.wait_ge(*read(("outs", c, 0)))
                    for d in range(KD):
                        dve.wait_ge(*made(("moe", d)))
                        s = bank(("moe", d))
                        for ts, c in COND:
                            ins = dve.scalar_tensor_tensor(out=xT[:, d, ts], in0=s[:, ts], scalar=mod[:, 5, d, c:c + 1],
                                                           in1=xT[:, d, ts], op0=ALU.mult, op1=ALU.add)
                        ins.then_inc(*reads(("moe", d)))
                        dve.wait_ge(*read(("moe", d)))

            clear_counts(loads=True)

            acc = carve(0, NT, D)
            hid = carve(3072, DE // P, T)
            sil = carve(4608, DE // P, T)
            moved = carve(6600, 512)
            over_w = carve(7168, 3, 4096)
            B_HID, B_OUT, N_OUT = 0, 4, 3
            BANKS = B_OUT + N_OUT
            with nc.Block() as block:
                @block.tensor
                def _(pe):
                    with pe.If(pe.value_load(overflow[0:1, 0:1], min_val=0, max_val=1) > 0):
                        for b in range(BANKS):
                            claim(pe, ("first", b), b)
                            pe.matmul(ps[0:2, b, 0:2], ident[:, 0:2], ident[:, 0:2], start=True, stop=True
                                      ).then_inc(*makes(("first", b)))
                        with pe.Fori(0, NE) as e:
                            def slot(i):
                                pe.wait_ge(over_loaded[i], e * 16 + 16)
                                k = (KD, KD, DE // P)[i]
                                return over_w[:, i, :].rearrange("p (k w) -> p k w", k=k)

                            w1 = slot(0)
                            w3 = slot(1)
                            for f in range(DE // P):
                                for i, w in ((0, w1), (1, w3)):
                                    b = B_HID + 2 * (f % 2) + i
                                    pe.wait_ge(psum_free[b], e * 2 + (1 + f // 2))
                                    matmuls(pe, ps[:, b, 0:T], [(w[:, k, P * f:P * f + P], hT[:, k, :]) for k in range(KD)]
                                            ).then_inc(psum_full[b], 1)
                            w2 = slot(2)
                            pe.wait_ge(sem["hidden_ready"], e * 4 + 4)
                            for n in range(2 * NT):
                                b = B_OUT + n % N_OUT
                                pe.wait_ge(psum_free[b], e * 2 + (1 + n // N_OUT))
                                matmuls(pe, ps[:, b, :], [(hid[:, k, tok(n // 2)], w2[:, k, 512 * (n % 2):512 * (n % 2) + 512])
                                                          for k in range(DE // P)]).then_inc(psum_full[b], 1)
                        for b in range(BANKS):
                            uses[b] += 2 * NE
                        pe.wait_ge(*following(pe, "moe_ready"))
                        to_features(pe, "mo", acc)

                @block.sync
                def _(sp):
                    with sp.If(l < DEPTH - 1):
                        load_weights(sp, nc.s_assert_within(l + 1, 0, DEPTH - 1), 0, RING)
                    with sp.If(sp.value_load(overflow[0:1, 0:1], min_val=0, max_val=1) > 0):
                        for i in range(3):
                            src, k, w = expert_source(i, l, 0)
                            sp.dma_start(over_w[:, i, :].rearrange("p (k w) -> p k w", k=k), src).then_inc(over_loaded[i], 16)
                        with sp.Fori(1, NE) as e:
                            for i, b in enumerate((B_HID + 2, B_HID + 3, B_OUT + N_OUT - 1)):
                                sp.wait_ge(psum_full[b], e * 2 + 1)
                                src, k, w = expert_source(i, l, e)
                                sp.dma_start(over_w[:, i, :].rearrange("p (k w) -> p k w", k=k), src).then_inc(over_loaded[i], 16)

                @block.scalar
                def _(act):
                    with act.If(act.value_load(overflow[0:1, 0:1], min_val=0, max_val=1) > 0):
                        with act.Fori(0, NE) as e:
                            for f in range(DE // P):
                                b = B_HID + 2 * (f % 2)
                                act.wait_ge(psum_full[b], e * 2 + (1 + f // 2 + 1))
                                act.activation(sil[:, f, :], ps[:, b, 0:T], ACT.Silu).then_inc(psum_free[b], 1)

                @block.vector
                def _(dve):
                    with dve.If(dve.value_load(overflow[0:1, 0:1], min_val=0, max_val=1) > 0):
                        for b in range(BANKS):
                            dve.wait_ge(*made(("first", b)))
                            dve.tensor_copy(moved[0:2, 0:2], ps[0:2, b, 0:2]).then_inc(*reads(("first", b)))
                            dve.wait_ge(*read(("first", b)))
                        dve.memset(acc, 0.0).then_inc(*counts("dve_step"))
                        dve.wait_ge(*counted("dve_step"))
                        with dve.Fori(0, NE) as e:
                            for f in range(DE // P):
                                a = B_HID + 2 * (f % 2)
                                dve.wait_ge(psum_full[a + 1], e * 2 + (1 + f // 2 + 1))
                                dve.wait_ge(psum_free[a], e * 2 + (1 + f // 2 + 1))
                                dve.tensor_tensor(hid[:, f, :], ps[:, a + 1, 0:T], sil[:, f, :], ALU.mult
                                                  ).then_inc(sem["hidden_ready"], 1)
                                dve.wait_ge(sem["hidden_ready"], e * 4 + (f + 1))
                                dve.tensor_copy(moved[:, 0:1], cst[:, 0:1]).then_inc(psum_free[a + 1], 1)
                            for n in range(2 * NT):
                                b = B_OUT + n % N_OUT
                                t = n // 2
                                out = acc[:, t, 512 * (n % 2):512 * (n % 2) + 512]
                                dve.wait_ge(psum_full[b], e * 2 + (1 + n // N_OUT + 1))
                                dve.scalar_tensor_tensor(out=out, in0=ps[:, b, :], scalar=gate_over[:, t, bass.ds(e, 1)],
                                                         in1=out, op0=ALU.mult, op1=ALU.add).then_inc(psum_free[b], 1)
                                dve.wait_ge(psum_free[b], e * 2 + (1 + n // N_OUT + 1))
                        dve.tensor_copy(moved[:, 0:1], cst[:, 0:1]).then_inc(*counts("moe_ready"))
                        dve.wait_ge(*counted("moe_ready"))
                        for t in range(NT):
                            c = 0 if t == 0 else 1
                            for q in range(2):
                                dve.wait_ge(*made(("mo", t, q)))
                                s = quad(bank(("mo", t, q)))
                                dve.tensor_tensor(quad(moved), s, over(mod[:, 5, 4 * q:4 * q + 4, c], P), ALU.mult
                                                  ).then_inc(*reads(("mo", t, q)))
                                dve.wait_ge(*read(("mo", t, q)))
                                out = xT[:, 4 * q:4 * q + 4, tok(t)]
                                dve.tensor_tensor(out, out, quad(moved), ALU.add).then_inc(*counts("dve_step"))
                                dve.wait_ge(*counted("dve_step"))

            clear_counts()

        y_out = carve(0, NT, D)
        with nc.Block() as block:
            @block.tensor
            def _(pe):
                for t in range(NT):
                    for q in range(2):
                        transposed(pe, ("y", t, q), [xT[:, 4 * q + i, tok(t)] for i in range(4)])

            @block.vector
            def _(dve):
                for t in range(NT):
                    for q in range(2):
                        dve.wait_ge(*made(("y", t, q)))
                        dve.tensor_copy(y_out[:, t, 512 * q:512 * q + 512], bank(("y", t, q))).then_inc(*reads(("y", t, q)))
                        dve.wait_ge(*read(("y", t, q)))

            @block.sync
            def _(sp):
                for t in range(NT):
                    for q in range(2):
                        sp.wait_ge(*read(("y", t, q)))
                sp.dma_start(y.rearrange("(t p) d -> p t d", p=P), y_out).then_inc(sem["stored"], 16)
                sp.wait_ge(sem["stored"], 16)


_OUTS = [(NT * P, D), (DEPTH, P, KVL), (DEPTH, P, ROPE), (DEPTH, 2, H_B, DK, DV), (DEPTH, 2, H_C * HP, N_ST)]


def _constants():
    import numpy as np
    s, i = np.arange(P)[:, None], np.arange(P)[None, :]
    half = P // 2
    f = np.float32
    c = np.zeros((P, N_CONST), f)
    c[:, C_ID:C_ID + P] = s == i
    c[:, C_REL:C_REL + P] = (s <= i).astype(f) - (s < half).astype(f)
    c[:, C_REL + P:C_REL + 2 * P] = (s >= i).astype(f) - (s >= half).astype(f)
    c[:, C_CUM:C_CUM + P] = s <= i
    c[:, C_CUM + P:C_CUM + 2 * P] = s >= i
    c[:, C_AFT:C_AFT + P] = s > i
    c[:, C_AFT + P:C_AFT + 2 * P] = s < i
    c[:, C_ONE:C_ONE + P] = 1
    c[:, C_SEL] = (s < half)[:, 0]
    c[:, C_SEL + 1] = (s >= half)[:, 0]
    grid_w, n_freq = 64, ROPE // 4
    tok = np.arange(2 * P)
    inv = (1.0 / (np.float32(10000.0) ** (np.arange(n_freq, dtype=f) / f(n_freq)))).astype(f)
    ang = np.concatenate([(tok // grid_w).astype(f)[:, None] * inv, (tok % grid_w).astype(f)[:, None] * inv], 1)
    for t in range(2):
        c[:, C_COS + 16 * t:C_COS + 16 * t + 16] = np.cos(ang[P * t:P * t + P])
        c[:, C_SIN + 16 * t:C_SIN + 16 * t + 16] = np.sin(ang[P * t:P * t + P])
    c[:, C_RANK:C_RANK + 16] = 16 - np.arange(16)
    return c


def kernel(**inputs):
    import numpy as np
    import concourse.bacc as _bacc
    from concourse import mybir as _mybir
    from concourse.bass_utils import run_bass_kernel_spmd as _run

    a = {k: np.asarray(v) for k, v in inputs.items()}
    f = np.float32

    def features(v):
        return v.reshape(DEPTH, -1, P).transpose(0, 2, 1)

    def rows_of(v):
        return np.broadcast_to(v.reshape(DEPTH, 1, -1), (DEPTH, P, v[0].size))

    w_in = a['w_in']
    gates = np.zeros((DEPTH, 2 * RANK + 1, 2, H_B * DK), f)
    for d in range(2):
        gates[:, RANK * d:RANK * d + RANK, d] = a['b_wg'][:, d]
        gates[:, 2 * RANK, d] = a['b_bg'][:, d]
    vecs = np.concatenate(
        [features(a[n]) for n in ('norm1', 'norm2', 'b_ada', 'a_q_norm', 'a_kv_norm', 'c_norm')]
        + [features(np.tile(a['b_onorm'], (1, H_B))),
           a['c_conv_w'].reshape(DEPTH, TAPS * NX, P).transpose(0, 2, 1), features(a['c_conv_b'])], axis=2)
    rows = np.concatenate(
        [rows_of(a[n]) for n in ('a_qk_qnorm', 'a_qk_knorm', 'c_dt_bias', 'c_A_log', 'c_D')]
        + [np.broadcast_to(a['router_bias'], (DEPTH, P, NE))], axis=2)
    named = [
        ('x', np.concatenate([a['x_prompt'][0], a['x_sample'][0]], 0)),
        ('cond', np.stack([a['c_ctx'], a['c'][0]], 0).reshape(2, KD, P).transpose(2, 1, 0)),
        ('consts', _constants()), ('iota', np.broadcast_to(np.arange(PAIRS, dtype=f), (P, PAIRS))), ('vecs', vecs), ('rows', rows),
        ('w_small', np.concatenate([w_in[:, :, KROPE:KROPE + ROPE], w_in[:, :, DTC:DTC + 32],
                                    w_in[:, :, GLOW:GLOW + 32]], 2)),
        ('w_gate_low', gates), ('router_w', a['router_w']), ('cache_ckv', a['cache_ckv'][0]),
        ('cache_krope', a['cache_krope'][0]), ('state_gla', a['state_gla'][0]),
        ('state_ssd', a['state_ssd'][0].reshape(DEPTH, 2, H_C * HP, N_ST)),
        ('w_ada', a['w_ada']), ('w_in', w_in), ('a_wq', a['a_wq']), ('a_wkv', a['a_wkv']), ('a_wo', a['a_wo']),
        ('b_wo', a['b_wo']), ('c_wo', a['c_wo']), ('w_out', a['w_out']),
        ('e_w1', a['e_w1'].reshape(DEPTH * NE, D, DE)), ('e_w3', a['e_w3'].reshape(DEPTH * NE, D, DE)),
        ('e_w2', a['e_w2'].reshape(DEPTH * NE, DE, D))]
    nc = _bacc.Bacc("TRN2", target_bir_lowering=False, num_devices=1)
    arrays, args = {}, []
    for name, v in named:
        v = np.ascontiguousarray(v)
        arrays[f"in_{name}"] = v
        args.append(nc.dram_tensor(f"in_{name}", v.shape, _mybir.dt.from_np(v.dtype), kind="ExternalInput").ap())
    for i, shape in enumerate(_OUTS):
        args.append(nc.dram_tensor(f"out_{i}", shape, _mybir.dt.from_np(np.dtype(f)), kind="ExternalOutput").ap())
    trunk_kernel(nc, *args)
    r = _run(nc, [arrays], core_ids=[0]).results[0]
    o = [r[f"out_{i}"] for i in range(len(_OUTS))]
    return (o[0][0:P][None], o[0][P:][None], o[1][None], o[2][None], o[3][None],
            o[4].reshape(1, DEPTH, 2, H_C, HP, N_ST))
```
